# Optimizing a Trainium2 kernel written in Bass

```python
import numpy as np
import jax
import jax.numpy as jnp
from jax import lax

D_MODEL = 2048
BATCH = 1
SEQ = 256
DEPTH = 1
DEC_BATCH = 8
DEC_SEQ = 4
PAST_LEN = 256
PAGE_SIZE = 128

POOL_WINDOWS = (2, 4, 8, 16)
N_POOL_GROUPS = len(POOL_WINDOWS)
POOL_WIDTH = D_MODEL // 2
POOL_GROUP = POOL_WIDTH // N_POOL_GROUPS
POOL_STATE = max(POOL_WINDOWS) - 1
N_HEADS = 16
HEAD_DIM = 128
N_KV = 4
HPG = N_HEADS // N_KV
ROT_DIM = HEAD_DIM // 4
ROPE_THETA = 500000.0
ATTN_SCALE = HEAD_DIM ** -0.5
CMP_LEN = 32
CMP_STRIDE = 16
CMP_RATIO = CMP_LEN // CMP_STRIDE
SLC_BLK = 64
N_SEL = 16
WINDOW = 512
WIN_QBLK = 128
SLC_QCHUNK = 64
PEER_HEADS = 8
N_KEYS = 128
N_EXPERTS = N_KEYS * N_KEYS
PEER_TOPK = 16
PEER_QDIM = 256
PEER_HALF = PEER_QDIM // 2
PEER_BLOCK = 64
DN_ALPHA = (2.0 * DEPTH) ** 0.25
DN_BETA = (8.0 * DEPTH) ** -0.25
LN_EPS = 1e-5

Q_WIDTH = N_HEADS * HEAD_DIM
KV_WIDTH = N_KV * HEAD_DIM
IN_SIZES = (POOL_WIDTH, Q_WIDTH, KV_WIDTH, KV_WIDTH, KV_WIDTH, KV_WIDTH, KV_WIDTH, KV_WIDTH, 3 * N_HEADS, 2 * D_MODEL)

kernel_name = 'hybrid_pool_nsa_peer_decode_step'

def layer_norm(x, g, b):
    xf = x.astype(jnp.float32)
    mu = jnp.mean(xf, axis=-1, keepdims=True)
    var = jnp.mean(jnp.square(xf - mu), axis=-1, keepdims=True)
    return ((xf - mu) * lax.rsqrt(var + LN_EPS) * g + b).astype(x.dtype)

def masked_softmax(s, mask):
    s = jnp.where(mask, s.astype(jnp.float32), -jnp.inf)
    m = jnp.max(s, axis=-1, keepdims=True)
    e = jnp.exp(s - jnp.where(jnp.isfinite(m), m, 0.0))
    den = jnp.sum(e, axis=-1, keepdims=True)
    return e / jnp.where(den > 0.0, den, 1.0)

def rope(x, pos):
    half = ROT_DIM // 2
    inv = ROPE_THETA ** (-jnp.arange(half, dtype=jnp.float32) / half)
    ang = pos.astype(jnp.float32)[:, None] * inv
    cos = jnp.cos(ang)[:, None, :]
    sin = jnp.sin(ang)[:, None, :]
    xr = x[..., :ROT_DIM].astype(jnp.float32)
    x1, x2 = xr[..., :half], xr[..., half:]
    rot = jnp.concatenate([x1 * cos - x2 * sin, x2 * cos + x1 * sin], axis=-1).astype(x.dtype)
    return jnp.concatenate([rot, x[..., ROT_DIM:]], axis=-1)

def pool_mixer(u, u_prev, pos0, w_grp, scale):
    B, L, P = u.shape
    ext = jnp.concatenate([u_prev, u], axis=1)
    cs = jnp.pad(jnp.cumsum(ext.astype(jnp.float32), axis=1), ((0, 0), (1, 0), (0, 0)))
    pos = pos0 + np.arange(L)
    upto = cs[:, POOL_STATE + 1:]
    means = []
    for gi, w in enumerate(POOL_WINDOWS):
        c = slice(gi * POOL_GROUP, (gi + 1) * POOL_GROUP)
        before = cs[:, POOL_STATE + 1 - w:POOL_STATE + 1 - w + L, c]
        cnt = np.minimum(w, pos + 1).astype(np.float32)[None, :, None]
        means.append((upto[..., c] - before) / cnt)
    d = (jnp.concatenate(means, axis=-1) - u.astype(jnp.float32)).astype(u.dtype)
    d = d.reshape(B, L, N_POOL_GROUPS, POOL_GROUP)
    y = jnp.einsum('blgc,gce->blge', d, w_grp).reshape(B, L, P) * scale
    return y, ext[:, -POOL_STATE:]

def compress(kv, pe, w1, w2):
    B, Lt = kv.shape[:2]
    n_chunk = Lt // CMP_STRIDE
    n_cmp = n_chunk - CMP_RATIO + 1
    ch = kv[:, :n_chunk * CMP_STRIDE].reshape(B, n_chunk, CMP_STRIDE, N_KV, HEAD_DIM)
    w1r = w1.reshape(CMP_RATIO, CMP_STRIDE, HEAD_DIM, HEAD_DIM)
    a = jnp.einsum('bcsgd,rsde->rbcge', ch, w1r)
    hid = jnp.einsum('jd,jde->e', pe, w1)
    for r in range(CMP_RATIO):
        hid = hid + a[r, :, r:r + n_cmp]
    return jnp.einsum('bnge,ef->bngf', jax.nn.gelu(hid, approximate=False), w2)

def cmp_attend(q, qpos, kcb, vcb):
    B, L = q.shape[:2]
    n_cmp = kcb.shape[1]
    qg = q.reshape(B, L, N_KV, HPG, HEAD_DIM)
    s = jnp.einsum('blghd,bngd->bghln', qg, kcb) * ATTN_SCALE
    ends = np.arange(n_cmp) * CMP_STRIDE + CMP_LEN - 1
    pr = masked_softmax(s, ends[None, :] <= qpos[:, None])
    o = jnp.einsum('bghln,bngd->blghd', pr.astype(vcb.dtype), vcb).reshape(B, L, N_HEADS, HEAD_DIM)
    return o, jnp.sum(pr, axis=2)

def select_blocks(imp_c, qpos, Lt):
    n_cmp = imp_c.shape[-1]
    n_slc = -(-Lt // SLC_BLK)
    cs = np.arange(n_cmp) * CMP_STRIDE
    bs = np.arange(n_slc) * SLC_BLK
    inter = ((cs[:, None] < bs[None, :] + SLC_BLK) & (cs[:, None] + CMP_LEN > bs[None, :])).astype(np.float32)
    imp = jnp.einsum('bgln,nj->bglj', imp_c, jnp.asarray(inter))
    cur = (qpos // SLC_BLK)[:, None]
    j = np.arange(n_slc)[None, :]
    valid = bs[None, :] <= qpos[:, None]
    forced = valid & ((j == 0) | (j == cur) | (j == cur - 1))
    score = jnp.where(forced, jnp.inf, jnp.where(valid, imp, -jnp.inf))
    _, idx = lax.top_k(score, min(N_SEL, n_slc))
    return idx

def slc_attend(q, qpos, idx, k, v):
    B, L = q.shape[:2]
    Lt = k.shape[1]
    n_slc = -(-Lt // SLC_BLK)
    padk = ((0, 0), (0, n_slc * SLC_BLK - Lt), (0, 0), (0, 0))

    def blocks(a):
        return jnp.pad(a, padk).reshape(B, n_slc, SLC_BLK, N_KV, HEAD_DIM).transpose(0, 3, 1, 2, 4)

    kb, vb = blocks(k), blocks(v)
    n_q = B * L
    n_pad = (-n_q) % SLC_QCHUNK

    def flat(a):
        a = jnp.pad(a, [(0, n_pad)] + [(0, 0)] * (a.ndim - 1))
        return a.reshape((-1, SLC_QCHUNK) + a.shape[1:])

    qf = flat(q.reshape(n_q, N_KV, HPG, HEAD_DIM))
    idf = flat(idx.transpose(0, 2, 1, 3).reshape(n_q, N_KV, -1))
    sid = flat(jnp.repeat(jnp.arange(B, dtype=jnp.int32), L))
    pf = flat(jnp.asarray(np.broadcast_to(qpos, (B, L)).reshape(-1), jnp.int32))
    g_ix = jnp.arange(N_KV)[None, :, None]

    def step(args):
        qc, ic, sc, pc = args
        C, _, n_sel = ic.shape
        kg = kb[sc[:, None, None], g_ix, ic]
        vg = vb[sc[:, None, None], g_ix, ic]
        s = jnp.einsum('cghd,cgnkd->cghnk', qc, kg).reshape(C, N_KV, HPG, n_sel * SLC_BLK) * ATTN_SCALE
        kpos = ic[..., None] * SLC_BLK + jnp.arange(SLC_BLK)
        mask = (kpos <= pc[:, None, None, None]).reshape(C, N_KV, 1, n_sel * SLC_BLK)
        pr = masked_softmax(s, mask)
        vflat = vg.reshape(C, N_KV, n_sel * SLC_BLK, HEAD_DIM)
        return jnp.einsum('cghm,cgmd->cghd', pr.astype(vg.dtype), vflat)

    o = lax.map(step, (qf, idf, sid, pf))
    return o.reshape(-1, N_HEADS, HEAD_DIM)[:n_q].reshape(B, L, N_HEADS, HEAD_DIM)

def window_attend(q, k_lead, v_lead, k_new, v_new, pos0):
    B, L = q.shape[:2]
    kf = jnp.concatenate([k_lead, k_new], axis=1)
    vf = jnp.concatenate([v_lead, v_new], axis=1)
    kpos = jnp.asarray(pos0 - WINDOW + np.arange(WINDOW + L), jnp.int32)
    qb = WIN_QBLK if L % WIN_QBLK == 0 else L
    nqb = L // qb
    qblocks = q.reshape(B, nqb, qb, N_KV, HPG, HEAD_DIM).transpose(1, 0, 2, 3, 4, 5)

    def step(args):
        b, qc = args
        start = b * qb
        kc = lax.dynamic_slice_in_dim(kf, start, WINDOW + qb, axis=1)
        vc = lax.dynamic_slice_in_dim(vf, start, WINDOW + qb, axis=1)
        kp = lax.dynamic_slice_in_dim(kpos, start, WINDOW + qb, axis=0)[None, :]
        qp = (pos0 + start + jnp.arange(qb))[:, None]
        s = jnp.einsum('bighd,bkgd->bghik', qc, kc) * ATTN_SCALE
        mask = (kp <= qp) & (kp > qp - WINDOW) & (kp >= 0)
        pr = masked_softmax(s, mask)
        return jnp.einsum('bghik,bkgd->bighd', pr.astype(vc.dtype), vc)

    o = lax.map(step, (jnp.arange(nqb, dtype=jnp.int32), qblocks))
    return o.transpose(1, 0, 2, 3, 4, 5).reshape(B, L, N_HEADS, HEAD_DIM)

def peer(h, wq, sub_keys, u_tab, v_tab):
    B, L, D = h.shape
    t = h.reshape(B * L, D)
    T = t.shape[0]
    q = jnp.dot(t, wq).reshape(T, PEER_HEADS, 2, PEER_HALF)
    s = jnp.einsum('thpc,hpkc->thpk', q, sub_keys).astype(jnp.float32)
    s1, i1 = lax.top_k(s[:, :, 0], PEER_TOPK)
    s2, i2 = lax.top_k(s[:, :, 1], PEER_TOPK)
    cand = (s1[..., :, None] + s2[..., None, :]).reshape(T, PEER_HEADS, PEER_TOPK * PEER_TOPK)
    cid = (i1[..., :, None] * N_KEYS + i2[..., None, :]).reshape(T, PEER_HEADS, PEER_TOPK * PEER_TOPK)
    top, sel = lax.top_k(cand, PEER_TOPK)
    eid = jnp.take_along_axis(cid, sel, axis=-1)
    gate = jax.nn.softmax(top, axis=-1)
    n_pad = (-T) % PEER_BLOCK

    def chunks(a):
        a = jnp.pad(a, [(0, n_pad)] + [(0, 0)] * (a.ndim - 1))
        return a.reshape((-1, PEER_BLOCK) + a.shape[1:])

    def step(args):
        tc, ec, gc = args
        act = jax.nn.gelu(jnp.einsum('cd,chkd->chk', tc, u_tab[ec]).astype(jnp.float32), approximate=False)
        return jnp.einsum('chk,chkd->cd', (gc * act).astype(tc.dtype), v_tab[ec])

    out = lax.map(step, (chunks(t), chunks(eid), chunks(gate)))
    return out.reshape(-1, D)[:T].reshape(B, L, D)

def decoder_layer(x, pos0, past, win_k, win_v, pool_prev, win_rows, p):
    B, L, _ = x.shape
    dt = x.dtype
    qpos = pos0 + np.arange(L)
    qpos_j = jnp.asarray(qpos, jnp.int32)
    proj = jnp.einsum('bld,dc->blc', x, p['w_in'])
    splits = np.cumsum(IN_SIZES)[:-1].tolist()
    u_pool, q, kc, vc, ks, vs, kw, vw, g_nsa, g_br = jnp.split(proj, splits, axis=-1)
    q = q.reshape(B, L, N_HEADS, HEAD_DIM)
    kc, vc, ks, vs, kw, vw = [a.reshape(B, L, N_KV, HEAD_DIM) for a in (kc, vc, ks, vs, kw, vw)]
    q_rot = rope(q, qpos_j)
    ks = rope(ks, qpos_j)
    kw = rope(kw, qpos_j)
    if past is None:
        kc_all, vc_all, ks_all, vs_all = kc, vc, ks, vs
    else:
        kc_all, vc_all, ks_all, vs_all = [jnp.concatenate([a, b], axis=1) for a, b in zip(past, (kc, vc, ks, vs))]
    kcb = compress(kc_all, p['cmp_pe_k'], p['cmp_w1_k'], p['cmp_w2_k'])
    vcb = compress(vc_all, p['cmp_pe_v'], p['cmp_w1_v'], p['cmp_w2_v'])
    o_cmp, imp = cmp_attend(q, qpos, kcb, vcb)
    idx = select_blocks(imp, qpos, ks_all.shape[1])
    o_slc = slc_attend(q_rot, qpos, idx, ks_all, vs_all)
    lead = ((0, 0), (WINDOW - win_k.shape[1], 0), (0, 0), (0, 0))
    o_win = window_attend(q_rot, jnp.pad(win_k, lead), jnp.pad(win_v, lead), kw, vw, pos0)
    g = jax.nn.sigmoid(g_nsa.astype(jnp.float32)).astype(dt).reshape(B, L, 3, N_HEADS, 1)
    o_attn = (g[:, :, 0] * o_cmp + g[:, :, 1] * o_slc + g[:, :, 2] * o_win).reshape(B, L, Q_WIDTH)
    o_pool, pool_new = pool_mixer(u_pool, pool_prev, pos0, p['pool_grp_w'], p['pool_scale'])
    gate = jax.nn.sigmoid(g_br.astype(jnp.float32)).astype(dt)
    merged = gate[..., :D_MODEL] * (o_pool @ p['w_branch_pool']) + gate[..., D_MODEL:] * (o_attn @ p['w_branch_attn'])
    h = layer_norm(DN_ALPHA * x + merged @ p['w_out'], p['ln1_g'], p['ln1_b'])
    z = peer(h, p['peer_wq'], p['peer_subkeys'], p['peer_u'], p['peer_v'])
    y = layer_norm(DN_ALPHA * h + z, p['ln2_g'], p['ln2_b'])
    win_k_new = jnp.concatenate([win_k, kw], axis=1)[:, -win_rows:]
    win_v_new = jnp.concatenate([win_v, vw], axis=1)[:, -win_rows:]
    return y, (kc, vc, ks, vs, win_k_new, win_v_new, pool_new)

def setup_inputs(seed: int = 0) -> dict:
    key = jax.random.key(seed)
    keys = iter(jax.random.split(key, 48))

    def nrm(shape, s=1.0):
        return jax.random.normal(next(keys), shape, jnp.float32) * s

    n_pages = PAST_LEN // PAGE_SIZE
    n_used = DEC_BATCH * n_pages
    n_phys = n_used + max(1, n_used // 4)
    perm = jax.random.permutation(next(keys), n_phys).astype(jnp.int32)
    page_table = perm[:n_used].reshape(DEC_BATCH, n_pages)
    win_rows = min(WINDOW, PAST_LEN)
    fi = D_MODEL ** -0.5
    paged = (DEPTH, n_phys, PAGE_SIZE, N_KV, HEAD_DIM)
    w_in = jnp.concatenate([
        nrm((DEPTH, D_MODEL, POOL_WIDTH), fi),
        nrm((DEPTH, D_MODEL, Q_WIDTH), fi),
        nrm((DEPTH, D_MODEL, KV_WIDTH), fi),
        nrm((DEPTH, D_MODEL, KV_WIDTH), fi * DN_BETA),
        nrm((DEPTH, D_MODEL, KV_WIDTH), fi),
        nrm((DEPTH, D_MODEL, KV_WIDTH), fi * DN_BETA),
        nrm((DEPTH, D_MODEL, KV_WIDTH), fi),
        nrm((DEPTH, D_MODEL, KV_WIDTH), fi * DN_BETA),
        nrm((DEPTH, D_MODEL, 3 * N_HEADS), fi),
        nrm((DEPTH, D_MODEL, 2 * D_MODEL), fi),
    ], axis=-1)
    return {
        'x_prompt': nrm((BATCH, SEQ, D_MODEL)),
        'x_sample': nrm((DEC_BATCH, DEC_SEQ, D_MODEL)),
        'cache_k_cmp': nrm(paged),
        'cache_v_cmp': nrm(paged),
        'cache_k_slc': nrm(paged),
        'cache_v_slc': nrm(paged),
        'cache_k_win': nrm((DEPTH, DEC_BATCH, win_rows, N_KV, HEAD_DIM)),
        'cache_v_win': nrm((DEPTH, DEC_BATCH, win_rows, N_KV, HEAD_DIM)),
        'state_pool': nrm((DEPTH, DEC_BATCH, POOL_STATE, POOL_WIDTH)),
        'page_table': page_table,
        'w_in': w_in,
        'pool_grp_w': nrm((DEPTH, N_POOL_GROUPS, POOL_GROUP, POOL_GROUP), POOL_GROUP ** -0.5),
        'pool_scale': 1.0 + nrm((DEPTH, POOL_WIDTH), 0.1),
        'cmp_pe_k': nrm((DEPTH, CMP_LEN, HEAD_DIM), 0.5),
        'cmp_w1_k': nrm((DEPTH, CMP_LEN, HEAD_DIM, HEAD_DIM), (CMP_LEN * HEAD_DIM) ** -0.5),
        'cmp_w2_k': nrm((DEPTH, HEAD_DIM, HEAD_DIM), HEAD_DIM ** -0.5),
        'cmp_pe_v': nrm((DEPTH, CMP_LEN, HEAD_DIM), 0.5),
        'cmp_w1_v': nrm((DEPTH, CMP_LEN, HEAD_DIM, HEAD_DIM), (CMP_LEN * HEAD_DIM) ** -0.5),
        'cmp_w2_v': nrm((DEPTH, HEAD_DIM, HEAD_DIM), HEAD_DIM ** -0.5),
        'w_branch_pool': nrm((DEPTH, POOL_WIDTH, D_MODEL), POOL_WIDTH ** -0.5 * DN_BETA),
        'w_branch_attn': nrm((DEPTH, Q_WIDTH, D_MODEL), Q_WIDTH ** -0.5 * DN_BETA),
        'w_out': nrm((DEPTH, D_MODEL, D_MODEL), fi * DN_BETA),
        'ln1_g': 1.0 + nrm((DEPTH, D_MODEL), 0.02),
        'ln1_b': nrm((DEPTH, D_MODEL), 0.02),
        'peer_wq': nrm((DEPTH, D_MODEL, PEER_HEADS * PEER_QDIM), fi),
        'peer_subkeys': nrm((DEPTH, PEER_HEADS, 2, N_KEYS, PEER_HALF), PEER_HALF ** -0.5),
        'peer_u': nrm((DEPTH, N_EXPERTS, D_MODEL), fi * DN_BETA),
        'peer_v': nrm((DEPTH, N_EXPERTS, D_MODEL), DN_BETA * PEER_HEADS ** -0.5),
        'ln2_g': 1.0 + nrm((DEPTH, D_MODEL), 0.02),
        'ln2_b': nrm((DEPTH, D_MODEL), 0.02),
    }

def reference(x_prompt, x_sample, cache_k_cmp, cache_v_cmp, cache_k_slc, cache_v_slc, cache_k_win, cache_v_win, state_pool, page_table, w_in, pool_grp_w, pool_scale, cmp_pe_k, cmp_w1_k, cmp_w2_k, cmp_pe_v, cmp_w1_v, cmp_w2_v, w_branch_pool, w_branch_attn, w_out, ln1_g, ln1_b, peer_wq, peer_subkeys, peer_u, peer_v, ln2_g, ln2_b):
    B, L = x_prompt.shape[:2]
    zero_win = jnp.zeros((B, 0, N_KV, HEAD_DIM), x_prompt.dtype)
    zero_pool = jnp.zeros((B, POOL_STATE, POOL_WIDTH), x_prompt.dtype)

    def gather_pages(c):
        g = c[page_table]
        return g.reshape(g.shape[0], -1, N_KV, HEAD_DIM)

    hp, hs = x_prompt, x_sample
    st_prompt, st_sample = [], []
    for l in range(DEPTH):
        p = {'w_in': w_in[l], 'pool_grp_w': pool_grp_w[l], 'pool_scale': pool_scale[l],
             'cmp_pe_k': cmp_pe_k[l], 'cmp_w1_k': cmp_w1_k[l], 'cmp_w2_k': cmp_w2_k[l],
             'cmp_pe_v': cmp_pe_v[l], 'cmp_w1_v': cmp_w1_v[l], 'cmp_w2_v': cmp_w2_v[l],
             'w_branch_pool': w_branch_pool[l], 'w_branch_attn': w_branch_attn[l], 'w_out': w_out[l],
             'ln1_g': ln1_g[l], 'ln1_b': ln1_b[l], 'peer_wq': peer_wq[l], 'peer_subkeys': peer_subkeys[l],
             'peer_u': peer_u[l], 'peer_v': peer_v[l], 'ln2_g': ln2_g[l], 'ln2_b': ln2_b[l]}
        hp, sp = decoder_layer(hp, 0, None, zero_win, zero_win, zero_pool, min(WINDOW, L), p)
        past = (gather_pages(cache_k_cmp[l]), gather_pages(cache_v_cmp[l]),
                gather_pages(cache_k_slc[l]), gather_pages(cache_v_slc[l]))
        hs, ss = decoder_layer(hs, PAST_LEN, past, cache_k_win[l], cache_v_win[l], state_pool[l],
                               cache_k_win.shape[2], p)
        st_prompt.append(sp)
        st_sample.append(ss)

    def stack(states, i):
        return jnp.stack([s[i] for s in states], axis=0)

    k_cmp_p = stack(st_prompt, 0)
    v_cmp_p = stack(st_prompt, 1)
    k_slc_p = stack(st_prompt, 2)
    v_slc_p = stack(st_prompt, 3)
    k_win_p = stack(st_prompt, 4)
    v_win_p = stack(st_prompt, 5)
    pool_p = stack(st_prompt, 6)
    k_cmp_s = stack(st_sample, 0)
    v_cmp_s = stack(st_sample, 1)
    k_slc_s = stack(st_sample, 2)
    v_slc_s = stack(st_sample, 3)
    k_win_s = stack(st_sample, 4)
    v_win_s = stack(st_sample, 5)
    pool_s = stack(st_sample, 6)
    return (hp, hs, k_cmp_p, v_cmp_p, k_slc_p, v_slc_p, k_win_p, v_win_p, pool_p, k_cmp_s, v_cmp_s, k_slc_s, v_slc_s, k_win_s, v_win_s, pool_s)


_drawn_inputs = setup_inputs


def setup_inputs(seed=0):
    import zlib

    import numpy as np

    out = dict(_drawn_inputs(seed))
    spreads = {}
    factors = {'cache_k_cmp': 5.7,
     'cache_v_cmp': 3.124,
     'cache_k_slc': 7.099,
     'cache_v_slc': 5.728,
     'pool_scale': 3.644,
     'cmp_pe_k': 8.0,
     'cmp_w1_k': 5.557,
     'cmp_w2_k': 5.503,
     'ln1_g': 7.452,
     'ln2_g': 23.172,
     'ln2_b': 23.15,
     'ln1_b': 18.233}
    for name, (base, spread) in spreads.items():
        noise = np.random.default_rng([zlib.crc32(name.encode()), seed]).standard_normal(out[name].shape)
        drawn = base * np.exp(spread * noise) if base else spread * noise
        out[name] = jnp.asarray(drawn.astype(out[name].dtype))
    for name, factor in factors.items():
        out[name] = (out[name] * factor).astype(out[name].dtype)
    return out
```

```python
from contextlib import ExitStack

import concourse.bass as bass
from concourse import mybir

F32 = mybir.dt.float32
U32 = mybir.dt.uint32
I32 = mybir.dt.int32
ALU = mybir.AluOpType
ACT = mybir.ActivationFunctionType
AX = mybir.AxisListType.X

P = 128
D = 2048
DK = D // P
NP_TOK = 256
NS_TOK = 32
T = NP_TOK + NS_TOK
TT = 2
BS = 8
LS = 4
NKV = 4
HPG = 4
NH = 16
HD = 128
NCMP = 15
NCHUNK = 16
POOL_CH = 8
POOL_ST = 15
SCALE = float(HD) ** -0.5
ALPHA = 2.0 ** 0.25
EPS = 1e-5
SLAB = 256
SLOTS = 4
Q0, KC0, VC0, KS0, VS0, KW0, VW0 = 8, 24, 28, 32, 36, 40, 44
N1 = 48
GT = 32
NG = T // GT
NSTEP = 32
SB = 8
NB = NSTEP // SB
NEG = -3.0e38


def build(nc, xT_d, x_d, win_d, nsa_d, gbr_d, wbp_d, wba_d, wo_d, wq_d, grp_d, pscale_d, stateT_d,
          state_d, kcT_d, vcT_d, ksT_d, vs_d, kwT_d, vw_d, kwin_d, vwin_d, ptab_d, w1_d, w2_d, peT_d,
          ln_d, skT_d, u_d, v_d, ident_d, rot_d, cs_d, maskp_d, maskn_d, maskc_d, keepc_d, rcnt_d,
          sel_d, iota_d, pidx_d,
          y_d, kvT_d, ktail_d, vtail_d, poolT_d, spool_d):
    h_d = nc.dram_tensor("h_rows", (T, D), F32).ap()
    gate_d = nc.dram_tensor("nsa_gates", (3 * NH, T), F32).ap()
    score_d = nc.dram_tensor("peer_scores", (NG, P, 512), F32).ap()
    top = ExitStack()

    def sem(name):
        return top.enter_context(nc.semaphore(name))

    def sb(scope, name, shape, dt=F32):
        return scope.enter_context(nc.sbuf_tensor(name, shape, dt))

    with top:
        PS = top.enter_context(nc.psum_tensor("PS", [P, 8, 512], F32))
        ident = sb(top, "ident", [P, P])
        actT = ExitStack()
        xT = sb(actT, "xT", [P, DK, T])
        attnT = sb(actT, "attnT", [P, NH, T])
        woT = pqT = attnT
        hT = xT
        ypoolT = sb(actT, "ypoolT", [P, POOL_CH, T])
        proj = ExitStack()
        PT = sb(proj, "PT", [P, N1, T])
        gateT = sb(proj, "gateT", [3 * NH, T])
        out_done = sem("out_done")
        n_out = [0]

        def out_dma(eng, dst, src):
            n_out[0] += 1
            eng.dma_start(dst, src).then_inc(out_done, 16)

        ring1 = ExitStack()
        W = [sb(ring1, f"win{s}", [P, DK, SLAB]) for s in range(SLOTS)]
        Wn = sb(ring1, "Wn", [P, DK, 3 * NH])
        x_ld = sem("x_ld")
        w1ld = [sem(f"w1ld{s}") for s in range(SLOTS)]
        wn_ld = sem("wn_ld")
        p1_done = sem("p1_done")
        p1_free = sem("p1_free")
        g_done = sem("g_done")
        sg_done = sem("sg_done")
        sg_st = sem("sg_st")
        N_IT = N1 * P // SLAB // SLOTS
        CPI = SLOTS * SLAB // P
        with nc.Block() as block:
            @block.sync
            def _(sp):
                sp.dma_start(ident[:, :], ident_d).then_inc(x_ld, 16)
                sp.dma_start(xT[:, :, :], xT_d.rearrange("(k p) t -> p k t", p=P)).then_inc(x_ld, 16)
                for s in range(SLOTS):
                    sp.dma_start(W[s][:, :, :], win_d[s].rearrange("p (k c) -> p k c", k=DK)).then_inc(w1ld[s], 16)
                sp.dma_start(Wn[:, :, :], nsa_d).then_inc(wn_ld, 16)
                with sp.Fori(0, N_IT - 1) as i:
                    for s in range(SLOTS):
                        sp.wait_ge(p1_done, i * CPI + 2 * (s + 1))
                        sp.dma_start(W[s][:, :, :], win_d[bass.ds(i * SLOTS + SLOTS + s, 1)].rearrange(
                            "a p (k c) -> p (a k) c", k=DK)).then_inc(w1ld[s], 16)
                out_dma(sp, ktail_d, kwin_d[:, 4:256])
                out_dma(sp, vtail_d, vwin_d[:, 4:256])
                out_dma(sp, spool_d, state_d[:, 4:15])
                sp.wait_ge(sg_done, 1)
                sp.dma_start(gate_d, gateT[:, :]).then_inc(sg_st, 16)
                sp.wait_ge(sg_st, 16)

            @block.tensor
            def _(pe):
                pe.wait_ge(x_ld, 32)
                with pe.Fori(0, N_IT) as i:
                    for s in range(SLOTS):
                        pe.wait_ge(w1ld[s], i * 16 + 16)
                        for j in range(2):
                            c = 2 * s + j
                            pe.wait_ge(p1_free, i * CPI + c + 1)
                            for k in range(DK):
                                m = nc.tensor.matmul(PS[:, c % 2, 0:T], W[s][:, k, j * P:(j + 1) * P], xT[:, k, :],
                                                     start=(k == 0), stop=(k == DK - 1))
                            m.then_inc(p1_done, 1)
                pe.wait_ge(wn_ld, 16)
                for k in range(DK):
                    m = nc.tensor.matmul(PS[0:3 * NH, 2, 0:T], Wn[:, k, :], xT[:, k, :],
                                         start=(k == 0), stop=(k == DK - 1))
                m.then_inc(g_done, 1)

            @block.scalar
            def _(act):
                act.sem_inc(p1_free, 2)
                with act.Fori(0, N_IT) as i:
                    for c in range(CPI):
                        act.wait_ge(p1_done, i * CPI + c + 1)
                        nc.scalar.copy(PT[:, bass.ds(i * CPI + c, 1), :].rearrange("p a t -> p (a t)"),
                                       PS[:, c % 2, 0:T]).then_inc(p1_free, 1)
                act.wait_ge(g_done, 1)
                nc.scalar.activation(gateT[:, :], PS[0:3 * NH, 2, 0:T], ACT.Sigmoid).then_inc(sg_done, 1)
        ring1.close()

        mid = ExitStack()
        qrT = sb(mid, "qrT", [P, NH, T])
        VR = sb(mid, "VR", [P, 3, 2, NKV * HD])
        scope = ExitStack()
        rot = sb(scope, "rot", [P, P])
        cs = sb(scope, "cs", [P, 2, T])
        rt = sb(scope, "rt", [P, 4, T])
        rt2 = sb(scope, "rt2", [P, 4, T])
        ypool_in = sb(scope, "ypool_in", [P, POOL_CH, T])
        S1 = sb(scope, "S1", [P, POOL_ST + NP_TOK])
        S2 = sb(scope, "S2", [P, BS, POOL_ST + LS])
        EP = sb(scope, "EP", [P, POOL_CH, POOL_ST + NP_TOK])
        ES = sb(scope, "ES", [P, POOL_CH, BS, POOL_ST + LS])
        past = sb(scope, "past", [P, POOL_CH, BS * POOL_ST])
        grpw = sb(scope, "grpw", [P, 4, 2, 256])
        pscale = sb(scope, "pscale", [P, POOL_CH])
        rcnt = sb(scope, "rcnt", [P, 4, 16])
        c2 = sem("c2")
        pst = sem("pst")
        rq = sem("rq")
        rd = sem("rd")
        qcp = sem("qcp")
        vt = sem("vt")
        vc = sem("vc")
        dv = sem("dv")
        pl = sem("pl")
        pd = sem("pd")
        ym = sem("ym")
        yc = sem("yc")
        with nc.Block() as block:
            @block.sync
            def _(sp):
                sp.dma_start(rot[:, :], rot_d).then_inc(c2, 16)
                sp.dma_start(cs[:, :, :], cs_d).then_inc(c2, 16)
                sp.dma_start(past[:, :, :], stateT_d.rearrange("(c p) n -> p c n", p=P)).then_inc(pst, 16)
                sp.dma_start(grpw[:, :, :, :], grp_d.rearrange("g (k p) e -> p g k e", p=P)).then_inc(pst, 16)
                sp.dma_start(pscale[:, :], pscale_d).then_inc(pst, 16)
                sp.dma_start(rcnt[:, :, :], rcnt_d).then_inc(pst, 16)
                for n, c0 in ((0, KC0), (1, VC0), (3, VS0), (5, VW0)):
                    out_dma(sp, kvT_d[:, n], PT[:, c0:c0 + NKV, :])
                out_dma(sp, poolT_d, PT[:, 0:POOL_CH, NP_TOK - POOL_ST:T])
                sp.wait_ge(rd, 6 * 3)
                for n, c0 in ((2, KS0), (4, KW0)):
                    out_dma(sp, kvT_d[:, n], PT[:, c0:c0 + NKV, :])

            @block.tensor
            def _(pe):
                pe.wait_ge(c2, 32)
                pe.wait_ge(qcp, 1)
                for n in range(6):
                    src = qrT[:, 4 * n:4 * n + 4, :] if n < 4 else PT[:, (KS0, KW0)[n - 4]:(KS0, KW0)[n - 4] + 4, :]
                    if n > 0:
                        pe.wait_ge(rd, 3 * n)
                    for j in range(4):
                        m = nc.tensor.matmul(PS[:, j, 0:T], rot[:, :], src[:, j, :], start=True, stop=True)
                    m.then_inc(rq, 1)
                for n in range(6):
                    t, v = n // 2, n % 2
                    w = P if t < TT else NS_TOK
                    c0 = (VS0, VW0)[v]
                    if n >= 2:
                        pe.wait_ge(vc, n - 1)
                    for j in range(NKV):
                        m = nc.tensor.transpose(PS[0:w, 4 + n % 2, j * P:(j + 1) * P],
                                                PT[:, c0 + j, t * P:t * P + w], ident[:, :])
                    m.then_inc(vt, 1)
                pe.wait_ge(pst, 64)
                pe.wait_ge(pd, 2)
                for c in range(POOL_CH):
                    g, e = c // 2, c % 2
                    if c >= 2:
                        pe.wait_ge(yc, c - 1)
                    for k in range(2):
                        m = nc.tensor.matmul(PS[:, 6 + c % 2, 0:T], grpw[:, g, k, e * P:(e + 1) * P],
                                             ypool_in[:, 2 * g + k, :], start=(k == 0), stop=(k == 1))
                    m.then_inc(ym, 1)

            @block.scalar
            def _(act):
                nc.scalar.copy(qrT[:, :, :], PT[:, Q0:Q0 + NH, :]).then_inc(qcp, 1)
                for n in range(6):
                    t, v = n // 2, n % 2
                    w = P if t < TT else NS_TOK
                    act.wait_ge(vt, n + 1)
                    nc.scalar.copy(VR[0:w, t, v, :], PS[0:w, 4 + n % 2, :]).then_inc(vc, 1)
                act.wait_ge(pst, 64)
                for c in range(POOL_CH):
                    act.wait_ge(ym, c + 1)
                    nc.scalar.activation(ypoolT[:, c, :], PS[:, 6 + c % 2, 0:T], ACT.Copy,
                                         scale=pscale[:, c:c + 1]).then_inc(yc, 1)

            @block.vector
            def _(v):
                cos = cs[:, 0:1, :].to_broadcast([P, 4, T])
                sin = cs[:, 1:2, :].to_broadcast([P, 4, T])
                v.wait_ge(c2, 32)
                for n in range(6):
                    x = qrT[:, 4 * n:4 * n + 4, :] if n < 4 else PT[:, (KS0, KW0)[n - 4]:(KS0, KW0)[n - 4] + 4, :]
                    v.wait_ge(rq, n + 1)
                    nc.vector.tensor_tensor(rt[:, :, :], PS[:, 0:4, 0:T], sin, op=ALU.mult).then_inc(rd, 1)
                    nc.vector.tensor_tensor(rt2[:, :, :], x, cos, op=ALU.mult).then_inc(rd, 1)
                    v.wait_ge(rd, 3 * n + 2)
                    nc.vector.tensor_tensor(x, rt[:, :, :], rt2[:, :, :], op=ALU.add).then_inc(rd, 1)

            @block.gpsimd
            def _(g):
                n = [0]

                def link(ins):
                    n[0] += 1
                    ins.then_inc(pl, 1)
                    g.wait_ge(pl, n[0])

                g.wait_ge(pst, 64)
                nc.gpsimd.memset(EP[:, :, 0:POOL_ST], 0.0).then_inc(pl, 1)
                nc.gpsimd.tensor_copy(EP[:, :, POOL_ST:], PT[:, 0:POOL_CH, 0:NP_TOK]).then_inc(pl, 1)
                for c in range(POOL_CH):
                    nc.gpsimd.tensor_copy(ES[:, c, :, 0:POOL_ST], past[:, c, :].rearrange(
                        "p (b s) -> p b s", s=POOL_ST)).then_inc(pl, 1)
                    nc.gpsimd.tensor_copy(ES[:, c, :, POOL_ST:], PT[:, c, NP_TOK:T].rearrange(
                        "p (b l) -> p b l", l=LS)).then_inc(pl, 1)
                n[0] = 2 + 2 * POOL_CH
                g.wait_ge(pl, n[0])
                for c in range(POOL_CH):
                    w = 2 ** (c // 2 + 1)
                    a, b = EP[:, c, :], S1[:, :]
                    sa, sbf = ES[:, c, :, :], S2[:, :, :]
                    LP, LSx = POOL_ST + NP_TOK, POOL_ST + LS
                    sh = 1
                    while sh < w:
                        link(nc.gpsimd.tensor_tensor(b[:, sh:LP], a[:, sh:LP], a[:, 0:LP - sh], op=ALU.add))
                        link(nc.gpsimd.tensor_copy(a[:, sh:LP], b[:, sh:LP]))
                        link(nc.gpsimd.tensor_tensor(sbf[:, :, sh:LSx], sa[:, :, sh:LSx], sa[:, :, 0:LSx - sh], op=ALU.add))
                        link(nc.gpsimd.tensor_copy(sa[:, :, sh:LSx], sbf[:, :, sh:LSx]))
                        sh *= 2
                    link(nc.gpsimd.tensor_tensor(a[:, POOL_ST:POOL_ST + 16], a[:, POOL_ST:POOL_ST + 16],
                                                 rcnt[:, c // 2, :], op=ALU.mult))
                    link(nc.gpsimd.tensor_scalar(b[:, POOL_ST:], a[:, POOL_ST:], 1.0 / w, None, op0=ALU.mult))
                    link(nc.gpsimd.tensor_tensor(ypool_in[:, c, 0:NP_TOK], b[:, POOL_ST:], PT[:, c, 0:NP_TOK],
                                                 op=ALU.subtract))
                    link(nc.gpsimd.tensor_scalar(sbf[:, :, POOL_ST:], sa[:, :, POOL_ST:], 1.0 / w, None, op0=ALU.mult))
                    link(nc.gpsimd.tensor_tensor(ypool_in[:, c, NP_TOK:T].rearrange("p (b l) -> p b l", l=LS),
                                                 sbf[:, :, POOL_ST:],
                                                 PT[:, c, NP_TOK:T].rearrange("p (b l) -> p b l", l=LS),
                                                 op=ALU.subtract))
                nc.gpsimd.sem_inc(pd, 2)
        scope.close()

        kcb = sb(mid, "kcb", [P, NKV * BS * NCMP])
        kcbp = sb(mid, "kcbp", [P, NKV * NCMP])
        vcb = sb(mid, "vcb", [BS * NCMP, NKV, HD])
        pgi = sb(mid, "pgi", [P, 2 * BS], I32)
        vcbp = sb(mid, "vcbp", [NCMP, NKV, HD])
        scope = ExitStack()
        CT = sb(scope, "CT", [P, 2 * BS, NKV * P])
        W1 = sb(scope, "W1", [P, 32, HD])
        w2 = sb(scope, "w2", [P, 2, HD])
        peT = sb(scope, "peT", [P, 2, 32])
        ptab = sb(scope, "ptab", [P, 2 * BS], I32)
        ptf = sb(scope, "ptf", [P, 2 * BS])
        pidx = sb(scope, "pidx", [P, 1])
        A1 = sb(scope, "A1", [P, 512])
        A1p = sb(scope, "A1p", [P, 64])
        peb = sb(scope, "peb", [P, 1])
        HS = sb(scope, "HS", [P, NKV, BS, NCMP])
        HP = sb(scope, "HP", [P, NKV, NCMP])
        HG = sb(scope, "HG", [P, NKV * BS * NCMP])
        HGp = sb(scope, "HGp", [P, NKV * NCMP])
        c3 = sem("c3")
        w1_ld = sem("w1_ld")
        ix = sem("ix")
        ct_ld = sem("ct_ld")
        cm = sem("cm")
        cr = sem("cr")
        ch = sem("ch")
        cg = sem("cg")
        ck = sem("ck")
        ce = sem("ce")
        with nc.Block() as block:
            @block.sync
            def _(sp):
                sp.dma_start(ptab[:, :], ptab_d.rearrange("(o n) -> o n", o=1).to_broadcast([P, 2 * BS])).then_inc(c3, 16)
                sp.dma_start(pidx[:, :], pidx_d).then_inc(c3, 16)
                sp.dma_start(w2[:, :, :], w2_d).then_inc(c3, 16)
                sp.dma_start(peT[:, :, :], peT_d).then_inc(c3, 16)
                sp.dma_start(W1[:, :, :], w1_d[0]).then_inc(w1_ld, 16)
                sp.wait_ge(cm, 1)
                sp.dma_start(W1[:, :, :], w1_d[1]).then_inc(w1_ld, 16)

            @block.gpsimd
            def _(g):
                g.wait_ge(ix, 3)
                for kv in range(2):
                    if kv:
                        g.wait_ge(cm, 1)
                    for n in range(2 * BS):
                        nc.gpsimd.indirect_dma_start(
                            out=CT[:, n, :], out_offset=None, in_=(kcT_d, vcT_d)[kv],
                            in_offset=bass.IndirectOffsetOnAxis(ap=pgi[:, n:n + 1], axis=0)).then_inc(ct_ld, 16)

            @block.tensor
            def _(pe):
                pe.wait_ge(c3, 64)
                for kv in range(2):
                    pe.wait_ge(w1_ld, 16 * (kv + 1))
                    pe.wait_ge(ct_ld, 16 * 16 * (kv + 1))
                    if kv:
                        pe.wait_ge(ch, 4)
                    cv = CT[:, :, :].rearrange("p b (g c s) -> p (b g) c s", g=NKV, s=16)
                    c0 = (KC0, VC0)[kv]
                    pv = PT[:, c0:c0 + NKV, 0:NP_TOK].rearrange("p g (c s) -> p g c s", s=16)
                    for r in range(2):
                        for s in range(16):
                            w = W1[:, 16 * r + s, :]
                            nc.tensor.matmul(PS[:, r, :], w, cv[:, :, :, s], start=(s == 0), stop=(s == 15))
                            nc.tensor.matmul(PS[:, 2 + r, 0:64], w, pv[:, :, :, s], start=(s == 0), stop=(s == 15))
                            m = nc.tensor.matmul(PS[:, 4, 0:1], w, peT[:, kv, 16 * r + s:16 * r + s + 1],
                                                 start=(r == 0 and s == 0), stop=(r == 1 and s == 15))
                    m.then_inc(cm, 1)
                    pe.wait_ge(cg, 2 * (kv + 1))
                    if kv == 0:
                        nc.tensor.matmul(PS[:, 5, 0:480], w2[:, 0, :], HG[:, :], start=True, stop=True)
                        nc.tensor.matmul(PS[:, 6, 0:60], w2[:, 0, :], HGp[:, :], start=True, stop=True).then_inc(ck, 1)
                    else:
                        pe.wait_ge(ce, 2)
                        for g in range(NKV):
                            nc.tensor.matmul(PS[0:120, 5, g * P:(g + 1) * P], HG[:, g * 120:(g + 1) * 120], w2[:, 1, :],
                                             start=True, stop=True)
                            m = nc.tensor.matmul(PS[0:NCMP, 6, g * P:(g + 1) * P], HGp[:, g * NCMP:(g + 1) * NCMP],
                                                 w2[:, 1, :], start=True, stop=True)
                        m.then_inc(ck, 1)

            @block.scalar
            def _(act):
                for kv in range(2):
                    act.wait_ge(cm, kv + 1)
                    if kv:
                        act.wait_ge(ch, 4)
                    nc.scalar.copy(A1[:, :], PS[:, 1, :]).then_inc(cr, 1)
                    nc.scalar.copy(A1p[:, :], PS[:, 3, 0:64]).then_inc(cr, 1)
                    nc.scalar.copy(peb[:, :], PS[:, 4, 0:1]).then_inc(cr, 1)
                    act.wait_ge(cr, 3 * kv + 3)
                    act.wait_ge(ch, 4 * (kv + 1))
                    if kv:
                        act.wait_ge(ck, 1)
                    nc.scalar.activation(HG[:, :], HS[:, :, :, :].rearrange("p g b n -> p (g b n)"), ACT.Gelu,
                                         bias=peb[:, 0:1]).then_inc(cg, 1)
                    nc.scalar.activation(HGp[:, :], HP[:, :, :].rearrange("p g n -> p (g n)"), ACT.Gelu,
                                         bias=peb[:, 0:1]).then_inc(cg, 1)
                    act.wait_ge(ck, kv + 1)
                    if kv == 0:
                        nc.scalar.copy(kcb[:, :], PS[:, 5, 0:480]).then_inc(ce, 1)
                        nc.scalar.copy(kcbp[:, :], PS[:, 6, 0:60]).then_inc(ce, 1)
                    else:
                        nc.scalar.copy(vcb[:, :, :], PS[0:120, 5, :].rearrange("p (g d) -> p g d", g=NKV)).then_inc(ce, 1)
                        nc.scalar.copy(vcbp[:, :, :], PS[0:NCMP, 6, :].rearrange("p (g d) -> p g d", g=NKV)).then_inc(ce, 1)

            @block.vector
            def _(v):
                v.wait_ge(c3, 64)
                nc.vector.tensor_copy(ptf[:, :], ptab[:, :]).then_inc(ix, 1)
                v.wait_ge(ix, 1)
                nc.vector.tensor_scalar(ptf[:, :], ptf[:, :], float(P), pidx[:, 0:1], op0=ALU.mult, op1=ALU.add).then_inc(ix, 1)
                v.wait_ge(ix, 2)
                nc.vector.tensor_copy(pgi[:, :], ptf[:, :]).then_inc(ix, 1)
                a0 = PS[:, 0, :].rearrange("p (b q g c) -> p q g b c", b=BS, q=2, g=NKV)
                a1 = A1[:, :].rearrange("p (b q g c) -> p q g b c", b=BS, q=2, g=NKV)
                a0p = PS[:, 2, 0:64].rearrange("p (g c) -> p g c", g=NKV)
                a1p = A1p[:, :].rearrange("p (g c) -> p g c", g=NKV)
                for kv in range(2):
                    v.wait_ge(cr, 3 * (kv + 1))
                    if kv:
                        v.wait_ge(cg, 2)
                    nc.vector.tensor_tensor(HS[:, :, :, 0:7], a0[:, 0, :, :, 0:7], a1[:, 0, :, :, 1:8], op=ALU.add).then_inc(ch, 1)
                    nc.vector.tensor_tensor(HS[:, :, :, 7:8], a0[:, 0, :, :, 7:8], a1[:, 1, :, :, 0:1], op=ALU.add).then_inc(ch, 1)
                    nc.vector.tensor_tensor(HS[:, :, :, 8:15], a0[:, 1, :, :, 0:7], a1[:, 1, :, :, 1:8], op=ALU.add).then_inc(ch, 1)
                    nc.vector.tensor_tensor(HP[:, :, :], a0p[:, :, 0:15], a1p[:, :, 1:16], op=ALU.add).then_inc(ch, 1)
        scope.close()

        PcT = sb(mid, "PcT", [NCMP, NH, NP_TOK])
        PcS = sb(mid, "PcS", [BS * NCMP, NKV, P])
        grow = sb(mid, "grow", [P, TT, 3 * NH])
        gs = sb(mid, "gs", [P, 4, 3])
        scope = ExitStack()
        maskc = sb(scope, "maskc", [P, 2, 480])
        keepc = sb(scope, "keepc", [P, 2, 480])
        E = sb(scope, "E", [P, 2, 480])
        mx = sb(scope, "mx", [P, 2, 32])
        gc = sb(scope, "gc", [P, NKV])
        qS = sb(scope, "qS", [P, NH, NS_TOK])
        c4 = sem("c4")
        gt = sem("gt")
        s4 = sem("s4")
        d4 = sem("d4")
        e4 = sem("e4")
        t4 = sem("t4")
        k4 = sem("k4")
        k5 = sem("k5")
        with nc.Block() as block:
            @block.sync
            def _(sp):
                sp.dma_start(maskc[:, :, :], maskc_d).then_inc(c4, 16)
                sp.dma_start(keepc[:, :, :], keepc_d).then_inc(c4, 16)
                for g in range(NKV):
                    for j in range(HPG):
                        sp.dma_start(gc[j * 32:(j + 1) * 32, g:g + 1],
                                     gate_d[4 * g + j, NP_TOK:T].rearrange("(t o) -> t o", o=1)).then_inc(c4, 16)
                for h in range(NH):
                    for r in range(3):
                        sp.dma_start(gs[8 * h:8 * h + 8, :, r],
                                     gate_d[r * NH + h, NP_TOK:T].rearrange("(p x) -> x p", x=8),
                                     allow_slow_non_contiguous=True).then_inc(c4, 16)
            NC4 = 16 * (2 + 16 + 48)

            @block.tensor
            def _(pe):
                for t in range(TT):
                    m = nc.tensor.transpose(PS[:, 2, t * 48:t * 48 + 48], gateT[:, t * P:(t + 1) * P], ident[0:48, 0:48])
                m.then_inc(gt, 1)
                for h in range(NH):
                    for t in range(TT):
                        m = nc.tensor.matmul(PS[:, 0, (2 * h + t) * NCMP:(2 * h + t + 1) * NCMP],
                                             PT[:, Q0 + h, t * P:(t + 1) * P],
                                             kcbp[:, (h // HPG) * NCMP:(h // HPG + 1) * NCMP], start=True, stop=True)
                m.then_inc(s4, 1)
                pe.wait_ge(d4, 1)
                for g in range(NKV):
                    m = nc.tensor.matmul(PS[:, 1, g * 120:(g + 1) * 120],
                                         qS[:, 4 * g:4 * g + 4, :].rearrange("p h t -> p (h t)"),
                                         kcb[:, g * 120:(g + 1) * 120], start=True, stop=True)
                m.then_inc(s4, 1)
                pe.wait_ge(d4, 10)
                for n in range(8):
                    if n >= 2:
                        pe.wait_ge(k4, n - 1)
                    for j in range(4):
                        h, t = 2 * n + j // 2, j % 2
                        m = nc.tensor.transpose(PS[0:NCMP, 4 + n % 2, j * P:(j + 1) * P],
                                                E[:, 0, (2 * h + t) * NCMP:(2 * h + t + 1) * NCMP], ident[:, :])
                    m.then_inc(t4, 1)
                pe.wait_ge(d4, 19)
                for g in range(NKV):
                    m = nc.tensor.transpose(PS[0:120, 6, g * P:(g + 1) * P], E[:, 1, g * 120:(g + 1) * 120], ident[:, :])
                m.then_inc(t4, 1)

            @block.scalar
            def _(act):
                act.wait_ge(gt, 1)
                nc.scalar.copy(grow[:, :, :], PS[:, 2, 0:96].rearrange("p (t c) -> p t c", t=TT)).then_inc(e4, 1)
                for u in range(2):
                    act.wait_ge(d4, 1 + 9 * u + 3)
                    nc.scalar.activation(E[:, u, :], E[:, u, :], ACT.Exp).then_inc(e4, 1)
                for n in range(8):
                    act.wait_ge(t4, n + 1)
                    nc.scalar.copy(PcT[:, 2 * n:2 * n + 2, :], PS[0:NCMP, 4 + n % 2, :].rearrange(
                        "p (h t) -> p h t", h=2)).then_inc(k4, 1)
                act.wait_ge(t4, 9)
                nc.scalar.copy(PcS[:, :, :], PS[0:120, 6, :].rearrange("p (g t) -> p g t", g=NKV)).then_inc(k4, 1)

            @block.vector
            def _(v):
                n = [0]

                def link(ins):
                    n[0] += 1
                    ins.then_inc(d4, 1)
                    v.wait_ge(d4, n[0])

                link(nc.vector.tensor_copy(qS[:, :, :], PT[:, Q0:Q0 + NH, NP_TOK:T]))
                v.wait_ge(c4, NC4)
                for u in range(2):
                    A, B = (32, NCMP) if u == 0 else (4, 120)
                    e = E[:, u, :].rearrange("p (a b) -> p a b", a=A)
                    m = mx[:, 0, 0:A]
                    r = mx[:, 1, 0:A]
                    v.wait_ge(s4, u + 1)
                    link(nc.vector.scalar_tensor_tensor(out=E[:, u, :], in0=PS[:, u, 0:480], scalar=SCALE, in1=maskc[:, u, :],
                                                        op0=ALU.mult, op1=ALU.add))
                    link(nc.vector.tensor_reduce(m, e, AX, ALU.max))
                    link(nc.vector.tensor_tensor(e, e, m.unsqueeze(2).to_broadcast([P, A, B]), op=ALU.subtract))
                    v.wait_ge(e4, 2 + u)
                    link(nc.vector.tensor_tensor(E[:, u, :], E[:, u, :], keepc[:, u, :], op=ALU.mult))
                    link(nc.vector.tensor_reduce(r, e, AX, ALU.add))
                    link(nc.vector.tensor_scalar(r, r, 0.5, None, op0=ALU.max))
                    link(nc.vector.reciprocal(r, r))
                    if u == 0:
                        for t in range(TT):
                            ins = nc.vector.tensor_tensor(r.rearrange("p (h t) -> p h t", t=TT)[:, :, t],
                                                          r.rearrange("p (h t) -> p h t", t=TT)[:, :, t],
                                                          grow[:, t, 0:NH], op=ALU.mult)
                            if t == 0:
                                ins.then_inc(k5, 1)
                        link(ins)
                        v.wait_ge(k5, 1)
                    else:
                        link(nc.vector.tensor_tensor(r, r, gc[:, :], op=ALU.mult))
                    link(nc.vector.tensor_tensor(e, e, r.unsqueeze(2).to_broadcast([P, A, B]), op=ALU.mult))
        scope.close()

        NKS = NP_TOK + NS_TOK
        scope = ExitStack()
        KT = [sb(scope, f"KT{i}", [P, 2, 2, NKV * P]) for i in range(2)]
        V = [sb(scope, f"V{i}", [P, 2, 2, NKV * HD]) for i in range(2)]
        maskn = sb(scope, "maskn", [P, BS, NS_TOK])
        qcur = sb(scope, "qcur", [P, NH, 8])
        stg = sb(scope, "stg", [P, 4], I32)
        Pr = [sb(scope, f"Pr{i}", [P, NKS]) for i in range(2)]
        PTr = [sb(scope, f"PTr{i}", [P, 3, P]) for i in range(2)]
        st5 = sb(scope, "st5", [P, 2, 4])
        c5 = sem("c5")
        kv_ld = [sem(f"kv_ld{i}") for i in range(2)]
        kw_ld = [sem(f"kw_ld{i}") for i in range(2)]
        kv_fr = [sem(f"kv_fr{i}") for i in range(2)]
        stg_ok = sem("stg_ok")
        kv_own = sem("kv_own")
        q_ok = sem("q_ok")
        q_fr = sem("q_fr")
        s5 = sem("s5")
        a5 = sem("a5")
        e5 = sem("e5")
        b5 = sem("b5")
        t5 = sem("t5")
        k5b = sem("k5b")
        v5 = sem("v5")
        o5 = sem("o5")
        d5 = sem("d5")
        d5a = sem("d5a")
        cmp_o = sem("cmp_o")
        cmp_c = sem("cmp_c")

        def done(i, per, u):
            return i * per + (u + 3)

        def free(i, per, u):
            return i * per + (u + 1)

        with nc.Block() as block:
            @block.sync
            def _(sp):
                sp.dma_start(maskn[:, :, :], maskn_d).then_inc(c5, 16)
                with sp.Fori(0, BS // 2) as i:
                    for b in range(2):
                        sp.wait_ge(kv_fr[b], i + 1)
                        sp.dma_start(KT[b][:, 1, :, :].rearrange("p a n -> p (a n)"),
                                     kwT_d[bass.ds(2 * i + b, 1)].rearrange("o p n -> p (o n)")).then_inc(kw_ld[b], 16)
                        sp.dma_start(V[b][:, 1, :, :].rearrange("p a n -> p (a n)"),
                                     vw_d[bass.ds(2 * i + b, 1)].rearrange("o p n -> p (o n)")).then_inc(kw_ld[b], 16)

            @block.gpsimd
            def _(g):
                with g.Fori(0, BS // 2) as i:
                    g.wait_ge(kv_fr[0], i + 1)
                    g.sem_inc(kv_own, 1)
                    nc.gpsimd.tensor_copy(stg[:, :], pgi[:, bass.ds(i * 4, 4)]).then_inc(stg_ok, 1)
                    g.wait_ge(stg_ok, 1)
                    g.sem_clear(stg_ok)
                    for b in range(2):
                        if b:
                            g.wait_ge(kv_fr[1], i + 1)
                            g.sem_inc(kv_own, 1)
                        for pg in range(2):
                            for dst, src in ((KT[b], ksT_d), (V[b], vs_d)):
                                nc.gpsimd.indirect_dma_start(
                                    out=dst[:, 0, pg, :], out_offset=None, in_=src,
                                    in_offset=bass.IndirectOffsetOnAxis(ap=stg[:, 2 * b + pg:2 * b + pg + 1], axis=0)
                                ).then_inc(kv_ld[b], 16)

            @block.tensor
            def _(pe):
                for g in range(NKV):
                    m = nc.tensor.matmul(PS[:, 6, g * P:(g + 1) * P], vcb[:, g, :], PcS[:, g, :], start=True, stop=True)
                m.then_inc(cmp_o, 1)
                pe.sem_inc(kv_fr[0], 1)
                pe.sem_inc(kv_fr[1], 1)
                pe.sem_inc(q_fr, 1)
                for x in (s5, t5, v5):
                    pe.sem_inc(x, 2)
                with pe.Fori(0, BS // 2) as i:
                    for step in range(6):
                        if step < 4:
                            u = step
                            b, br = u // 2, u % 2
                            if u == 0:
                                pe.wait_ge(q_ok, i + 1)
                            if br == 0:
                                pe.wait_ge(kv_ld[b], i * 64 + 64)
                                pe.wait_ge(kw_ld[b], i * 32 + 32)
                            pe.wait_ge(a5, free(i, 4, u))
                            for g in range(NKV):
                                nc.tensor.matmul(PS[32 * g:32 * g + 32, u % 2, 0:NP_TOK],
                                                 qcur[:, 4 * g:4 * g + 4, :].rearrange("p h x -> p (h x)"),
                                                 KT[b][:, br, :, g * P:(g + 1) * P], start=True, stop=True,
                                                 tile_position=(0, 32 * g))
                                m = nc.tensor.matmul(PS[32 * g:32 * g + 32, u % 2, NP_TOK:NKS],
                                                     qcur[:, 4 * g:4 * g + 4, :].rearrange("p h x -> p (h x)"),
                                                     PT[:, (KS0, KW0)[br] + g, NP_TOK:T], start=True, stop=True,
                                                     tile_position=(0, 32 * g))
                            m.then_inc(s5, 1)
                        if 1 <= step <= 4:
                            u = step - 1
                            pe.wait_ge(b5, done(i, 4, u))
                            pe.wait_ge(k5b, free(i, 4, u))
                            for kb in range(3):
                                w = P if kb < 2 else NS_TOK
                                m = nc.tensor.transpose(PS[0:w, 2 + u % 2, kb * P:(kb + 1) * P],
                                                        Pr[u % 2][:, kb * P:kb * P + w], ident[:, :])
                            m.then_inc(t5, 1)
                        if step >= 2:
                            u = step - 2
                            b, br = u // 2, u % 2
                            pe.wait_ge(k5b, done(i, 4, u))
                            if br == 0:
                                pe.wait_ge(o5, i * 2 + b + 1)
                            for g in range(NKV):
                                for kb in range(3):
                                    w = P if kb < 2 else NS_TOK
                                    lhs = V[b][:, br, kb, g * P:(g + 1) * P] if kb < 2 else VR[0:w, 2, br, g * P:(g + 1) * P]
                                    rhs = PTr[u % 2][0:w, kb, :].rearrange("k (h x) -> k h x", x=8)[
                                        :, 4 * g:4 * g + 4, 4 * b:4 * b + 4]
                                    m = nc.tensor.matmul(PS[:, 4 + b, g * 16:(g + 1) * 16], lhs, rhs,
                                                         start=(br == 0 and kb == 0 and g == 0),
                                                         stop=(br == 1 and kb == 2), skip_group_check=True)
                            m.then_inc(v5, 1)
                            if br == 1:
                                pe.wait_ge(v5, done(i, 4, u))
                                pe.sem_inc(kv_fr[b], 1)
                                if b:
                                    pe.sem_inc(q_fr, 1)

            @block.scalar
            def _(act):
                act.wait_ge(cmp_o, 1)
                nc.scalar.copy(attnT[:, :, NP_TOK:T], PS[:, 6, :].rearrange("p (h t) -> p h t", h=NH)).then_inc(cmp_c, 1)
                for x in (e5, k5b):
                    act.sem_inc(x, 2)
                with act.Fori(0, BS // 2) as i:
                    for step in range(5):
                        if step < 4:
                            u = step
                            act.wait_ge(a5, done(i, 4, u))
                            nc.scalar.activation(Pr[u % 2][:, :], Pr[u % 2][:, :], ACT.Exp, bias=st5[:, u % 2, 0:1],
                                                 accum_out=st5[:, u % 2, 1:2]).then_inc(e5, 1)
                        if step >= 1:
                            u = step - 1
                            act.wait_ge(t5, done(i, 4, u))
                            act.wait_ge(v5, free(i, 4, u))
                            nc.scalar.copy(PTr[u % 2][:, 0:2, :], PS[:, 2 + u % 2, 0:256].rearrange(
                                "p (k r) -> p k r", k=2)).then_inc(d5a, 1)
                            nc.scalar.copy(PTr[u % 2][0:NS_TOK, 2, :], PS[0:NS_TOK, 2 + u % 2, 256:384]).then_inc(d5a, 1)
                            act.wait_ge(d5a, 2 * step)
                            act.sem_inc(k5b, 1)
                    act.sem_clear(d5a)

            @block.vector
            def _(v):
                for x in (a5, b5, o5):
                    v.sem_inc(x, 2)
                v.wait_ge(c5, 16)
                v.wait_ge(cmp_c, 1)
                with v.Fori(0, BS // 2) as i:
                    n = [0]

                    def link(ins):
                        n[0] += 1
                        ins.then_inc(d5, 1)
                        v.wait_ge(d5, n[0])

                    v.wait_ge(q_fr, i + 1)
                    nc.vector.tensor_copy(qcur[:, :, :], qrT[:, :, bass.ds(i * 8 + NP_TOK, 8)]).then_inc(q_ok, 1)
                    for step in range(5):
                        if step < 4:
                            u = step
                            b = u // 2
                            v.wait_ge(s5, done(i, 4, u))
                            v.wait_ge(t5, free(i, 4, u))
                            link(nc.vector.tensor_scalar(Pr[u % 2][:, 0:NP_TOK], PS[:, u % 2, 0:NP_TOK], SCALE, None,
                                                         op0=ALU.mult))
                            link(nc.vector.scalar_tensor_tensor(
                                out=Pr[u % 2][:, NP_TOK:NKS], in0=PS[:, u % 2, NP_TOK:NKS], scalar=SCALE,
                                in1=maskn[:, bass.ds(i * 2 + b, 1), :].rearrange("p o k -> p (o k)"),
                                op0=ALU.mult, op1=ALU.add))
                            link(nc.vector.tensor_reduce(st5[:, u % 2, 0:1], Pr[u % 2][:, :], AX, ALU.max))
                            link(nc.vector.tensor_scalar(st5[:, u % 2, 0:1], st5[:, u % 2, 0:1], -1.0, None, op0=ALU.mult))
                            v.sem_inc(a5, 1)
                        if step >= 1:
                            u = step - 1
                            br = u % 2
                            v.wait_ge(e5, done(i, 4, u))
                            link(nc.vector.reciprocal(st5[:, u % 2, 2:3], st5[:, u % 2, 1:2]))
                            link(nc.vector.tensor_tensor(st5[:, u % 2, 3:4], st5[:, u % 2, 2:3],
                                                         gs[:, bass.ds(i, 1), 1 + br], op=ALU.mult))
                            link(nc.vector.tensor_scalar(Pr[u % 2][:, :], Pr[u % 2][:, :], st5[:, u % 2, 3:4], None,
                                                         op0=ALU.mult))
                            v.sem_inc(b5, 1)
                    for b in range(2):
                        v.wait_ge(v5, done(i, 4, 2 * b + 1))
                        dst = attnT[:, :, bass.ds(i * 8 + (NP_TOK + 4 * b), 4)]
                        link(nc.vector.tensor_tensor(dst, dst, PS[:, 4 + b, 0:64].rearrange("p (h l) -> p h l", l=4),
                                                     op=ALU.add))
                        v.sem_inc(o5, 1)
                    v.sem_clear(d5)
        scope.close()

        NKP = 384
        scope = ExitStack()
        QR = sb(scope, "QR", [P, HPG, NP_TOK])
        VG = sb(scope, "VG", [P, TT, 2, HD])
        VCG = sb(scope, "VCG", [NCMP, HD])
        maskp = sb(scope, "maskp", [P, NKP])
        Pp = [sb(scope, f"Pp{i}", [P, NKP]) for i in range(2)]
        PTp = [sb(scope, f"PTp{i}", [P, NKP]) for i in range(2)]
        st6 = sb(scope, "st6", [P, 2, 4, TT])
        c6 = sem("c6")
        stg6 = sem("stg6")
        stg6_own = sem("stg6_own")
        s6, a6, e6, b6, t6, k6, v6, o6 = [sem(f"{x}6_") for x in "saebtkvo"]
        d6, d6a = sem("d6"), sem("d6a")
        SEG = ((0, P), (P, NKP))
        with nc.Block() as block:
            @block.sync
            def _(sp):
                sp.dma_start(maskp[:, :], maskp_d).then_inc(c6, 16)

            @block.gpsimd
            def _(g):
                with g.Fori(0, NKV) as i:
                    g.wait_ge(v6, i * 8 + 2)
                    g.sem_inc(stg6_own, 1)
                    nc.gpsimd.tensor_copy(QR[:, :, :], qrT[:, bass.ds(i * HPG, HPG), 0:NP_TOK]).then_inc(stg6, 1)
                    for t in range(TT):
                        nc.gpsimd.tensor_copy(VG[:, t, :, :], VR[:, t, :, bass.ds(i * HD, HD)]).then_inc(stg6, 1)
                    nc.gpsimd.tensor_copy(VCG[:, :], vcbp[:, bass.ds(i, 1), :].rearrange("p o d -> p (o d)")).then_inc(stg6, 1)

            @block.tensor
            def _(pe):
                for x in (s6, t6, v6):
                    pe.sem_inc(x, 2)
                with pe.Fori(0, NKV) as i:
                    pe.wait_ge(stg6, i * 4 + 4)
                    for step in range(10):
                        if step < 8:
                            u = step
                            j, br = u // 2, u % 2
                            key = PT[:, bass.ds(i + (KS0, KW0)[br], 1), :].rearrange("p o t -> p (o t)")
                            pe.wait_ge(a6, free(i, 8, u))
                            nc.tensor.matmul(PS[:, u % 2, 0:P], QR[:, j, 0:P], key[:, 0:P], start=True, stop=True)
                            nc.tensor.matmul(PS[:, u % 2, P:NKP], QR[:, j, P:NP_TOK], key[:, 0:NP_TOK],
                                             start=True, stop=True).then_inc(s6, 1)
                        if 1 <= step <= 8:
                            u = step - 1
                            pe.wait_ge(b6, done(i, 8, u))
                            pe.wait_ge(k6, free(i, 8, u))
                            for kb in range(3):
                                m = nc.tensor.transpose(PS[:, 2 + u % 2, kb * P:(kb + 1) * P],
                                                        Pp[u % 2][:, kb * P:(kb + 1) * P], ident[:, :])
                            m.then_inc(t6, 1)
                        if step >= 2:
                            u = step - 2
                            j, br = u // 2, u % 2
                            o = PS[:, 4 + j % 2, 0:NP_TOK]
                            pe.wait_ge(k6, done(i, 8, u))
                            if br == 0:
                                pe.wait_ge(o6, free(i, 4, j))
                                nc.tensor.matmul(o, VCG[:, :],
                                                 PcT[:, bass.ds(i * HPG + j, 1), :].rearrange("p o t -> p (o t)"),
                                                 start=True, stop=False, skip_group_check=True)
                            nc.tensor.matmul(o, VG[:, 0, br, :], PTp[u % 2][:, 0:NP_TOK], start=False, stop=False,
                                             skip_group_check=True)
                            nc.tensor.matmul(o[:, P:NP_TOK], VG[:, 1, br, :], PTp[u % 2][:, NP_TOK:NKP],
                                             start=False, stop=(br == 1), skip_group_check=True).then_inc(v6, 1)

            @block.scalar
            def _(act):
                for x in (e6, k6):
                    act.sem_inc(x, 2)
                with act.Fori(0, NKV) as i:
                    for step in range(9):
                        if step < 8:
                            u = step
                            act.wait_ge(a6, done(i, 8, u))
                            for t, (a, b) in enumerate(SEG):
                                m = nc.scalar.activation(Pp[u % 2][:, a:b], Pp[u % 2][:, a:b], ACT.Exp,
                                                         bias=st6[:, u % 2, 0, t:t + 1], accum_out=st6[:, u % 2, 1, t:t + 1])
                                m.then_inc(d6a, 1)
                            act.wait_ge(d6a, 2 * u + 2)
                            act.sem_inc(e6, 1)
                        if step >= 1:
                            u = step - 1
                            act.wait_ge(t6, done(i, 8, u))
                            act.wait_ge(v6, free(i, 8, u))
                            nc.scalar.copy(PTp[u % 2][:, :], PS[:, 2 + u % 2, 0:NKP]).then_inc(k6, 1)
                    act.sem_clear(d6a)

            @block.vector
            def _(v):
                for x in (a6, b6, o6):
                    v.sem_inc(x, 2)
                v.wait_ge(c6, 16)
                with v.Fori(0, NKV) as i:
                    n = [0]

                    def link(ins):
                        n[0] += 1
                        ins.then_inc(d6, 1)
                        v.wait_ge(d6, n[0])

                    for step in range(10):
                        if step < 8:
                            u = step
                            v.wait_ge(s6, done(i, 8, u))
                            v.wait_ge(t6, free(i, 8, u))
                            link(nc.vector.scalar_tensor_tensor(out=Pp[u % 2][:, :], in0=PS[:, u % 2, 0:NKP], scalar=SCALE,
                                                                in1=maskp[:, :], op0=ALU.mult, op1=ALU.add))
                            for t, (a, b) in enumerate(SEG):
                                link(nc.vector.tensor_reduce(st6[:, u % 2, 0, t:t + 1], Pp[u % 2][:, a:b], AX, ALU.max))
                            link(nc.vector.tensor_scalar(st6[:, u % 2, 0, :], st6[:, u % 2, 0, :], -1.0, None, op0=ALU.mult))
                            v.sem_inc(a6, 1)
                        if 1 <= step <= 8:
                            u = step - 1
                            j, br = u // 2, u % 2
                            v.wait_ge(e6, done(i, 8, u))
                            link(nc.vector.reciprocal(st6[:, u % 2, 2, :], st6[:, u % 2, 1, :]))
                            link(nc.vector.tensor_tensor(st6[:, u % 2, 3, :], st6[:, u % 2, 2, :],
                                                         grow[:, :, bass.ds(i * HPG + ((1 + br) * NH + j), 1)].rearrange(
                                                             "p t o -> p (t o)"), op=ALU.mult))
                            for t, (a, b) in enumerate(SEG):
                                link(nc.vector.tensor_scalar(Pp[u % 2][:, a:b], Pp[u % 2][:, a:b],
                                                             st6[:, u % 2, 3, t:t + 1], None, op0=ALU.mult))
                            v.sem_inc(b6, 1)
                        if step >= 3 and step % 2:
                            j = (step - 3) // 2
                            v.wait_ge(v6, done(i, 8, 2 * j + 1))
                            link(nc.vector.tensor_copy(attnT[:, bass.ds(i * HPG + j, 1), 0:NP_TOK].rearrange(
                                "p o t -> p (o t)"), PS[:, 4 + j % 2, 0:NP_TOK]))
                            v.sem_inc(o6, 1)
                    v.sem_clear(d6)
        scope.close()
        mid.close()
        proj.close()

        ring3 = ExitStack()
        W = [sb(ring3, f"wmix{s}", [P, DK, SLAB]) for s in range(SLOTS)]
        mergedT = sb(ring3, "mergedT", [P, DK, T])
        sg = sb(ring3, "sg", [P, 2, 2, T])
        pr = sb(ring3, "pr", [P, 2, 2, T])
        w7 = [sem(f"w7{s}") for s in range(SLOTS)]
        m7 = sem("m7")
        f7 = sem("f7")
        x7 = sem("x7")
        y7 = sem("y7")
        d7 = sem("d7")
        m8 = sem("m8")
        f8 = sem("f8")
        NPAIR = D // SLAB
        NIT8 = NPAIR // SLOTS
        with nc.Block() as block:
            @block.sync
            def _(sp):
                srcs = (gbr_d, gbr_d, wba_d, wbp_d)

                def load(n, s):
                    k = POOL_CH if s == 3 else DK
                    off = NPAIR if s == 1 else 0
                    sp.dma_start(W[s][:, 0:k, :], srcs[s][bass.ds(n + off, 1)].rearrange(
                        "a p (k c) -> p (a k) c", k=k)).then_inc(w7[s], 16)

                for s in range(SLOTS):
                    load(0, s)
                with sp.Fori(0, NPAIR - 1) as i:
                    for s in range(SLOTS):
                        sp.wait_ge(m7, i * 8 + 2 * (s + 1))
                        load(i + 1, s)
                for s in range(SLOTS):
                    sp.wait_ge(m7, (NPAIR - 1) * 8 + 2 * (s + 1))
                    sp.dma_start(W[s][:, :, :], wo_d[s].rearrange("p (k c) -> p k c", k=DK)).then_inc(w7[s], 16)
                for s in range(SLOTS):
                    sp.wait_ge(m8, 2 * (s + 1))
                    sp.dma_start(W[s][:, :, :], wo_d[SLOTS + s].rearrange("p (k c) -> p k c", k=DK)).then_inc(w7[s], 16)

            @block.tensor
            def _(pe):
                with pe.Fori(0, NPAIR) as i:
                    for s in range(SLOTS):
                        pe.wait_ge(w7[s], i * 16 + 16)
                        src, nk = ((xT, DK), (xT, DK), (attnT, DK), (ypoolT, POOL_CH))[s]
                        for j in range(2):
                            if s < 2:
                                pe.wait_ge(f7, i * 4 + 2 * s + j + 1)
                            else:
                                pe.wait_ge(x7, i * 4 + 2 * (s - 2) + j + 1)
                            for k in range(nk):
                                m = nc.tensor.matmul(PS[:, 2 * s + j, 0:T], W[s][:, k, j * P:(j + 1) * P], src[:, k, :],
                                                     start=(k == 0), stop=(k == nk - 1))
                            m.then_inc(m7, 1)
                pe.wait_ge(y7, D // P + 2)
                for n in range(NPAIR):
                    s = n % SLOTS
                    pe.wait_ge(w7[s], 16 * (NPAIR + n // SLOTS + 1))
                    for j in range(2):
                        c = 2 * n + j
                        if c >= 2:
                            pe.wait_ge(f8, c - 1)
                        for k in range(DK):
                            m = nc.tensor.matmul(PS[:, c % 2, 0:T], W[s][:, k, j * P:(j + 1) * P], mergedT[:, k, :],
                                                 start=(k == 0), stop=(k == DK - 1))
                        m.then_inc(m8, 1)

            @block.scalar
            def _(act):
                act.sem_inc(f7, 4)
                with act.Fori(0, NPAIR) as i:
                    for s in range(2):
                        for j in range(2):
                            act.wait_ge(m7, i * 8 + 2 * s + j + 1)
                            act.wait_ge(x7, i * 4 + 4)
                            nc.scalar.activation(sg[:, s, j, :], PS[:, 2 * s + j, 0:T], ACT.Sigmoid).then_inc(f7, 1)
                for c in range(DK):
                    act.wait_ge(m8, c + 1)
                    nc.scalar.copy(woT[:, c, :], PS[:, c % 2, 0:T]).then_inc(f8, 1)

            @block.vector
            def _(v):
                v.sem_inc(x7, 4)
                v.sem_inc(y7, 2)
                with v.Fori(0, NPAIR) as i:
                    v.wait_ge(f7, i * 4 + 8)
                    v.wait_ge(y7, i * 2 + 2)
                    for s in range(2):
                        for j in range(2):
                            v.wait_ge(m7, i * 8 + 4 + 2 * s + j + 1)
                            nc.vector.tensor_tensor(pr[:, s, j, :], PS[:, 4 + 2 * s + j, 0:T], sg[:, 1 - s, j, :],
                                                    op=ALU.mult).then_inc(x7, 1)
                    v.wait_ge(x7, i * 4 + 8)
                    nc.vector.tensor_tensor(mergedT[:, bass.ds(i * 2, 2), :], pr[:, 0, :, :], pr[:, 1, :, :],
                                            op=ALU.add).then_inc(y7, 2)
        ring3.close()

        scope = ExitStack()
        XR = sb(scope, "XR", [P, 3, D])
        lnp = sb(scope, "lnp", [P, 2, D])
        bst = sb(scope, "bst", [P, 3, 4, 6])
        mv = sb(scope, "mv", [P, 3, 2])
        rs = sb(scope, "rs", [P, 3, 2])
        eps = sb(scope, "eps", [P, 1])
        c8 = sem("c8")
        t9 = sem("t9")
        r9 = sem("r9")
        n9 = sem("n9")
        q9 = sem("q9")
        h9 = sem("h9")
        u9 = sem("u9")
        z9 = sem("z9")
        h_st = sem("h_st")
        wd = (P, P, NS_TOK)
        with nc.Block() as block:
            @block.sync
            def _(sp):
                sp.dma_start(XR[:, 0:TT, :], x_d[0:NP_TOK].rearrange("(t p) d -> p t d", p=P)).then_inc(c8, 16)
                sp.dma_start(XR[0:NS_TOK, 2, :], x_d[NP_TOK:T]).then_inc(c8, 16)
                for n in range(2):
                    sp.dma_start(lnp[:, n, :], ln_d[n:n + 1, :].to_broadcast([P, D])).then_inc(c8, 16)
                for t in range(3):
                    sp.wait_ge(h9, t + 1)
                    sp.dma_start(h_d[t * P:t * P + wd[t], :], XR[0:wd[t], t, :]).then_inc(h_st, 16)
                sp.wait_ge(h_st, 48)

            @block.tensor
            def _(pe):
                for t in range(3):
                    for q in range(4):
                        n = 4 * t + q
                        if n >= 2:
                            pe.wait_ge(r9, n - 1)
                        for j in range(4):
                            m = nc.tensor.transpose(PS[0:wd[t], n % 2, j * P:(j + 1) * P],
                                                    woT[:, 4 * q + j, t * P:t * P + wd[t]], ident[:, :])
                        m.then_inc(t9, 1)
                for t in range(3):
                    pe.wait_ge(h9, t + 1)
                    for q in range(4):
                        n = 4 * t + q
                        if n >= 2:
                            pe.wait_ge(z9, n - 1)
                        for j in range(4):
                            m = nc.tensor.transpose(PS[:, 2 + n % 2, j * P:j * P + wd[t]],
                                                    XR[0:wd[t], t, (4 * q + j) * P:(4 * q + j + 1) * P],
                                                    ident[0:wd[t], 0:wd[t]])
                        m.then_inc(u9, 1)

            @block.scalar
            def _(act):
                for t in range(3):
                    act.wait_ge(n9, t + 1)
                    nc.scalar.activation(rs[0:wd[t], t, 0:1], mv[0:wd[t], t, 1:2], ACT.Sqrt, bias=eps[0:wd[t], 0:1]).then_inc(q9, 1)
                for t in range(3):
                    for q in range(4):
                        act.wait_ge(u9, 4 * t + q + 1)
                        nc.scalar.copy(hT[:, 4 * q:4 * q + 4, t * P:t * P + wd[t]],
                                       PS[:, 2 + (4 * t + q) % 2, :].rearrange("p (j t) -> p j t", j=4)[:, :, 0:wd[t]]
                                       ).then_inc(z9, 1)

            @block.vector
            def _(v):
                n = [0]

                def link(ins):
                    n[0] += 1
                    ins.then_inc(d7, 1)
                    v.wait_ge(d7, n[0])

                link(nc.vector.memset(eps[:, :], EPS))
                v.wait_ge(c8, 64)
                for t in range(3):
                    w = wd[t]
                    for q in range(4):
                        x = XR[0:w, t, q * 512:(q + 1) * 512]
                        v.wait_ge(t9, 4 * t + q + 1)
                        nc.vector.scalar_tensor_tensor(out=x, in0=x, scalar=ALPHA, in1=PS[0:w, (4 * t + q) % 2, :],
                                                       op0=ALU.mult, op1=ALU.add).then_inc(r9, 1)
                        v.wait_ge(r9, 4 * t + q + 1)
                        link(nc.vector.bn_stats(bst[0:w, t, q, :], x))
                    link(nc.vector.bn_aggr(mv[0:w, t, :], bst[0:w, t, :, :]))
                    v.sem_inc(n9, 1)
                for t in range(3):
                    w = wd[t]
                    x = XR[0:w, t, :]
                    v.wait_ge(q9, t + 1)
                    link(nc.vector.reciprocal(rs[0:w, t, 1:2], rs[0:w, t, 0:1]))
                    link(nc.vector.tensor_scalar(x, x, mv[0:w, t, 0:1], rs[0:w, t, 1:2], op0=ALU.subtract, op1=ALU.mult))
                    link(nc.vector.tensor_tensor(x, x, lnp[0:w, 0, :], op=ALU.mult))
                    link(nc.vector.tensor_tensor(x, x, lnp[0:w, 1, :], op=ALU.add))
                    v.sem_inc(h9, 1)
        scope.close()

        scope = ExitStack()
        Sst = [sb(scope, f"Sst{i}", [P, 512]) for i in range(2)]
        W = [sb(scope, f"wq{s}", [P, DK, SLAB]) for s in range(SLOTS)]
        skT = sb(scope, "skT2", [P, 16, P])
        qg = [sb(scope, f"qg{i}", [P, 16, GT]) for i in range(2)]
        w9 = [sem(f"w9{s}") for s in range(SLOTS)]
        c9 = sem("c9")
        m9 = sem("m9")
        f9 = sem("f9")
        qg_ok = sem("qg_ok")
        sc_m = sem("sc_m")
        sc_c = sem("sc_c")
        sc_st = [sem(f"sc_st{i}") for i in range(2)]
        with nc.Block() as block:
            @block.sync
            def _(sp):
                for n in range(NPAIR):
                    s = n % SLOTS
                    if n >= SLOTS:
                        sp.wait_ge(m9, 2 * (n - SLOTS + 1))
                    sp.dma_start(W[s][:, :, :], wq_d[n].rearrange("p (k c) -> p k c", k=DK)).then_inc(w9[s], 16)
                sp.dma_start(skT[:, :, :], skT_d).then_inc(c9, 16)
                for gr in range(NG):
                    sp.wait_ge(sc_c, gr + 1)
                    sp.dma_start(score_d[gr], Sst[gr % 2][:, :]).then_inc(sc_st[gr % 2], 16)
                sp.wait_ge(sc_st[0], 16 * 5)
                sp.wait_ge(sc_st[1], 16 * 4)

            @block.tensor
            def _(pe):
                for n in range(NPAIR):
                    s = n % SLOTS
                    pe.wait_ge(w9[s], 16 * (n // SLOTS + 1))
                    for j in range(2):
                        c = 2 * n + j
                        if c >= 2:
                            pe.wait_ge(f9, c - 1)
                        for k in range(DK):
                            m = nc.tensor.matmul(PS[:, c % 2, 0:T], W[s][:, k, j * P:(j + 1) * P], hT[:, k, :],
                                                 start=(k == 0), stop=(k == DK - 1))
                        m.then_inc(m9, 1)
                pe.wait_ge(c9, 16)
                for gr in range(NG):
                    pe.wait_ge(qg_ok, gr + 1)
                    if gr >= 2:
                        pe.wait_ge(sc_c, gr - 1)
                    for h in range(8):
                        for hf in range(2):
                            m = nc.tensor.matmul(
                                PS[32 * (h // 2):32 * (h // 2) + 32, 2 + gr % 2,
                                   (2 * (h % 2) + hf) * P:(2 * (h % 2) + hf + 1) * P],
                                qg[gr % 2][:, 2 * h + hf, :], skT[:, 2 * h + hf, :], start=True, stop=True,
                                tile_position=(0, 32 * (h // 2)))
                    m.then_inc(sc_m, 1)

            @block.vector
            def _(v):
                v.wait_ge(f9, DK)
                for gr in range(NG):
                    if gr >= 2:
                        v.wait_ge(sc_m, gr - 1)
                    nc.vector.tensor_copy(qg[gr % 2][:, :, :], pqT[:, :, gr * GT:(gr + 1) * GT]).then_inc(qg_ok, 1)

            @block.scalar
            def _(act):
                for c in range(DK):
                    act.wait_ge(m9, c + 1)
                    nc.scalar.copy(pqT[:, c, :], PS[:, c % 2, 0:T]).then_inc(f9, 1)
                for gr in range(NG):
                    act.wait_ge(sc_m, gr + 1)
                    if gr >= 2:
                        act.wait_ge(sc_st[gr % 2], 16 * (gr // 2))
                    nc.scalar.copy(Sst[gr % 2][:, :], PS[:, 2 + gr % 2, :]).then_inc(sc_c, 1)
        scope.close()
        actT.close()

        Ur = [sb(top, f"Ur{s}", [P, D]) for s in range(SB)]
        Vr = [sb(top, f"Vr{s}", [P, D]) for s in range(SB)]
        hnext = sb(top, "hnext", [P, D])
        hcur = sb(top, "hcur", [P, D])
        hres = sb(top, "hres", [GT, D])
        R = sb(top, "R", [GT, D])
        lnq = sb(top, "lnq", [GT, 2, D])
        sel = sb(top, "sel", [P, GT])
        iot = sb(top, "iot", [P, 16])
        sw = sb(top, "sw", [P, 4, P])
        keys = sb(top, "keys", [P, 4, P])
        m16 = sb(top, "m16", [P, 4, 16])
        i16 = sb(top, "i16", [P, 4, 16], U32)
        i16f = sb(top, "i16f", [P, 4, 16])
        cand = sb(top, "cand", [P, 2, 256])
        tv = sb(top, "tv", [P, 2, 16])
        ti = sb(top, "ti", [P, 2, 16], U32)
        tab = sb(top, "tab", [P, 2, 2, 16], U32)
        tabf = sb(top, "tabf", [P, 2, 2, 16])
        oh = sb(top, "oh", [P, 2, 16, 16])
        es = sb(top, "es", [P, 2, 2, 16])
        ef = sb(top, "ef", [P, 2, 16])
        eid_next = sb(top, "eid_next", [P, NSTEP], I32)
        eid = sb(top, "eid", [P, 2, NSTEP], I32)
        gsum = sb(top, "gsum", [P, 2, 2])
        gate_next = sb(top, "gate_next", [P, NSTEP])
        gate = sb(top, "gate", [P, NSTEP])
        dots = sb(top, "dots", [P, 2, SB])
        gel = sb(top, "gel", [P, 2, SB])
        wgt = sb(top, "wgt", [P, 2, SB])
        Dm = sb(top, "Dm", [P, 2, SB, GT])
        bs2 = sb(top, "bs2", [GT, 4, 6])
        mv2 = sb(top, "mv2", [GT, 2])
        rs2 = sb(top, "rs2", [GT, 3])
        ep2 = sb(top, "ep2", [GT, 1])
        cA = sem("cA")
        h_ld, h_fr, h_ok = sem("h_ld"), sem("h_fr"), sem("h_ok")
        sw_ld, sw_fr = sem("sw_ld"), sem("sw_fr")
        top_ok = sem("top_ok")
        eid_ok, eid_own = sem("eid_ok"), sem("eid_own")
        exp_in, exp_ok = sem("exp_in"), sem("exp_ok")
        u_ld = [sem(f"u_ld{s}") for s in range(SB)]
        v_ld = [sem(f"v_ld{s}") for s in range(SB)]
        dot = sem("dot")
        gelu = sem("gelu")
        dm = sem("dm")
        pv = sem("pv")
        z_fr = sem("z_fr")
        ln_a, ln_s, ln_b, ln_c = sem("ln_a"), sem("ln_s"), sem("ln_b"), sem("ln_c")
        y_st, r_fr = sem("y_st"), sem("r_fr")
        dA = sem("dA")
        gathers = sem("gathers")
        with nc.Block() as block:
            @block.sync
            def _(sp):
                sp.dma_start(sel[:, :], sel_d).then_inc(cA, 16)
                sp.dma_start(iot[:, :], iota_d).then_inc(cA, 16)
                for n in range(2):
                    sp.dma_start(lnq[:, n, :], ln_d[2 + n:3 + n, :].to_broadcast([GT, D])).then_inc(cA, 16)

                def load_scores(gr):
                    sp.wait_ge(sw_fr, gr + 1)
                    sp.dma_start(sw[:, :, :].rearrange("p a k -> p (a k)"),
                                 score_d[bass.ds(gr, 1)].rearrange("o p k -> (o p) k")).then_inc(sw_ld, 16)

                def load_h(gr):
                    sp.wait_ge(h_fr, gr + 1)
                    for q in range(4):
                        sp.dma_start(hnext[32 * q:32 * q + 32, :], h_d[bass.ds(gr * GT, GT)]).then_inc(h_ld, 16)

                def store_y(gr):
                    sp.wait_ge(ln_c, gr + 1)
                    sp.dma_start(y_d[bass.ds(gr * GT, GT)], R[:, :]).then_inc(y_st, 16)
                    sp.wait_ge(y_st, gr * 16 + 16)
                    sp.sem_inc(r_fr, 1)

                sp.sem_inc(r_fr, 1)
                load_scores(0)
                load_h(0)
                load_scores(1)
                load_h(1)
                with sp.Fori(0, NG - 2) as i:
                    load_scores(i + 2)
                    load_h(i + 2)
                    store_y(i)
                store_y(NG - 2)
                store_y(NG - 1)
                sp.wait_ge(y_st, 16 * NG)
                sp.wait_ge(out_done, 16 * n_out[0])

            @block.gpsimd
            def _(g):
                def group(gr, par):
                    g.wait_ge(top_ok, gr + 1)
                    g.sem_inc(gathers, 1)
                    nc.gpsimd.tensor_copy(eid[:, par, :], eid_next[:, :]).then_inc(eid_own, 1)
                    g.wait_ge(eid_own, 1)
                    g.sem_clear(eid_own)
                    g.sem_inc(eid_ok, 1)
                    for b in range(NB):
                        for s in range(SB):
                            c = b * SB + s
                            g.wait_ge(dot, gr * NSTEP + (c + 1))
                            g.sem_inc(gathers, 1)
                            nc.gpsimd.indirect_dma_start(
                                out=Ur[s][:, :], out_offset=None, in_=u_d,
                                in_offset=bass.IndirectOffsetOnAxis(ap=eid[:, par, c:c + 1], axis=0)).then_inc(u_ld[s], 16)
                        for s in range(SB):
                            c = b * SB + s
                            g.wait_ge(pv, gr * NSTEP + (c + 1))
                            g.sem_inc(gathers, 1)
                            nc.gpsimd.indirect_dma_start(
                                out=Vr[s][:, :], out_offset=None, in_=v_d,
                                in_offset=bass.IndirectOffsetOnAxis(ap=eid[:, par, c:c + 1], axis=0)).then_inc(v_ld[s], 16)


                with g.Fori(0, NG // 2) as i:
                    group(2 * i, 0)
                    group(2 * i + 1, 1)
                group(NG - 1, (NG - 1) % 2)

            @block.tensor
            def _(pe):
                pe.sem_inc(pv, SB)
                with pe.Fori(0, NG) as i:
                    pe.wait_ge(z_fr, i + 1)
                    for b in range(NB):
                        pe.wait_ge(dm, i * NB + (b + 1))
                        for s in range(SB):
                            pe.wait_ge(v_ld[s], i * (16 * NB) + 16 * (b + 1))
                            for q in range(4):
                                m = nc.tensor.matmul(PS[0:GT, q, :], Dm[:, b % 2, s, :], Vr[s][:, q * 512:(q + 1) * 512],
                                                     start=(b == 0 and s == 0), stop=(b == NB - 1 and s == SB - 1),
                                                     tile_position=(0, 0))
                            m.then_inc(pv, 1)

            @block.scalar
            def _(act):
                act.sem_inc(h_fr, 1)

                def exps(gr):
                    act.wait_ge(exp_in, gr + 1)
                    nc.scalar.activation(gate_next[:, :], tv[:, :, :].rearrange("p h k -> p (h k)"), ACT.Exp).then_inc(exp_ok, 1)

                def group(gr, first, last):
                    act.wait_ge(h_ld, gr * 64 + 64)
                    act.wait_ge(dot, gr * NSTEP + SB)
                    if not first:
                        act.wait_ge(h_ok, 2 * gr)
                    nc.scalar.copy(hcur[:, :], hnext[:, :]).then_inc(h_ok, 1)
                    act.wait_ge(h_ok, 2 * gr + 1)
                    act.sem_inc(h_fr, 1)
                    for b in range(NB):
                        act.wait_ge(dot, gr * NSTEP + (b + 2) * SB)
                        nc.scalar.activation(gel[:, b % 2, :], dots[:, b % 2, :], ACT.Gelu).then_inc(gelu, 1)
                        if b == 0 and not first:
                            norm(gr - 1)
                        if b == 1 and not last:
                            exps(gr + 1)
                    if not first:
                        act.wait_ge(z_fr, gr + 1)
                    nc.scalar.copy(hres[:, :], hcur[0:GT, :]).then_inc(h_ok, 1)

                def norm(gr):
                    act.wait_ge(ln_a, gr + 1)
                    nc.scalar.activation(rs2[:, 0:1], mv2[:, 1:2], ACT.Sqrt, bias=ep2[:, 0:1]).then_inc(ln_s, 1)

                exps(0)
                group(0, True, False)
                with act.Fori(1, NG - 1) as i:
                    group(i, False, False)
                group(NG - 1, False, True)
                norm(NG - 1)

            @block.vector
            def _(v):
                n = [0]

                def link(ins):
                    n[0] += 1
                    ins.then_inc(dA, 1)
                    v.wait_ge(dA, n[0])

                def unlink():
                    v.sem_clear(dA)
                    n[0] = 0

                def top16(vals, idx, src):
                    link(nc.vector.max(vals[:, 0:8], src))
                    link(nc.vector.max_index(idx[:, 0:8], vals[:, 0:8], src))
                    link(nc.vector.match_replace(src, vals[:, 0:8], src, NEG))
                    link(nc.vector.max(vals[:, 8:16], src))
                    link(nc.vector.max_index(idx[:, 8:16], vals[:, 8:16], src))

                def choose(gr):
                    v.wait_ge(sw_ld, gr * 16 + 16)
                    link(nc.vector.tensor_copy(keys[:, :, :], sw[:, :, :]))
                    v.sem_inc(sw_fr, 1)
                    for a in range(4):
                        top16(m16[:, a, :], i16[:, a, :], keys[:, a, :])
                    mh = m16[:, :, :].rearrange("p (h f) k -> p h f k", f=2)
                    for h in range(2):
                        link(nc.vector.tensor_tensor(cand[:, h, :].rearrange("p (i j) -> p i j", i=16),
                                                     mh[:, h, 0, :].unsqueeze(2).to_broadcast([P, 16, 16]),
                                                     mh[:, h, 1, :].unsqueeze(1).to_broadcast([P, 16, 16]), op=ALU.add))
                    link(nc.vector.tensor_copy(i16f[:, :, :], i16[:, :, :]))
                    for h in range(2):
                        top16(tv[:, h, :], ti[:, h, :], cand[:, h, :])
                    link(nc.vector.tensor_copy(gsum[:, :, 0:1], tv[:, :, 0:1]))
                    link(nc.vector.tensor_tensor(tv[:, :, :], tv[:, :, :], gsum[:, :, 0:1].to_broadcast([P, 2, 16]),
                                                 op=ALU.subtract))
                    v.sem_inc(exp_in, 1)
                    link(nc.vector.tensor_scalar(tab[:, 0, :, :], ti[:, :, :], 4, None, op0=ALU.logical_shift_right))
                    link(nc.vector.tensor_scalar(tab[:, 1, :, :], ti[:, :, :], 15, None, op0=ALU.bitwise_and))
                    link(nc.vector.tensor_copy(tabf[:, :, :, :], tab[:, :, :, :]))
                    fh = i16f[:, :, :].rearrange("p (h f) k -> p h f k", f=2)
                    for f in range(2):
                        for h in range(2):
                            link(nc.vector.tensor_tensor(oh[:, h, :, :],
                                                         tabf[:, f, h, :].unsqueeze(2).to_broadcast([P, 16, 16]),
                                                         iot[:, :].unsqueeze(1).to_broadcast([P, 16, 16]),
                                                         op=ALU.is_equal))
                            link(nc.vector.tensor_tensor(oh[:, h, :, :], oh[:, h, :, :],
                                                         fh[:, h, f, :].unsqueeze(1).to_broadcast([P, 16, 16]),
                                                         op=ALU.mult))
                        link(nc.vector.tensor_reduce(es[:, f, :, :], oh[:, :, :, :], AX, ALU.add))
                    link(nc.vector.tensor_scalar(es[:, 0, :, :], es[:, 0, :, :], 128.0, None, op0=ALU.mult))
                    link(nc.vector.tensor_tensor(ef[:, :, :], es[:, 0, :, :], es[:, 1, :, :], op=ALU.add))
                    v.wait_ge(eid_ok, gr + 1)
                    link(nc.vector.tensor_copy(eid_next[:, :], ef[:, :, :].rearrange("p h k -> p (h k)")))
                    v.sem_inc(top_ok, 1)
                    v.wait_ge(exp_ok, gr + 1)
                    gn = gate_next[:, :].rearrange("p (h k) -> p h k", h=2)
                    link(nc.vector.tensor_reduce(gsum[:, :, 0], gn, AX, ALU.add))
                    link(nc.vector.reciprocal(gsum[:, :, 1], gsum[:, :, 0]))
                    link(nc.vector.tensor_tensor(gn, gn, gsum[:, :, 1:2].to_broadcast([P, 2, 16]), op=ALU.mult))
                    unlink()

                def norm_a(gr):
                    v.wait_ge(pv, gr * NSTEP + (NSTEP + SB))
                    v.wait_ge(h_ok, 2 * gr + 2)
                    v.wait_ge(r_fr, gr + 1)
                    link(nc.vector.scalar_tensor_tensor(out=R[:, :], in0=hres[:, :], scalar=ALPHA,
                                                        in1=PS[0:GT, 0:4, :].rearrange("p q d -> p (q d)"),
                                                        op0=ALU.mult, op1=ALU.add))
                    v.sem_inc(z_fr, 1)
                    for q in range(4):
                        link(nc.vector.bn_stats(bs2[:, q, :], R[:, q * 512:(q + 1) * 512]))
                    link(nc.vector.bn_aggr(mv2[:, :], bs2[:, :, :]))
                    v.sem_inc(ln_a, 1)
                    unlink()

                def norm_b(gr):
                    v.wait_ge(ln_s, gr + 1)
                    link(nc.vector.reciprocal(rs2[:, 1:2], rs2[:, 0:1]))
                    link(nc.vector.tensor_scalar(R[:, :], R[:, :], mv2[:, 0:1], rs2[:, 1:2], op0=ALU.subtract, op1=ALU.mult))
                    link(nc.vector.tensor_tensor(R[:, :], R[:, :], lnq[:, 0, :], op=ALU.mult))
                    link(nc.vector.tensor_tensor(R[:, :], R[:, :], lnq[:, 1, :], op=ALU.add))
                    v.sem_inc(ln_c, 1)
                    unlink()

                def group(gr, first, last):
                    link(nc.vector.tensor_copy(gate[:, :], gate_next[:, :]))
                    unlink()
                    v.wait_ge(h_ok, 2 * gr + 1)
                    for b in range(NB):
                        for s in range(SB):
                            v.wait_ge(u_ld[s], gr * (16 * NB) + 16 * (b + 1))
                            nc.vector.tensor_tensor_reduce(out=Ur[s][:, :], in0=Ur[s][:, :], in1=hcur[:, :], scale=1.0,
                                                           scalar=0.0, op0=ALU.mult, op1=ALU.add,
                                                           accum_out=dots[:, b % 2, s:s + 1]).then_inc(dot, 1)
                        v.wait_ge(gelu, gr * NB + (b + 1))
                        link(nc.vector.tensor_tensor(wgt[:, b % 2, :], gel[:, b % 2, :], gate[:, b * SB:(b + 1) * SB],
                                                     op=ALU.mult))
                        if b or not first:
                            v.wait_ge(pv, gr * NSTEP + b * SB)
                        link(nc.vector.tensor_tensor(Dm[:, b % 2, :, :],
                                                     sel[:, :].unsqueeze(1).to_broadcast([P, SB, GT]),
                                                     wgt[:, b % 2, :].unsqueeze(2).to_broadcast([P, SB, GT]), op=ALU.mult))
                        v.sem_inc(dm, 1)
                        unlink()
                        if b == 0 and not first:
                            norm_a(gr - 1)
                        if b == 1 and not first:
                            norm_b(gr - 1)
                        if b == 1 and not last:
                            choose(gr + 1)

                v.sem_inc(dot, SB)
                for x in (sw_fr, eid_ok, z_fr):
                    v.sem_inc(x, 1)
                link(nc.vector.memset(ep2[:, :], EPS))
                unlink()
                v.wait_ge(cA, 64)
                choose(0)
                group(0, True, False)
                with v.Fori(1, NG - 1) as i:
                    group(i, False, False)
                group(NG - 1, False, True)
                norm_a(NG - 1)
                norm_b(NG - 1)


_OUTS = [("y", (T, D)), ("kvT", (P, 6, NKV, T)), ("ktail", (BS, 252, 512)), ("vtail", (BS, 252, 512)),
         ("poolT", (P, POOL_CH, POOL_ST + NS_TOK)), ("spool", (BS, 11, 1024))]


def constants(np):
    f = np.float32
    p = np.arange(P)
    ident = np.eye(P, dtype=f)
    rot = np.zeros((P, P), f)
    for m in range(32):
        rot[(m + 16) % 32, m] = 1.0
    pos = np.concatenate([np.arange(NP_TOK), np.tile(256 + np.arange(LS), BS)]).astype(f)
    inv = (f(500000.0) ** (-np.arange(16, dtype=f) / f(16))).astype(f)
    ang = (pos[:, None] * inv).astype(f)
    cs = np.zeros((P, 2, T), f)
    cs[:, 0] = 1.0
    cs[0:16, 0] = cs[16:32, 0] = np.cos(ang).T
    cs[0:16, 1] = -np.sin(ang).T
    cs[16:32, 1] = np.sin(ang).T
    big = f(-1e30)
    diag = np.where(p[None, :] <= p[:, None], f(0), big).astype(f)
    maskp = np.concatenate([diag, np.zeros((P, P), f), diag], 1)
    x = p % 8
    maskn = np.full((P, BS, NS_TOK), big, f)
    for b in range(BS):
        for l2 in range(LS):
            maskn[:, b, b * LS + l2] = np.where(l2 <= x % LS, f(0), big)
    maskc = np.zeros((P, 2, 480), f)
    n = np.arange(NCMP)
    for t in range(TT):
        ok = 16 * n[None, :] + 31 <= (t * P + p)[:, None]
        maskc[:, 0].reshape(P, NH, TT, NCMP)[:, :, t, :] = np.where(ok, f(0), big)[:, None, :]
    rb = (p % 32) // LS
    ok = rb[:, None] == np.arange(BS)[None, :]
    maskc[:, 1].reshape(P, NKV, BS, NCMP)[:] = np.where(ok, f(0), big)[:, None, :, None]
    keepc = (maskc == 0).astype(f)
    rcnt = np.ones((P, 4, 16), f)
    for g, w in enumerate((2, 4, 8, 16)):
        rcnt[:, g] = (w / np.minimum(w, np.arange(16) + 1)).astype(f)
    sel = (p[:, None] % GT == np.arange(GT)[None, :]).astype(f)
    iota = np.tile(np.arange(16, dtype=f), (P, 1))
    pidx = p.astype(f)[:, None].copy()
    return dict(ident=ident, rot=rot, cs=cs, maskp=maskp, maskn=maskn, maskc=maskc, keepc=keepc, rcnt=rcnt,
                sel=sel, iota=iota, pidx=pidx)


def kernel(**inputs):
    import numpy as np
    import concourse.bacc as _bacc
    from concourse.bass_utils import run_bass_kernel_spmd as _run

    a = {k: np.asarray(v) for k, v in inputs.items()}

    def slabs(w):
        k, n = w.shape
        return w.reshape(k // P, P, n // SLAB, SLAB).transpose(2, 1, 0, 3).reshape(n // SLAB, P, (k // P) * SLAB)

    def pagesT(c):
        return c[0].transpose(0, 3, 2, 1).reshape(-1, NKV * P)

    x = np.concatenate([a["x_prompt"][0], a["x_sample"].reshape(NS_TOK, D)], 0)
    w_in = a["w_in"][0]
    kwin = a["cache_k_win"][0].reshape(BS, 256, 512)
    vwin = a["cache_v_win"][0].reshape(BS, 256, 512)
    arrays = dict(
        xT=x.T, x=x, win=slabs(w_in[:, :6144]),
        nsa=w_in[:, 6144:6192].reshape(DK, P, 48).transpose(1, 0, 2),
        gbr=slabs(w_in[:, 6192:]), wbp=slabs(a["w_branch_pool"][0]), wba=slabs(a["w_branch_attn"][0]),
        wo=slabs(a["w_out"][0]), wq=slabs(a["peer_wq"][0]), grp=a["pool_grp_w"][0],
        pscale=a["pool_scale"][0].reshape(POOL_CH, P).T,
        stateT=a["state_pool"][0].transpose(2, 0, 1).reshape(1024, BS * POOL_ST), state=a["state_pool"][0],
        kcT=pagesT(a["cache_k_cmp"]), vcT=pagesT(a["cache_v_cmp"]), ksT=pagesT(a["cache_k_slc"]),
        vs=a["cache_v_slc"][0].reshape(-1, 512),
        kwT=kwin.reshape(BS, 2, P, NKV, HD).transpose(0, 4, 1, 3, 2).reshape(BS, P, 1024),
        vw=vwin.reshape(BS, 2, P, 512).transpose(0, 2, 1, 3).reshape(BS, P, 1024),
        kwin=kwin, vwin=vwin, ptab=a["page_table"].reshape(-1),
        w1=np.stack([a["cmp_w1_k"][0].transpose(1, 0, 2), a["cmp_w1_v"][0].transpose(1, 0, 2)]),
        w2=np.stack([a["cmp_w2_k"][0], a["cmp_w2_v"][0]], 1),
        peT=np.stack([a["cmp_pe_k"][0].T, a["cmp_pe_v"][0].T], 1),
        ln=np.stack([a["ln1_g"][0], a["ln1_b"][0], a["ln2_g"][0], a["ln2_b"][0]]),
        skT=a["peer_subkeys"][0].reshape(16, P, P).transpose(2, 0, 1), u=a["peer_u"][0], v=a["peer_v"][0])
    arrays.update(constants(np))
    nc = _bacc.Bacc("TRN2", target_bir_lowering=False, num_devices=1)
    feeds, args = {}, []
    for name, arr in arrays.items():
        feeds[f"in_{name}"] = np.ascontiguousarray(arr)
        args.append(nc.dram_tensor(f"in_{name}", arr.shape, mybir.dt.from_np(arr.dtype), kind="ExternalInput").ap())
    for name, shape in _OUTS:
        args.append(nc.dram_tensor(f"out_{name}", shape, F32, kind="ExternalOutput").ap())
    build(nc, *args)
    r = _run(nc, [feeds], core_ids=[0]).results[0]
    y, kvT, ktail, vtail, poolT, spool = [r[f"out_{name}"] for name, _ in _OUTS]
    kv = kvT.transpose(1, 3, 2, 0)
    kv_p = [kv[n, :NP_TOK][None, None] for n in range(6)]
    kv_s = [kv[n, NP_TOK:].reshape(1, BS, LS, NKV, HD) for n in range(6)]

    def tail(old, new):
        return np.concatenate([old.reshape(1, BS, 252, NKV, HD), new], 2)

    pool = poolT.transpose(2, 1, 0).reshape(POOL_ST + NS_TOK, 1024)
    pool_s = np.concatenate([spool, pool[POOL_ST:].reshape(BS, LS, 1024)], 1)[None]
    return (y[None, :NP_TOK], y[NP_TOK:].reshape(BS, LS, D), *kv_p, pool[None, None, :POOL_ST], *kv_s[:4],
            tail(ktail, kv_s[4]), tail(vtail, kv_s[5]), pool_s)
```

```python
import math
from contextlib import ExitStack

import concourse.bass as bass
from concourse import mybir

F32 = mybir.dt.float32
F32R = mybir.dt.float32r
U32 = mybir.dt.uint32
I32 = mybir.dt.int32
ALU = mybir.AluOpType
ACT = mybir.ActivationFunctionType
AX = mybir.AxisListType.X

P = 128
D = 2048
DK = D // P
NP_TOK = 256
NS_TOK = 32
T = NP_TOK + NS_TOK
TT = 2
BS = 8
LS = 4
NKV = 4
HPG = 4
NH = 16
HD = 128
NCMP = 15
NCHUNK = 16
POOL_CH = 8
POOL_ST = 15
SCALE = float(HD) ** -0.5
ALPHA = 2.0 ** 0.25
EPS = 1e-5
SLOTS = 4
Q0, KS0, KW0, KC0, VC0, VS0, VW0 = 8, 24, 28, 32, 36, 40, 44
N1 = 48
L_QKV, L_POOL, L_GP, L_GA, L_BP, L_BA, L_WO, L_WQ = 0, 40, 48, 64, 80, 88, 104, 120
N_LOADS = 136
GT = 32
NG = T // GT
NSTEP = 32
SB = 8
NB = NSTEP // SB
NEG = -3.0e38


def build(nc, xT_d, x_d, w_d, nsa_d, grp_d, pscale_d, stateT_d,
          state_d, kcT_d, vcT_d, ksT_d, vs_d, kwT_d, vw_d, kwin_d, vwin_d, ptab_d, w1_d, w2_d, peT_d,
          ln_d, skT_d, u_d, v_d, ident_d, rot_d, cs_d, maskp_d, maskn_d, maskc_d, keepc_d, rcnt_d,
          sel_d, iota_d, pidx_d,
          y_d, kvT_d, ktail_d, vtail_d, poolT_d, spool_d):
    h_d = nc.dram_tensor("h_rows", (T, D), F32).ap()
    gate_d = nc.dram_tensor("sample_gates", (3 * NH, NS_TOK), F32).ap()
    gatep_d = nc.dram_tensor("sample_gates_by_pair", (3 * NH, 8, 4), F32).ap()
    score_d = nc.dram_tensor("peer_scores", (NG, P, 512), F32).ap()
    top = ExitStack()

    def sem(name):
        return top.enter_context(nc.semaphore(name))

    def sb(scope, name, shape, dt=F32):
        buf = scope.enter_context(nc.sbuf_tensor(name, shape, dt))
        place[name] = nc.sbuf_base - 4 * math.prod(shape[1:])
        return buf

    place = {}

    def in_place_of(name, shape):
        return nc.alloc_sbuf_tensor_at(name + "_r", shape, F32R, offset=place[name])

    with top:
        PS = top.enter_context(nc.psum_tensor("PS", [P, 8, 512], F32))
        ident = sb(top, "ident", [P, P])
        rings = ExitStack()
        ring = [sb(rings, f"ring{s}", [P, DK, P]) for s in range(SLOTS)]
        ring_lo = [in_place_of(f"ring{s}", [P, DK, P]) for s in range(SLOTS)]
        lds = [sem(f"lds{s}") for s in range(SLOTS)]
        gd = sem("gd")
        ge = sem("ge")
        out_done = sem("out_done")
        raw_out = sem("raw_out")
        pool_out = sem("pool_out")
        n_out = [0]

        def out_dma(eng, dst, src):
            n_out[0] += 1
            eng.dma_start(dst, src).then_inc(out_done, 16)

        GB = 6

        def product(n):
            return n + 1 + min(max(n + 1 - L_BP, 0), L_BA - L_BP)

        w_hi, w_lo = sem("w_hi"), sem("w_lo")
        wh = [None]

        def split(n):
            return n + 1 if n < L_POOL else n + 1 - (L_BP - L_POOL)

        def load(sp, n, s):
            sp.dma_start(ring[s][:, :, :], w_d[bass.ds(n, 1)].rearrange("o p (k c) -> p (o k) c", k=DK)).then_inc(lds[s], 16)

        def next_loads(sp, first, count, per=1):
            count = min(count, N_LOADS - SLOTS - first)
            with sp.Fori(0, count // SLOTS) as i:
                for s in range(SLOTS):
                    sp.wait_ge(gd, i * (SLOTS * per) + (product(first) + s * per))
                    load(sp, i * SLOTS + (first + SLOTS + s), s)

        def gemm(pe, n, i, j, src, part=(0, DK)):
            if part[0] == 0:
                pe.wait_ge(lds[j], i * 16 + 16 * ((n + j) // SLOTS + 1))
                pe.wait_ge(ge, i * SLOTS + product(n + j))
            for k in range(*part):
                m = nc.tensor.matmul(PS[:, GB + (product(n + j) - 1) % 2, 0:T], ring[j][:, k, :], src[:, k, :],
                                     start=(k == 0), stop=(k == DK - 1))
            if part[1] == DK:
                m.then_inc(gd, 1)

        def hi_w(n, i, j):
            nj = n + j
            nc.scalar.wait_ge(lds[nj % SLOTS], i * 16 + 16 * (nj // SLOTS + 1))
            nc.scalar.copy(wh[0][nj % 2], ring[nj % SLOTS][:, :, :]).then_inc(w_hi, 1)

        def lo_w(eng, n, i, j):
            nj = n + j
            r = ring[nj % SLOTS][:, :, :]
            eng.wait_ge(w_hi, i * SLOTS + split(nj))
            eng.tensor_tensor(ring_lo[nj % SLOTS][:, :, :], r, wh[0][nj % 2].bitcast(F32), op=ALU.subtract).then_inc(w_lo, 1)

        def split_gemm(n, j, hi, lo, out, chunks, ready=None):
            nj = n + j
            for c, (a, b) in enumerate(chunks):
                if ready is not None:
                    ready(b)
                for m_, (w, x) in enumerate(((wh[0][nj % 2], hi), (wh[0][nj % 2], lo),
                                             (ring_lo[nj % SLOTS][:, :, :], hi))):
                    m = nc.tensor.matmul(out, w[:, a, :], x[:, b, :], start=(c == 0 and m_ == 0),
                                         stop=(c == len(chunks) - 1 and m_ == 2))
            m.then_inc(gd, 1)

        def gemm3(pe, n, i, j, hi, lo, ready=None):
            pe.wait_ge(w_lo, i * SLOTS + split(n + j))
            pe.wait_ge(ge, i * SLOTS + product(n + j))
            split_gemm(n, j, hi, lo, bank(n, j), [(k, k) for k in range(DK)], ready)

        def bank(n, j):
            return PS[:, GB + (product(n + j) - 1) % 2, 0:T]

        def gemm_out(eng, n, i, j):
            eng.wait_ge(gd, i * SLOTS + product(n + j))

        actT = ExitStack()
        xT = sb(actT, "xT", [P, DK, T])
        attnT = sb(actT, "attnT", [P, NH, T])
        mergedT = pqT = xT
        ypoolT = sb(actT, "ypoolT", [P, POOL_CH, T])
        PT = sb(actT, "PT", [P, N1, T])
        gatesP = PT[:, KC0:N1, :]
        woT = PT[:, KC0:N1, :]
        x_r, attn_r, PT_r = [in_place_of(b, [P, n, T])[:, :, :] for b, n in (("xT", DK), ("attnT", DK), ("PT", 2 * DK))]
        xHL = (attn_r, x_r)
        ypHL = (PT_r[:, POOL_CH:DK, :], in_place_of("ypoolT", [P, POOL_CH, T])[:, :, :])
        atHL = (PT_r[:, DK:2 * DK, :], attn_r)
        meHL = (PT_r[:, 0:DK, :], x_r)
        hHL = (PT_r[:, 0:DK, :], attn_r)
        gateT = ypoolT[0:3 * NH, 0, :]
        gateq = ypoolT[0:3 * NH, 1, 0:NS_TOK]
        mid = ExitStack()
        kcb = sb(mid, "kcb", [P, NKV * BS * NCMP])
        kcbp = sb(mid, "kcbp", [P, NKV * NCMP])
        vcb = sb(mid, "vcb", [BS * NCMP, NKV, HD])
        vcbp = sb(mid, "vcbp", [NCMP, NKV, HD])
        pgi = sb(mid, "pgi", [P, 2 * BS], I32)
        cmps = ExitStack()
        CT = sb(cmps, "CT", [P, 2 * BS, NKV * P])
        W1 = sb(cmps, "W1", [P, 32, HD])
        w2 = sb(cmps, "w2", [P, 2, HD])
        peT = sb(cmps, "peT", [P, 2, 32])
        ptab = sb(cmps, "ptab", [P, 2 * BS], I32)
        ptf = sb(cmps, "ptf", [P, 2 * BS])
        pidx = sb(cmps, "pidx", [P, 1])
        c3 = sem("c3")
        w1_ld = sem("w1_ld")
        ix = sem("ix")
        ct_ld = sem("ct_ld")

        def gather_past(g, kv):
            for n in range(2 * BS):
                nc.gpsimd.indirect_dma_start(
                    out=CT[:, n, :], out_offset=None, in_=(kcT_d, vcT_d)[kv],
                    in_offset=bass.IndirectOffsetOnAxis(ap=pgi[:, n:n + 1], axis=0)).then_inc(ct_ld, 16)

        Wn = sb(cmps, "Wn", [P, DK, 3 * NH])
        parts = ExitStack()
        whq = sb(parts, "whq", [P, 2, DK, P], F32R)
        wh[0] = [whq[:, n, :, :] for n in range(2)]
        x_ld = [sem(f"x_ld{q}") for q in range(4)]
        x_hi, x_lo = sem("x_hi"), sem("x_lo")
        x_again = sem("x_again")
        wn_ld = sem("wn_ld")
        g_done = sem("g_done")
        sg_done = sem("sg_done")
        sg_st = sem("sg_st")
        def page_rows(v):
            v.wait_ge(c3, 80)
            nc.vector.tensor_copy(ptf[:, :], ptab[:, :]).then_inc(ix, 1)
            v.wait_ge(ix, 1)
            nc.vector.tensor_scalar(ptf[:, :], ptf[:, :], float(P), pidx[:, 0:1], op0=ALU.mult, op1=ALU.add).then_inc(ix, 1)
            v.wait_ge(ix, 2)
            nc.vector.tensor_copy(pgi[:, :], ptf[:, :]).then_inc(ix, 1)

        with nc.Block() as block:
            @block.sync
            def _(sp):
                for q in range(4):
                    sp.dma_start(xT[:, 4 * q:4 * q + 4, :],
                                 xT_d[q * 512:(q + 1) * 512].rearrange("(k p) t -> p k t", p=P)).then_inc(x_ld[q], 16)
                    load(sp, q, q)
                sp.dma_start(Wn[:, :, :], nsa_d).then_inc(wn_ld, 16)
                sp.dma_start(ptab[:, :], ptab_d.rearrange("(o n) -> o n", o=1).to_broadcast([P, 2 * BS])).then_inc(c3, 16)
                sp.dma_start(pidx[:, :], pidx_d).then_inc(c3, 16)
                sp.dma_start(ident[:, :], ident_d).then_inc(c3, 16)
                sp.dma_start(w2[:, :, :], w2_d).then_inc(c3, 16)
                sp.dma_start(peT[:, :, :], peT_d).then_inc(c3, 16)
                sp.dma_start(W1[:, :, :], w1_d[0]).then_inc(w1_ld, 16)
                next_loads(sp, L_QKV, L_POOL - L_QKV)
                out_dma(sp, ktail_d, kwin_d[:, 4:256])
                out_dma(sp, vtail_d, vwin_d[:, 4:256])
                out_dma(sp, spool_d, state_d[:, 4:15])
                sp.wait_ge(gd, product(L_POOL - 1))
                sp.dma_start(xT[:, :, :], xT_d.rearrange("(k p) t -> p k t", p=P)).then_inc(x_again, 16)
                sp.wait_ge(wn_ld, 16)

            @block.gpsimd
            def _(g):
                g.wait_ge(ix, 3)
                gather_past(g, 0)

            @block.vector
            def _(v):
                for q in range(4):
                    x = xT[:, 4 * q:4 * q + 4, :]
                    v.wait_ge(x_hi, q + 1)
                    nc.vector.tensor_tensor(xHL[1][:, 4 * q:4 * q + 4, :], x, xHL[0][:, 4 * q:4 * q + 4, :].bitcast(F32),
                                            op=ALU.subtract).then_inc(x_lo, 1)
                    if q < 2:
                        lo_w(nc.vector, L_QKV, 0, q)
                page_rows(v)
                with v.Fori(0, (L_POOL - L_QKV) // SLOTS - 1) as i:
                    for j in range(SLOTS):
                        lo_w(nc.vector, L_QKV, i, j + 2)
                for j in range(2):
                    lo_w(nc.vector, L_POOL - SLOTS, 0, j + 2)

            @block.tensor
            def _(pe):
                with pe.Fori(0, (L_POOL - L_QKV) // SLOTS) as i:
                    for j in range(SLOTS):
                        def ready(k):
                            if j == 0 and k % 4 == 0:
                                pe.wait_ge(x_lo, k // 4 + 1)
                        gemm3(pe, L_QKV, i, j, *xHL, ready)

            @block.scalar
            def _(act):
                def out(i, j):
                    gemm_out(act, L_QKV, i, j)
                    nc.scalar.copy(PT[:, bass.ds(i * SLOTS + (Q0 + j), 1), :].rearrange("p a t -> p (a t)"),
                                   bank(L_QKV, j)).then_inc(ge, 1)

                act.sem_inc(ge, 2)
                for q in range(4):
                    act.wait_ge(x_ld[q], 16)
                    nc.scalar.copy(xHL[0][:, 4 * q:4 * q + 4, :], xT[:, 4 * q:4 * q + 4, :]).then_inc(x_hi, 1)
                    if q < 2:
                        hi_w(L_QKV, 0, q)
                with act.Fori(0, (L_POOL - L_QKV) // SLOTS - 1) as i:
                    for j in range(SLOTS):
                        out(i, j)
                        hi_w(L_QKV, i, j + 2)
                for j in range(SLOTS):
                    out((L_POOL - L_QKV) // SLOTS - 1, j)
                    if j < 2:
                        hi_w(L_POOL - SLOTS, 0, j + 2)
        parts.close()

        A1 = sb(cmps, "A1", [P, 512])
        A1p = sb(cmps, "A1p", [P, 64])
        peb = sb(cmps, "peb", [P, 1])
        HS = sb(cmps, "HS", [P, NKV, BS, NCMP])
        HP = sb(cmps, "HP", [P, NKV, NCMP])
        HG = sb(cmps, "HG", [P, NKV * BS * NCMP])
        HGp = sb(cmps, "HGp", [P, NKV * NCMP])
        cm = sem("cm")
        cr = sem("cr")
        ch = sem("ch")
        cg = sem("cg")
        ck = sem("ck")
        ce = sem("ce")
        with nc.Block() as block:
            @block.sync
            def _(sp):
                for n, c0 in ((0, KC0), (1, VC0), (3, VS0), (5, VW0)):
                    sp.dma_start(kvT_d[:, n], PT[:, c0:c0 + NKV, :]).then_inc(raw_out, 16)
                sp.wait_ge(cm, 1)
                sp.dma_start(W1[:, :, :], w1_d[1]).then_inc(w1_ld, 16)
                next_loads(sp, L_POOL, SLOTS)
                sp.wait_ge(sg_done, 1)
                sp.dma_start(gate_d, gateT[:, NP_TOK:T]).then_inc(sg_st, 16)
                sp.wait_ge(sg_done, 2)
                sp.dma_start(gatep_d.rearrange("c x p -> c (x p)"), gateq).then_inc(sg_st, 16)
                sp.wait_ge(sg_st, 32)

            @block.gpsimd
            def _(g):
                g.wait_ge(cm, 1)
                gather_past(g, 1)

            @block.tensor
            def _(pe):
                for kv in range(2):
                    pe.wait_ge(w1_ld, 16 * (kv + 1))
                    pe.wait_ge(ct_ld, 16 * 16 * (kv + 1))
                    if kv:
                        pe.wait_ge(ch, 4)
                        pe.wait_ge(sg_done, 1)
                    cv = CT[:, :, :].rearrange("p b (g c s) -> p (b g) c s", g=NKV, s=16)
                    c0 = (KC0, VC0)[kv]
                    pv = PT[:, c0:c0 + NKV, 0:NP_TOK].rearrange("p g (c s) -> p g c s", s=16)
                    for r in range(2):
                        for s in range(16):
                            w = W1[:, 16 * r + s, :]
                            nc.tensor.matmul(PS[:, r, :], w, cv[:, :, :, s], start=(s == 0), stop=(s == 15))
                            nc.tensor.matmul(PS[:, 2 + r, 0:64], w, pv[:, :, :, s], start=(s == 0), stop=(s == 15))
                            m = nc.tensor.matmul(PS[:, 4, 0:1], w, peT[:, kv, 16 * r + s:16 * r + s + 1],
                                                 start=(r == 0 and s == 0), stop=(r == 1 and s == 15))
                    m.then_inc(cm, 1)
                    if kv == 0:
                        pe.wait_ge(x_again, 16)
                    for j in ((0, 1, 2), (3,))[kv]:
                        gemm(pe, L_POOL, 0, j, xT)
                    if kv == 0:
                        pe.wait_ge(ch, 4)
                        for k in range(DK):
                            m = nc.tensor.matmul(PS[0:3 * NH, 2, 0:T], Wn[:, k, :], xT[:, k, :],
                                                 start=(k == 0), stop=(k == DK - 1))
                        m.then_inc(g_done, 1)
                    pe.wait_ge(cg, 2 * (kv + 1))
                    if kv == 0:
                        nc.tensor.matmul(PS[:, 5, 0:480], w2[:, 0, :], HG[:, :], start=True, stop=True)
                        nc.tensor.matmul(PS[:, 4, 0:60], w2[:, 0, :], HGp[:, :], start=True, stop=True).then_inc(ck, 1)
                        pe.wait_ge(ce, 2)
                    else:
                        for g in range(NKV):
                            nc.tensor.matmul(PS[0:120, 5, g * P:(g + 1) * P], HG[:, g * 120:(g + 1) * 120], w2[:, 1, :],
                                             start=True, stop=True)
                            m = nc.tensor.matmul(PS[0:NCMP, 4, g * P:(g + 1) * P], HGp[:, g * NCMP:(g + 1) * NCMP],
                                                 w2[:, 1, :], start=True, stop=True)
                        m.then_inc(ck, 1)

            @block.scalar
            def _(act):
                for kv in range(2):
                    act.wait_ge(cm, kv + 1)
                    if kv:
                        act.wait_ge(ch, 4)
                    nc.scalar.copy(A1[:, :], PS[:, 1, :]).then_inc(cr, 1)
                    nc.scalar.copy(A1p[:, :], PS[:, 3, 0:64]).then_inc(cr, 1)
                    nc.scalar.copy(peb[:, :], PS[:, 4, 0:1]).then_inc(cr, 1)
                    act.wait_ge(cr, 3 * kv + 3)
                    act.wait_ge(ch, 4 * (kv + 1))
                    if kv:
                        act.wait_ge(ck, 1)
                    nc.scalar.activation(HG[:, :], HS[:, :, :, :].rearrange("p g b n -> p (g b n)"), ACT.Gelu,
                                         bias=peb[:, 0:1]).then_inc(cg, 1)
                    nc.scalar.activation(HGp[:, :], HP[:, :, :].rearrange("p g n -> p (g n)"), ACT.Gelu,
                                         bias=peb[:, 0:1]).then_inc(cg, 1)
                    for j in ((0, 1, 2), (3,))[kv]:
                        gemm_out(act, L_POOL, 0, j)
                        nc.scalar.copy(PT[:, j, :], bank(L_POOL, j)).then_inc(ge, 1)
                    if kv == 0:
                        act.wait_ge(g_done, 1)
                        nc.scalar.activation(gateT, PS[0:3 * NH, 2, 0:T], ACT.Sigmoid).then_inc(sg_done, 1)
                        act.wait_ge(sg_done, 1)
                        nc.scalar.copy(gateq.rearrange("c (x p) -> c x p", p=4),
                                       gateT[:, NP_TOK:T].rearrange("c (p x) -> c x p", p=4)).then_inc(sg_done, 1)
                    act.wait_ge(ck, kv + 1)
                    if kv == 0:
                        nc.scalar.copy(kcb[:, :], PS[:, 5, 0:480]).then_inc(ce, 1)
                        nc.scalar.copy(kcbp[:, :], PS[:, 4, 0:60]).then_inc(ce, 1)
                    else:
                        nc.scalar.copy(vcb[:, :, :], PS[0:120, 5, :].rearrange("p (g d) -> p g d", g=NKV)).then_inc(ce, 1)
                        nc.scalar.copy(vcbp[:, :, :], PS[0:NCMP, 4, :].rearrange("p (g d) -> p g d", g=NKV)).then_inc(ce, 1)

            @block.vector
            def _(v):
                a0 = PS[:, 0, :].rearrange("p (b q g c) -> p q g b c", b=BS, q=2, g=NKV)
                a1 = A1[:, :].rearrange("p (b q g c) -> p q g b c", b=BS, q=2, g=NKV)
                a0p = PS[:, 2, 0:64].rearrange("p (g c) -> p g c", g=NKV)
                a1p = A1p[:, :].rearrange("p (g c) -> p g c", g=NKV)
                for kv in range(2):
                    v.wait_ge(cr, 3 * (kv + 1))
                    if kv:
                        v.wait_ge(cg, 2)
                    nc.vector.tensor_tensor(HS[:, :, :, 0:7], a0[:, 0, :, :, 0:7], a1[:, 0, :, :, 1:8], op=ALU.add).then_inc(ch, 1)
                    nc.vector.tensor_tensor(HS[:, :, :, 7:8], a0[:, 0, :, :, 7:8], a1[:, 1, :, :, 0:1], op=ALU.add).then_inc(ch, 1)
                    nc.vector.tensor_tensor(HS[:, :, :, 8:15], a0[:, 1, :, :, 0:7], a1[:, 1, :, :, 1:8], op=ALU.add).then_inc(ch, 1)
                    nc.vector.tensor_tensor(HP[:, :, :], a0p[:, :, 0:15], a1p[:, :, 1:16], op=ALU.add).then_inc(ch, 1)
        cmps.close()

        VR = sb(mid, "VR", [P, 3, 2, NKV * HD])
        PcT = sb(mid, "PcT", [P, NH, NP_TOK])[0:NCMP, :, :]
        PcS = sb(mid, "PcS", [BS * NCMP, NKV, P])
        grow = sb(mid, "grow", [P, TT, 3 * NH])
        gs = sb(mid, "gs", [P, 3, 4])
        scope = ExitStack()
        maskc = sb(scope, "maskc", [P, 2, 480])
        keepc = sb(scope, "keepc", [P, 2, 480])
        E = sb(scope, "E", [P, 2, 480])
        mx = sb(scope, "mx", [P, 2, 32])
        gc = sb(scope, "gc", [P, NKV])
        qS = sb(scope, "qS", [P, NH, NS_TOK])
        rot = sb(scope, "rot", [P, P])
        cs = sb(scope, "cs", [P, 2, T])
        rt = sb(scope, "rt", [P, 4, T])
        rt2 = sb(scope, "rt2", [P, 4, T])
        c2 = sem("c2")
        rq = sem("rq")
        rd = sem("rd")
        vt = sem("vt")
        vc = sem("vc")
        c4 = sem("c4")
        c4g = sem("c4g")
        gt = sem("gt")
        s4 = sem("s4")
        d4 = sem("d4")
        e4 = sem("e4")
        t4 = sem("t4")
        k4 = sem("k4")
        k5 = sem("k5")
        QUADS = (KS0, KW0, Q0, Q0 + 4, Q0 + 8, Q0 + 12)
        with nc.Block() as block:
            @block.sync
            def _(sp):
                sp.dma_start(maskc[:, :, :], maskc_d).then_inc(c4, 16)
                sp.dma_start(keepc[:, :, :], keepc_d).then_inc(c4, 16)
                sp.dma_start(rot[:, :], rot_d).then_inc(c2, 16)
                sp.dma_start(cs[:, :, :], cs_d).then_inc(c2, 16)
                sp.dma_start(gc[:, :], gate_d[0:NH].rearrange("(g j) t -> (j t) g", g=NKV),
                             allow_slow_non_contiguous=True).then_inc(c4g, 16)
                sp.dma_start(gs[:, :, :], gatep_d.rearrange("(r h) x p -> (h x) r p", r=3)).then_inc(c4g, 16)
                next_loads(sp, L_POOL + SLOTS, SLOTS)
                sp.wait_ge(rd, 2 * 3)
                for n, c0 in ((2, KS0), (4, KW0)):
                    out_dma(sp, kvT_d[:, n], PT[:, c0:c0 + NKV, :])
                sp.wait_ge(c4g, 32)

            @block.tensor
            def _(pe):
                for t in range(TT):
                    m = nc.tensor.transpose(PS[:, 2, t * 48:t * 48 + 48], gateT[:, t * P:(t + 1) * P], ident[0:48, 0:48])
                m.then_inc(gt, 1)
                for h in range(NH):
                    for t in range(TT):
                        m = nc.tensor.matmul(PS[:, 0, (2 * h + t) * NCMP:(2 * h + t + 1) * NCMP],
                                             PT[:, Q0 + h, t * P:(t + 1) * P],
                                             kcbp[:, (h // HPG) * NCMP:(h // HPG + 1) * NCMP], start=True, stop=True)
                m.then_inc(s4, 1)
                pe.wait_ge(d4, 1)
                for g in range(NKV):
                    m = nc.tensor.matmul(PS[:, 1, g * 120:(g + 1) * 120],
                                         qS[:, 4 * g:4 * g + 4, :].rearrange("p h t -> p (h t)"),
                                         kcb[:, g * 120:(g + 1) * 120], start=True, stop=True)
                m.then_inc(s4, 1)

                def swap(n):
                    if n > 0:
                        pe.wait_ge(rd, 3 * n)
                    for j in range(4):
                        m = nc.tensor.matmul(PS[:, 2 + j, 0:T], rot[:, :], PT[:, QUADS[n] + j, :], start=True, stop=True)
                    m.then_inc(rq, 1)

                gemm(pe, L_POOL + SLOTS, 0, 0, xT)
                pe.wait_ge(d4, 10)
                for n in range(8):
                    if n >= 2:
                        pe.wait_ge(k4, n - 1)
                    for j in range(4):
                        h, t = 2 * n + j // 2, j % 2
                        m = nc.tensor.transpose(PS[0:NCMP, 4 + n % 2, j * P:(j + 1) * P],
                                                E[:, 0, (2 * h + t) * NCMP:(2 * h + t + 1) * NCMP], ident[:, :])
                    m.then_inc(t4, 1)
                pe.wait_ge(d4, 11)
                for n in range(6):
                    t, v = n // 2, n % 2
                    w = P if t < TT else NS_TOK
                    c0 = (VS0, VW0)[v]
                    if n >= 2:
                        pe.wait_ge(vc, n - 1)
                    for j in range(NKV):
                        m = nc.tensor.transpose(PS[0:w, n % 2, j * P:(j + 1) * P],
                                                PT[:, c0 + j, t * P:t * P + w], ident[:, :])
                    m.then_inc(vt, 1)
                pe.wait_ge(d4, 19)
                pe.wait_ge(vc, 6)
                for g in range(NKV):
                    m = nc.tensor.transpose(PS[0:120, 0, g * P:(g + 1) * P], E[:, 1, g * 120:(g + 1) * 120], ident[:, :])
                m.then_inc(t4, 1)
                pe.wait_ge(c2, 32)
                pe.wait_ge(k4, 8)
                for n in range(6):
                    swap(n)
                    if n < 3:
                        gemm(pe, L_POOL + SLOTS, 0, n + 1, xT)

            @block.scalar
            def _(act):
                act.wait_ge(gt, 1)
                nc.scalar.copy(grow[:, :, :], PS[:, 2, 0:96].rearrange("p (t c) -> p t c", t=TT)).then_inc(e4, 1)
                for u in range(2):
                    act.wait_ge(d4, 1 + 9 * u + 3)
                    nc.scalar.activation(E[:, u, :], E[:, u, :], ACT.Exp).then_inc(e4, 1)
                    if u == 0:
                        gemm_out(act, L_POOL + SLOTS, 0, 0)
                        nc.scalar.copy(PT[:, SLOTS, :], bank(L_POOL + SLOTS, 0)).then_inc(ge, 1)
                for n in range(8):
                    act.wait_ge(t4, n + 1)
                    nc.scalar.copy(PcT[:, 2 * n:2 * n + 2, :], PS[0:NCMP, 4 + n % 2, :].rearrange(
                        "p (h t) -> p h t", h=2)).then_inc(k4, 1)
                for n in range(6):
                    t, v = n // 2, n % 2
                    w = P if t < TT else NS_TOK
                    act.wait_ge(vt, n + 1)
                    nc.scalar.copy(VR[0:w, t, v, :], PS[0:w, n % 2, :]).then_inc(vc, 1)
                act.wait_ge(t4, 9)
                nc.scalar.copy(PcS[:, :, :], PS[0:120, 0, :].rearrange("p (g t) -> p g t", g=NKV)).then_inc(k4, 1)
                for j in range(1, SLOTS):
                    gemm_out(act, L_POOL + SLOTS, 0, j)
                    nc.scalar.copy(PT[:, SLOTS + j, :], bank(L_POOL + SLOTS, j)).then_inc(ge, 1)

            @block.vector
            def _(v):
                n = [0]

                def link(ins):
                    n[0] += 1
                    ins.then_inc(d4, 1)
                    v.wait_ge(d4, n[0])

                link(nc.vector.tensor_copy(qS[:, :, :], PT[:, Q0:Q0 + NH, NP_TOK:T]))
                v.wait_ge(c4, 32)
                for u in range(2):
                    A, B = (32, NCMP) if u == 0 else (4, 120)
                    e = E[:, u, :].rearrange("p (a b) -> p a b", a=A)
                    m = mx[:, 0, 0:A]
                    r = mx[:, 1, 0:A]
                    v.wait_ge(s4, u + 1)
                    link(nc.vector.scalar_tensor_tensor(out=E[:, u, :], in0=PS[:, u, 0:480], scalar=SCALE, in1=maskc[:, u, :],
                                                        op0=ALU.mult, op1=ALU.add))
                    link(nc.vector.tensor_reduce(m, e, AX, ALU.max))
                    link(nc.vector.tensor_tensor(e, e, m.unsqueeze(2).to_broadcast([P, A, B]), op=ALU.subtract))
                    v.wait_ge(e4, 2 + u)
                    link(nc.vector.tensor_tensor(E[:, u, :], E[:, u, :], keepc[:, u, :], op=ALU.mult))
                    link(nc.vector.tensor_reduce(r, e, AX, ALU.add))
                    link(nc.vector.tensor_scalar(r, r, 0.5, None, op0=ALU.max))
                    link(nc.vector.reciprocal(r, r))
                    if u == 0:
                        for t in range(TT):
                            ins = nc.vector.tensor_tensor(r.rearrange("p (h t) -> p h t", t=TT)[:, :, t],
                                                          r.rearrange("p (h t) -> p h t", t=TT)[:, :, t],
                                                          grow[:, t, 0:NH], op=ALU.mult)
                            if t == 0:
                                ins.then_inc(k5, 1)
                        link(ins)
                        v.wait_ge(k5, 1)
                    else:
                        v.wait_ge(c4g, 32)
                        link(nc.vector.tensor_tensor(r, r, gc[:, :], op=ALU.mult))
                    link(nc.vector.tensor_tensor(e, e, r.unsqueeze(2).to_broadcast([P, A, B]), op=ALU.mult))
                cos = cs[:, 0:1, :].to_broadcast([P, 4, T])
                sin = cs[:, 1:2, :].to_broadcast([P, 4, T])
                v.wait_ge(c2, 32)
                for n in range(6):
                    x = PT[:, QUADS[n]:QUADS[n] + 4, :]
                    v.wait_ge(rq, n + 1)
                    nc.vector.tensor_tensor(rt[:, :, :], PS[:, 2:6, 0:T], sin, op=ALU.mult).then_inc(rd, 1)
                    nc.vector.tensor_tensor(rt2[:, :, :], x, cos, op=ALU.mult).then_inc(rd, 1)
                    v.wait_ge(rd, 3 * n + 2)
                    nc.vector.tensor_tensor(x, rt[:, :, :], rt2[:, :, :], op=ALU.add).then_inc(rd, 1)
        scope.close()

        NKS = NP_TOK + NS_TOK
        scope = ExitStack()
        KT = [sb(scope, f"KT{i}", [P, 2, 2, NKV * P]) for i in range(2)]
        V = [sb(scope, f"V{i}", [P, 2, 2, NKV * HD]) for i in range(2)]
        maskn = sb(scope, "maskn", [P, BS, NS_TOK])
        qcur = sb(scope, "qcur", [P, NH, 8])
        stg = sb(scope, "stg", [P, 4], I32)
        Pr = [sb(scope, f"Pr{i}", [P, NKS]) for i in range(2)]
        PTr = [sb(scope, f"PTr{i}", [P, 3, P]) for i in range(2)]
        st5 = sb(scope, "st5", [P, 2, 4])
        c5 = sem("c5")
        kv_ld = [sem(f"kv_ld{i}") for i in range(2)]
        kw_ld = [sem(f"kw_ld{i}") for i in range(2)]
        kv_fr = [sem(f"kv_fr{i}") for i in range(2)]
        stg_ok = sem("stg_ok")
        kv_own = sem("kv_own")
        q_ok = sem("q_ok")
        q_fr = sem("q_fr")
        s5 = sem("s5")
        a5 = sem("a5")
        e5 = sem("e5")
        b5 = sem("b5")
        t5 = sem("t5")
        k5b = sem("k5b")
        v5 = sem("v5")
        o5 = sem("o5")
        d5 = sem("d5")
        d5a = sem("d5a")
        cmp_o = sem("cmp_o")
        cmp_c = sem("cmp_c")

        def done(i, per, u):
            return i * per + (u + 3)

        def free(i, per, u):
            return i * per + (u + 1)

        with nc.Block() as block:
            @block.sync
            def _(sp):
                sp.dma_start(maskn[:, :, :], maskn_d).then_inc(c5, 16)
                sp.dma_start(poolT_d, PT[:, 0:POOL_CH, NP_TOK - POOL_ST:T]).then_inc(pool_out, 16)
                with sp.Fori(0, BS // 2) as i:
                    for b in range(2):
                        sp.wait_ge(kv_fr[b], i + 1)
                        sp.dma_start(KT[b][:, 1, :, :].rearrange("p a n -> p (a n)"),
                                     kwT_d[bass.ds(2 * i + b, 1)].rearrange("o p n -> p (o n)")).then_inc(kw_ld[b], 16)
                        sp.dma_start(V[b][:, 1, :, :].rearrange("p a n -> p (a n)"),
                                     vw_d[bass.ds(2 * i + b, 1)].rearrange("o p n -> p (o n)")).then_inc(kw_ld[b], 16)
                    for s in range(SLOTS):
                        sp.wait_ge(gd, i * SLOTS + product(L_GP + s))
                        load(sp, i * SLOTS + (L_GP + SLOTS + s), s)

            @block.gpsimd
            def _(g):
                with g.Fori(0, BS // 2) as i:
                    g.wait_ge(kv_fr[0], i + 1)
                    g.sem_inc(kv_own, 1)
                    nc.gpsimd.tensor_copy(stg[:, :], pgi[:, bass.ds(i * 4, 4)]).then_inc(stg_ok, 1)
                    g.wait_ge(stg_ok, 1)
                    g.sem_clear(stg_ok)
                    for b in range(2):
                        if b:
                            g.wait_ge(kv_fr[1], i + 1)
                            g.sem_inc(kv_own, 1)
                        for pg in range(2):
                            for dst, src in ((KT[b], ksT_d), (V[b], vs_d)):
                                nc.gpsimd.indirect_dma_start(
                                    out=dst[:, 0, pg, :], out_offset=None, in_=src,
                                    in_offset=bass.IndirectOffsetOnAxis(ap=stg[:, 2 * b + pg:2 * b + pg + 1], axis=0)
                                ).then_inc(kv_ld[b], 16)

            @block.tensor
            def _(pe):
                for g in range(NKV):
                    m = nc.tensor.matmul(PS[:, 4, g * P:(g + 1) * P], vcb[:, g, :], PcS[:, g, :], start=True, stop=True)
                m.then_inc(cmp_o, 1)
                pe.sem_inc(kv_fr[0], 1)
                pe.sem_inc(kv_fr[1], 1)
                pe.sem_inc(q_fr, 1)
                for x in (s5, t5, v5):
                    pe.sem_inc(x, 2)
                pe.wait_ge(cmp_c, 1)
                with pe.Fori(0, BS // 2) as i:
                    for step in range(6):
                        if step < 4:
                            u = step
                            b, br = u // 2, u % 2
                            if u == 0:
                                pe.wait_ge(q_ok, i + 1)
                            if br == 0:
                                pe.wait_ge(kv_ld[b], i * 64 + 64)
                                pe.wait_ge(kw_ld[b], i * 32 + 32)
                            pe.wait_ge(a5, free(i, 4, u))
                            for g in range(NKV):
                                nc.tensor.matmul(PS[32 * g:32 * g + 32, u % 2, 0:NP_TOK],
                                                 qcur[:, 4 * g:4 * g + 4, :].rearrange("p h x -> p (h x)"),
                                                 KT[b][:, br, :, g * P:(g + 1) * P], start=True, stop=True,
                                                 tile_position=(0, 32 * g))
                                m = nc.tensor.matmul(PS[32 * g:32 * g + 32, u % 2, NP_TOK:NKS],
                                                     qcur[:, 4 * g:4 * g + 4, :].rearrange("p h x -> p (h x)"),
                                                     PT[:, (KS0, KW0)[br] + g, NP_TOK:T], start=True, stop=True,
                                                     tile_position=(0, 32 * g))
                            m.then_inc(s5, 1)
                            gemm(pe, L_GP, i, u, xT)
                        if 1 <= step <= 4:
                            u = step - 1
                            pe.wait_ge(b5, done(i, 4, u))
                            pe.wait_ge(k5b, free(i, 4, u))
                            for kb in range(3):
                                w = P if kb < 2 else NS_TOK
                                m = nc.tensor.transpose(PS[0:w, 2 + u % 2, kb * P:(kb + 1) * P],
                                                        Pr[u % 2][:, kb * P:kb * P + w], ident[:, :])
                            m.then_inc(t5, 1)
                        if step >= 2:
                            u = step - 2
                            b, br = u // 2, u % 2
                            pe.wait_ge(k5b, done(i, 4, u))
                            if br == 0:
                                pe.wait_ge(o5, i * 2 + b + 1)
                            for g in range(NKV):
                                for kb in range(3):
                                    w = P if kb < 2 else NS_TOK
                                    lhs = V[b][:, br, kb, g * P:(g + 1) * P] if kb < 2 else VR[0:w, 2, br, g * P:(g + 1) * P]
                                    rhs = PTr[u % 2][0:w, kb, :].rearrange("k (h x) -> k h x", x=8)[
                                        :, 4 * g:4 * g + 4, 4 * b:4 * b + 4]
                                    m = nc.tensor.matmul(PS[:, 4 + b, g * 16:(g + 1) * 16], lhs, rhs,
                                                         start=(br == 0 and kb == 0 and g == 0),
                                                         stop=(br == 1 and kb == 2), skip_group_check=True)
                            m.then_inc(v5, 1)
                            if br == 1:
                                pe.wait_ge(v5, done(i, 4, u))
                                pe.sem_inc(kv_fr[b], 1)
                                if b:
                                    pe.sem_inc(q_fr, 1)

            @block.scalar
            def _(act):
                act.wait_ge(cmp_o, 1)
                nc.scalar.copy(attnT[:, :, NP_TOK:T], PS[:, 4, :].rearrange("p (h t) -> p h t", h=NH)).then_inc(cmp_c, 1)
                for x in (e5, k5b):
                    act.sem_inc(x, 2)
                act.wait_ge(raw_out, 64)
                with act.Fori(0, BS // 2) as i:
                    for step in range(5):
                        if step < 4:
                            u = step
                            act.wait_ge(a5, done(i, 4, u))
                            nc.scalar.activation(Pr[u % 2][:, :], Pr[u % 2][:, :], ACT.Exp, bias=st5[:, u % 2, 0:1],
                                                 accum_out=st5[:, u % 2, 1:2]).then_inc(e5, 1)
                        if step >= 1:
                            u = step - 1
                            act.wait_ge(t5, done(i, 4, u))
                            act.wait_ge(v5, free(i, 4, u))
                            nc.scalar.copy(PTr[u % 2][:, 0:2, :], PS[:, 2 + u % 2, 0:256].rearrange(
                                "p (k r) -> p k r", k=2)).then_inc(d5a, 1)
                            nc.scalar.copy(PTr[u % 2][0:NS_TOK, 2, :], PS[0:NS_TOK, 2 + u % 2, 256:384]).then_inc(d5a, 1)
                            act.wait_ge(d5a, 2 * step)
                            act.sem_inc(k5b, 1)
                        if step < 4:
                            gemm_out(act, L_GP, i, step)
                            nc.scalar.copy(gatesP[:, bass.ds(i * SLOTS + step, 1), :].rearrange("p a t -> p (a t)"),
                                           bank(L_GP, step)).then_inc(ge, 1)
                    act.sem_clear(d5a)

            @block.vector
            def _(v):
                for x in (a5, b5, o5):
                    v.sem_inc(x, 2)
                v.wait_ge(c5, 16)
                v.wait_ge(cmp_c, 1)
                with v.Fori(0, BS // 2) as i:
                    n = [0]

                    def link(ins):
                        n[0] += 1
                        ins.then_inc(d5, 1)
                        v.wait_ge(d5, n[0])

                    v.wait_ge(q_fr, i + 1)
                    nc.vector.tensor_copy(qcur[:, :, :], PT[:, Q0:Q0 + NH, bass.ds(i * 8 + NP_TOK, 8)]).then_inc(q_ok, 1)
                    for step in range(5):
                        if step < 4:
                            u = step
                            b = u // 2
                            v.wait_ge(s5, done(i, 4, u))
                            v.wait_ge(t5, free(i, 4, u))
                            link(nc.vector.tensor_scalar(Pr[u % 2][:, 0:NP_TOK], PS[:, u % 2, 0:NP_TOK], SCALE, None,
                                                         op0=ALU.mult))
                            link(nc.vector.scalar_tensor_tensor(
                                out=Pr[u % 2][:, NP_TOK:NKS], in0=PS[:, u % 2, NP_TOK:NKS], scalar=SCALE,
                                in1=maskn[:, bass.ds(i * 2 + b, 1), :].rearrange("p o k -> p (o k)"),
                                op0=ALU.mult, op1=ALU.add))
                            link(nc.vector.tensor_reduce(st5[:, u % 2, 0:1], Pr[u % 2][:, :], AX, ALU.max))
                            link(nc.vector.tensor_scalar(st5[:, u % 2, 0:1], st5[:, u % 2, 0:1], -1.0, None, op0=ALU.mult))
                            v.sem_inc(a5, 1)
                        if step >= 1:
                            u = step - 1
                            br = u % 2
                            v.wait_ge(e5, done(i, 4, u))
                            link(nc.vector.reciprocal(st5[:, u % 2, 2:3], st5[:, u % 2, 1:2]))
                            link(nc.vector.tensor_tensor(st5[:, u % 2, 3:4], st5[:, u % 2, 2:3],
                                                         gs[:, 1 + br, bass.ds(i, 1)], op=ALU.mult))
                            link(nc.vector.tensor_scalar(Pr[u % 2][:, :], Pr[u % 2][:, :], st5[:, u % 2, 3:4], None,
                                                         op0=ALU.mult))
                            v.sem_inc(b5, 1)
                    for b in range(2):
                        v.wait_ge(v5, done(i, 4, 2 * b + 1))
                        dst = attnT[:, :, bass.ds(i * 8 + (NP_TOK + 4 * b), 4)]
                        link(nc.vector.tensor_tensor(dst, dst, PS[:, 4 + b, 0:64].rearrange("p (h l) -> p h l", l=4),
                                                     op=ALU.add))
                        v.sem_inc(o5, 1)
                    v.sem_clear(d5)
        scope.close()

        NKP = 384
        gas = ExitStack()
        gatesA = sb(gas, "gatesA", [P, DK, T])
        scope = ExitStack()
        past = sb(scope, "past", [P, POOL_CH, BS * POOL_ST])
        EP = [sb(scope, f"EP{i}", [P, POOL_ST + NP_TOK]) for i in range(2)]
        ES = [sb(scope, f"ES{i}", [P, BS, POOL_ST + LS]) for i in range(2)]
        rcnt = sb(scope, "rcnt", [P, 4, 16])
        pst = sem("pst")
        pl = sem("pl")
        QR = sb(scope, "QR", [P, HPG, NP_TOK])
        VG = sb(scope, "VG", [P, TT, 2, HD])
        VCG = sb(scope, "VCG", [NCMP, HD])
        maskp = sb(scope, "maskp", [P, NKP])
        Pp = [sb(scope, f"Pp{i}", [P, NKP]) for i in range(2)]
        PTp = [sb(scope, f"PTp{i}", [P, NKP]) for i in range(2)]
        st6 = sb(scope, "st6", [P, 2, 4, TT])
        c6 = sem("c6")
        stg6 = sem("stg6")
        s6, a6, e6, b6, t6, k6, v6, o6 = [sem(f"{x}6_") for x in "saebtkvo"]
        d6, d6a = sem("d6"), sem("d6a")
        SEG = ((0, P), (P, NKP))
        with nc.Block() as block:
            @block.sync
            def _(sp):
                sp.dma_start(maskp[:, :], maskp_d).then_inc(c6, 16)
                sp.dma_start(past[:, :, :], stateT_d.rearrange("(c p) n -> p c n", p=P)).then_inc(pst, 16)
                sp.dma_start(rcnt[:, :, :], rcnt_d).then_inc(pst, 16)
                next_loads(sp, L_GA, L_BP - L_GA)

            @block.gpsimd
            def _(g):
                n = [0]

                def link(ins):
                    n[0] += 1
                    ins.then_inc(pl, 1)
                    g.wait_ge(pl, n[0])

                def mean_minus_input(c):
                    w = 2 ** (c // 2 + 1)
                    (a, b), (sa, sbf) = EP, ES
                    ud = PT[:, c, NP_TOK:T].rearrange("p (b l) -> p b l", l=LS)
                    link(nc.gpsimd.memset(a[:, 0:POOL_ST], 0.0))
                    link(nc.gpsimd.tensor_copy(a[:, POOL_ST:], PT[:, c, 0:NP_TOK]))
                    link(nc.gpsimd.tensor_copy(sa[:, :, 0:POOL_ST], past[:, c, :].rearrange("p (b s) -> p b s", s=POOL_ST)))
                    link(nc.gpsimd.tensor_copy(sa[:, :, POOL_ST:], ud))
                    LP, LSx = POOL_ST + NP_TOK, POOL_ST + LS
                    sh = 1
                    while sh < w:
                        lo = 2 * sh - 1
                        link(nc.gpsimd.tensor_tensor(b[:, lo:LP], a[:, lo:LP], a[:, lo - sh:LP - sh], op=ALU.add))
                        link(nc.gpsimd.tensor_tensor(sbf[:, :, lo:LSx], sa[:, :, lo:LSx], sa[:, :, lo - sh:LSx - sh],
                                                     op=ALU.add))
                        a, b, sa, sbf = b, a, sbf, sa
                        sh *= 2
                    link(nc.gpsimd.tensor_tensor(a[:, POOL_ST:POOL_ST + 16], a[:, POOL_ST:POOL_ST + 16],
                                                 rcnt[:, c // 2, :], op=ALU.mult))
                    link(nc.gpsimd.tensor_scalar(b[:, POOL_ST:], a[:, POOL_ST:], 1.0 / w, None, op0=ALU.mult))
                    link(nc.gpsimd.tensor_tensor(PT[:, c, 0:NP_TOK], b[:, POOL_ST:], PT[:, c, 0:NP_TOK], op=ALU.subtract))
                    link(nc.gpsimd.tensor_scalar(sbf[:, :, POOL_ST:], sa[:, :, POOL_ST:], 1.0 / w, None, op0=ALU.mult))
                    link(nc.gpsimd.tensor_tensor(ud, sbf[:, :, POOL_ST:], ud, op=ALU.subtract))

                for g0 in range(NKV):
                    if g0:
                        g.wait_ge(v6, g0 * 8 + 2)
                    nc.gpsimd.tensor_copy(QR[:, :, :], PT[:, Q0 + g0 * HPG:Q0 + (g0 + 1) * HPG, 0:NP_TOK]).then_inc(stg6, 1)
                    for t in range(TT):
                        nc.gpsimd.tensor_copy(VG[:, t, :, :], VR[:, t, :, g0 * HD:(g0 + 1) * HD]).then_inc(stg6, 1)
                    nc.gpsimd.tensor_copy(VCG[:, :], vcbp[:, g0, :]).then_inc(stg6, 1)
                    if g0 == 0:
                        g.wait_ge(pst, 32)
                        g.wait_ge(pool_out, 16)
                    for c in (2 * g0, 2 * g0 + 1):
                        mean_minus_input(c)

            @block.tensor
            def _(pe):
                for x in (s6, t6, v6):
                    pe.sem_inc(x, 2)
                with pe.Fori(0, NKV) as i:
                    pe.wait_ge(stg6, i * 4 + 4)
                    for step in range(10):
                        if step < 8:
                            u = step
                            j, br = u // 2, u % 2
                            key = PT[:, bass.ds(i + (KS0, KW0)[br], 1), :].rearrange("p o t -> p (o t)")
                            pe.wait_ge(a6, free(i, 8, u))
                            nc.tensor.matmul(PS[:, u % 2, 0:P], QR[:, j, 0:P], key[:, 0:P], start=True, stop=True)
                            nc.tensor.matmul(PS[:, u % 2, P:NKP], QR[:, j, P:NP_TOK], key[:, 0:NP_TOK],
                                             start=True, stop=True).then_inc(s6, 1)
                            gemm(pe, L_GA, i, u // 2, xT, (u % 2 * (DK // 2), (u % 2 + 1) * (DK // 2)))
                        if 1 <= step <= 8:
                            u = step - 1
                            pe.wait_ge(b6, done(i, 8, u))
                            pe.wait_ge(k6, free(i, 8, u))
                            for kb in range(3):
                                m = nc.tensor.transpose(PS[:, 2 + u % 2, kb * P:(kb + 1) * P],
                                                        Pp[u % 2][:, kb * P:(kb + 1) * P], ident[:, :])
                            m.then_inc(t6, 1)
                        if step >= 2:
                            u = step - 2
                            j, br = u // 2, u % 2
                            o = PS[:, 4 + j % 2, 0:NP_TOK]
                            pe.wait_ge(k6, done(i, 8, u))
                            if br == 0:
                                pe.wait_ge(o6, free(i, 4, j))
                                nc.tensor.matmul(o, VCG[:, :],
                                                 PcT[:, bass.ds(i * HPG + j, 1), :].rearrange("p o t -> p (o t)"),
                                                 start=True, stop=False, skip_group_check=True)
                            nc.tensor.matmul(o, VG[:, 0, br, :], PTp[u % 2][:, 0:NP_TOK], start=False, stop=False,
                                             skip_group_check=True)
                            nc.tensor.matmul(o[:, P:NP_TOK], VG[:, 1, br, :], PTp[u % 2][:, NP_TOK:NKP],
                                             start=False, stop=(br == 1), skip_group_check=True).then_inc(v6, 1)

            @block.scalar
            def _(act):
                for x in (e6, k6):
                    act.sem_inc(x, 2)
                with act.Fori(0, NKV) as i:
                    for step in range(9):
                        if step < 8:
                            u = step
                            act.wait_ge(a6, done(i, 8, u))
                            for t, (a, b) in enumerate(SEG):
                                m = nc.scalar.activation(Pp[u % 2][:, a:b], Pp[u % 2][:, a:b], ACT.Exp,
                                                         bias=st6[:, u % 2, 0, t:t + 1], accum_out=st6[:, u % 2, 1, t:t + 1])
                                m.then_inc(d6a, 1)
                            act.wait_ge(d6a, 2 * u + 2)
                            act.sem_inc(e6, 1)
                        if step >= 1:
                            u = step - 1
                            act.wait_ge(t6, done(i, 8, u))
                            act.wait_ge(v6, free(i, 8, u))
                            nc.scalar.copy(PTp[u % 2][:, :], PS[:, 2 + u % 2, 0:NKP]).then_inc(k6, 1)
                        if step < 8 and step % 2:
                            gemm_out(act, L_GA, i, step // 2)
                            nc.scalar.copy(gatesA[:, bass.ds(i * SLOTS + step // 2, 1), :].rearrange("p a t -> p (a t)"),
                                           bank(L_GA, step // 2)).then_inc(ge, 1)
                    act.sem_clear(d6a)

            @block.vector
            def _(v):
                for x in (a6, b6, o6):
                    v.sem_inc(x, 2)
                v.wait_ge(c6, 16)
                with v.Fori(0, NKV) as i:
                    n = [0]

                    def link(ins):
                        n[0] += 1
                        ins.then_inc(d6, 1)
                        v.wait_ge(d6, n[0])

                    for step in range(10):
                        if step < 8:
                            u = step
                            v.wait_ge(s6, done(i, 8, u))
                            v.wait_ge(t6, free(i, 8, u))
                            link(nc.vector.scalar_tensor_tensor(out=Pp[u % 2][:, :], in0=PS[:, u % 2, 0:NKP], scalar=SCALE,
                                                                in1=maskp[:, :], op0=ALU.mult, op1=ALU.add))
                            for t, (a, b) in enumerate(SEG):
                                link(nc.vector.tensor_reduce(st6[:, u % 2, 0, t:t + 1], Pp[u % 2][:, a:b], AX, ALU.max))
                            link(nc.vector.tensor_scalar(st6[:, u % 2, 0, :], st6[:, u % 2, 0, :], -1.0, None, op0=ALU.mult))
                            v.sem_inc(a6, 1)
                        if 1 <= step <= 8:
                            u = step - 1
                            j, br = u // 2, u % 2
                            v.wait_ge(e6, done(i, 8, u))
                            link(nc.vector.reciprocal(st6[:, u % 2, 2, :], st6[:, u % 2, 1, :]))
                            link(nc.vector.tensor_tensor(st6[:, u % 2, 3, :], st6[:, u % 2, 2, :],
                                                         grow[:, :, bass.ds(i * HPG + ((1 + br) * NH + j), 1)].rearrange(
                                                             "p t o -> p (t o)"), op=ALU.mult))
                            for t, (a, b) in enumerate(SEG):
                                link(nc.vector.tensor_scalar(Pp[u % 2][:, a:b], Pp[u % 2][:, a:b],
                                                             st6[:, u % 2, 3, t:t + 1], None, op0=ALU.mult))
                            v.sem_inc(b6, 1)
                        if step >= 3 and step % 2:
                            j = (step - 3) // 2
                            v.wait_ge(v6, done(i, 8, 2 * j + 1))
                            link(nc.vector.tensor_copy(attnT[:, bass.ds(i * HPG + j, 1), 0:NP_TOK].rearrange(
                                "p o t -> p (o t)"), PS[:, 4 + j % 2, 0:NP_TOK]))
                            v.sem_inc(o6, 1)
                    v.sem_clear(d6)
        scope.close()

        scope = ExitStack()
        grpw = sb(scope, "grpw", [P, 4, 2, 256])
        pscale = sb(scope, "pscale", [P, POOL_CH])
        tmp = sb(scope, "tmp", [P, 2, T])
        PcT_r = in_place_of("PcT", [P, 2, DK, P])
        wh[0] = [PcT_r[:, n, :, :] for n in range(2)]
        c7 = sem("c7")
        ym = sem("ym")
        y_hi, y_lo = sem("y_hi"), sem("y_lo")
        sgp, sga = sem("sgp"), sem("sga")
        a_hi, a_lo = sem("a_hi"), sem("a_lo")
        mg = sem("mg")
        m_hi, m_lo = sem("m_hi"), sem("m_lo")
        d7 = sem("d7")
        N_BP, N_BA, N_WO = L_BA - L_BP, L_WO - L_BA, L_WQ - L_WO

        def chunk(x, c, n=1):
            return x[:, bass.ds(c, n), :].rearrange("p a t -> p (a t)")

        with nc.Block() as block:
            @block.sync
            def _(sp):
                sp.dma_start(grpw[:, :, :, :], grp_d.rearrange("g (k p) e -> p g k e", p=P)).then_inc(c7, 16)
                sp.dma_start(pscale[:, :], pscale_d).then_inc(c7, 16)
                next_loads(sp, L_BP, N_BP, per=2)
                next_loads(sp, L_BA, N_BA)
                next_loads(sp, L_WO, N_WO)

            @block.tensor
            def _(pe):
                pe.wait_ge(c7, 32)
                for c in range(POOL_CH):
                    g, e = c // 2, c % 2
                    if c >= 2:
                        pe.wait_ge(y_lo, c - 1)
                    for k in range(2):
                        m = nc.tensor.matmul(PS[:, c % 2, 0:T], grpw[:, g, k, e * P:(e + 1) * P],
                                             PT[:, 2 * g + k, :], start=(k == 0), stop=(k == 1))
                    m.then_inc(ym, 1)
                pe.wait_ge(y_lo, POOL_CH)
                first = product(L_BP - 1)
                with pe.Fori(0, N_BP // SLOTS) as i:
                    for j in range(SLOTS):
                        pe.wait_ge(w_lo, i * SLOTS + split(L_BP + j))
                        for h in range(2):
                            pe.wait_ge(ge, i * (2 * SLOTS) + (first + 2 * j + h + 1))
                            split_gemm(L_BP, j, *ypHL, PS[:, GB + h, 0:T],
                                       [(h * POOL_CH + k, k) for k in range(POOL_CH)])
                pe.wait_ge(a_lo, N_BP)
                with pe.Fori(0, N_BA // SLOTS) as i:
                    for j in range(SLOTS):
                        gemm3(pe, L_BA, i, j, *atHL)
                with pe.Fori(0, N_WO // SLOTS) as i:
                    for j in range(SLOTS):
                        def ready(k):
                            if j == 0 and k in (0, DK - 1):
                                pe.wait_ge(m_lo, DK - 1 if k == 0 else DK)
                        gemm3(pe, L_WO, i, j, *meHL, ready)

            @block.scalar
            def _(act):
                hi_w(L_BP, 0, 0)
                act.wait_ge(c7, 32)
                for c in range(POOL_CH):
                    act.wait_ge(ym, c + 1)
                    nc.scalar.activation(ypHL[0][:, c, :], PS[:, c % 2, 0:T], ACT.Copy, scale=pscale[:, c:c + 1]).then_inc(y_hi, 1)
                hi_w(L_BP, 0, 1)
                for q in range(4):
                    x = gatesP[:, 4 * q:4 * q + 4, :]
                    nc.scalar.activation(x, x, ACT.Sigmoid).then_inc(sgp, 1)
                first = product(L_BP - 1)
                with act.Fori(0, N_BP // SLOTS) as i:
                    for j in range(SLOTS):
                        act.wait_ge(gd, i * (2 * SLOTS) + (first + 2 * j + 2))
                        hi_w(L_BP, i, j + 2)
                        nc.scalar.copy(chunk(atHL[0], i * (2 * SLOTS) + 2 * j, 2),
                                       chunk(attnT, i * (2 * SLOTS) + 2 * j, 2)).then_inc(a_hi, 1)
                        x = chunk(gatesA, i * (2 * SLOTS) + 2 * j, 2)
                        nc.scalar.activation(x, x, ACT.Sigmoid).then_inc(sga, 1)
                with act.Fori(0, N_BA // SLOTS) as i:
                    for j in range(SLOTS):
                        gemm_out(act, L_BA, i, j)
                        hi_w(L_BA, i, j + 2)
                        act.wait_ge(mg, i * SLOTS + (j + 1))
                        nc.scalar.copy(chunk(meHL[0], i * SLOTS + j), chunk(mergedT, i * SLOTS + j)).then_inc(m_hi, 1)

                def out(i, j):
                    gemm_out(act, L_WO, i, j)
                    nc.scalar.copy(chunk(woT, i * SLOTS + j), bank(L_WO, j)).then_inc(ge, 1)

                with act.Fori(0, N_WO // SLOTS - 1) as i:
                    for j in range(SLOTS):
                        out(i, j)
                        hi_w(L_WO, i, j + 2)
                for j in range(SLOTS):
                    out(N_WO // SLOTS - 1, j)
                    if j < 2:
                        hi_w(L_WQ - SLOTS, 0, j + 2)

            @block.vector
            def _(v):
                lo_w(nc.vector, L_BP, 0, 0)
                for c in range(POOL_CH):
                    v.wait_ge(y_hi, c + 1)
                    nc.vector.scalar_tensor_tensor(out=ypHL[1][:, c, :], in0=PS[:, c % 2, 0:T], scalar=pscale[:, c:c + 1],
                                                   in1=ypHL[0][:, c, :].bitcast(F32), op0=ALU.mult,
                                                   op1=ALU.subtract).then_inc(y_lo, 1)
                lo_w(nc.vector, L_BP, 0, 1)
                first = product(L_BP - 1)
                v.wait_ge(sgp, 4)
                with v.Fori(0, N_BP // SLOTS) as i:
                    for j in range(SLOTS):
                        for h in range(2):
                            v.wait_ge(gd, i * (2 * SLOTS) + (first + 2 * j + h + 1))
                            c = i * (2 * SLOTS) + (2 * j + h)
                            nc.vector.tensor_tensor(chunk(mergedT, c), PS[:, GB + h, 0:T], chunk(gatesP, c),
                                                    op=ALU.mult).then_inc(ge, 1)
                        lo_w(nc.vector, L_BP, i, j + 2)
                        v.wait_ge(a_hi, i * SLOTS + (j + 1))
                        c = i * (2 * SLOTS) + 2 * j
                        nc.vector.tensor_tensor(chunk(atHL[1], c, 2), chunk(attnT, c, 2), chunk(atHL[0], c, 2).bitcast(F32),
                                                op=ALU.subtract).then_inc(a_lo, 1)
                v.wait_ge(sga, N_BP)
                v.wait_ge(ge, product(L_BA - 1) + 2)
                with v.Fori(0, N_BA // SLOTS) as i:
                    for j in range(SLOTS):
                        c = i * SLOTS + j
                        m = chunk(mergedT, c)
                        gemm_out(v, L_BA, i, j)
                        nc.vector.tensor_tensor(tmp[:, j % 2, :], bank(L_BA, j), chunk(gatesA, c), op=ALU.mult).then_inc(ge, 1)
                        v.wait_ge(ge, i * SLOTS + (product(L_BA + j) + 2))
                        nc.vector.tensor_tensor(m, m, tmp[:, j % 2, :], op=ALU.add).then_inc(mg, 1)
                        lo_w(nc.vector, L_BA, i, j + 2)
                        v.wait_ge(m_hi, i * SLOTS + (j + 1))
                        nc.vector.tensor_tensor(chunk(meHL[1], c), m, chunk(meHL[0], c).bitcast(F32),
                                                op=ALU.subtract).then_inc(m_lo, 1)
                with v.Fori(0, N_WO // SLOTS - 1) as i:
                    for j in range(SLOTS):
                        lo_w(nc.vector, L_WO, i, j + 2)
                for j in range(2):
                    lo_w(nc.vector, L_WQ - SLOTS, 0, j + 2)
        scope.close()
        gas.close()
        mid.close()
        spare = PT_r[:, DK:2 * DK, :].rearrange("p a t -> p (a t)")
        wh[0] = [spare[:, n * D:(n + 1) * D].rearrange("p (k c) -> p k c", c=P) for n in range(2)]

        scope = ExitStack()
        XR = sb(scope, "XR", [P, 3, D])
        lnp = sb(scope, "lnp", [P, 2, D])
        bst = sb(scope, "bst", [P, 3, 4, 6])
        mv = sb(scope, "mv", [P, 3, 2])
        rs = sb(scope, "rs", [P, 3, 3])
        eps = sb(scope, "eps", [P, 1])
        c8 = sem("c8")
        t9 = sem("t9")
        r9 = sem("r9")
        n9 = sem("n9")
        q9 = sem("q9")
        s9 = sem("s9")
        x9 = sem("x9")
        g9 = sem("g9")
        h9g, h9v = sem("h9g"), sem("h9v")
        u9 = sem("u9")
        z9 = sem("z9")
        l9 = sem("l9")
        ADD = 1024
        h_st = sem("h_st")
        wd = (P, P, NS_TOK)
        with nc.Block() as block:
            @block.sync
            def _(sp):
                sp.dma_start(XR[:, 0:TT, :], x_d[0:NP_TOK].rearrange("(t p) d -> p t d", p=P)).then_inc(c8, 16)
                sp.dma_start(XR[0:NS_TOK, 2, :], x_d[NP_TOK:T]).then_inc(c8, 16)
                for n in range(2):
                    sp.dma_start(lnp[:, n, :], ln_d[n:n + 1, :].to_broadcast([P, D])).then_inc(c8, 16)
                for t in range(3):
                    sp.wait_ge(h9g, t + 1)
                    sp.wait_ge(h9v, t + 1)
                    sp.dma_start(h_d[t * P:t * P + wd[t], :], XR[0:wd[t], t, :]).then_inc(h_st, 16)
                sp.wait_ge(h_st, 48)

            @block.tensor
            def _(pe):
                for t in range(3):
                    for q in range(4):
                        n = 4 * t + q
                        if n >= 2:
                            pe.wait_ge(r9, n - 1)
                        for j in range(4):
                            m = nc.tensor.transpose(PS[0:wd[t], n % 2, j * P:(j + 1) * P],
                                                    woT[:, 4 * q + j, t * P:t * P + wd[t]], ident[:, :])
                        m.then_inc(t9, 1)
                for t in range(3):
                    pe.wait_ge(h9g, t + 1)
                    pe.wait_ge(h9v, t + 1)
                    for q in range(4):
                        n = 4 * t + q
                        if n >= 2:
                            pe.wait_ge(l9, n - 1)
                        for j in range(4):
                            m = nc.tensor.transpose(PS[:, 2 + n % 2, j * P:j * P + wd[t]],
                                                    XR[0:wd[t], t, (4 * q + j) * P:(4 * q + j + 1) * P],
                                                    ident[0:wd[t], 0:wd[t]])
                        m.then_inc(u9, 1)

            def columns(t, q):
                return ([x[:, 4 * q:4 * q + 4, t * P:t * P + wd[t]] for x in hHL],
                        PS[:, 2 + (4 * t + q) % 2, :].rearrange("p (j t) -> p j t", j=4)[:, :, 0:wd[t]])

            @block.scalar
            def _(act):
                for n in range(2):
                    hi_w(L_WQ, 0, n)
                for t in range(3):
                    w = wd[t]
                    act.wait_ge(n9, t + 1)
                    nc.scalar.activation(rs[0:w, t, 0:1], mv[0:w, t, 1:2], ACT.Sqrt, bias=eps[0:w, 0:1]).then_inc(q9, 1)
                    act.wait_ge(s9, t + 1)
                    nc.scalar.activation(XR[0:w, t, :], XR[0:w, t, :], ACT.Identity, bias=rs[0:w, t, 2:3],
                                         scale=rs[0:w, t, 1:2]).then_inc(x9, 1)
                for t in range(3):
                    for q in range(4):
                        act.wait_ge(u9, 4 * t + q + 1)
                        (hi, lo), src = columns(t, q)
                        nc.scalar.copy(hi, src).then_inc(z9, 1)

            @block.gpsimd
            def _(g):
                for n in range(2):
                    lo_w(nc.gpsimd, L_WQ, 0, n)
                for t in range(3):
                    g.wait_ge(g9, t + 1)
                    x = XR[0:wd[t], t, 0:ADD]
                    nc.gpsimd.tensor_tensor(x, x, lnp[0:wd[t], 1, 0:ADD], op=ALU.add).then_inc(h9g, 1)

            @block.vector
            def _(v):
                n = [0]

                def link(ins):
                    n[0] += 1
                    ins.then_inc(d7, 1)
                    v.wait_ge(d7, n[0])

                def moments(t):
                    w = wd[t]
                    for q in range(4):
                        x = XR[0:w, t, q * 512:(q + 1) * 512]
                        v.wait_ge(t9, 4 * t + q + 1)
                        nc.vector.scalar_tensor_tensor(out=x, in0=x, scalar=ALPHA, in1=PS[0:w, (4 * t + q) % 2, :],
                                                       op0=ALU.mult, op1=ALU.add).then_inc(r9, 1)
                        if q > 0:
                            v.wait_ge(r9, 4 * t + q)
                            nc.vector.bn_stats(bst[0:w, t, q - 1, :], XR[0:w, t, (q - 1) * 512:q * 512])
                    v.wait_ge(r9, 4 * t + 4)
                    link(nc.vector.bn_stats(bst[0:w, t, 3, :], XR[0:w, t, 3 * 512:]))
                    nc.vector.bn_aggr(mv[0:w, t, :], bst[0:w, t, :, :]).then_inc(n9, 1)

                def rstd(t):
                    w = wd[t]
                    v.wait_ge(q9, t + 1)
                    link(nc.vector.reciprocal(rs[0:w, t, 1:2], rs[0:w, t, 0:1]))
                    nc.vector.scalar_tensor_tensor(out=rs[0:w, t, 2:3], in0=mv[0:w, t, 0:1], scalar=-1.0,
                                                   in1=rs[0:w, t, 1:2], op0=ALU.mult, op1=ALU.mult).then_inc(s9, 1)

                def affine(t):
                    w = wd[t]
                    v.wait_ge(x9, t + 1)
                    x = XR[0:w, t, :]
                    link(nc.vector.tensor_tensor(x, x, lnp[0:w, 0, :], op=ALU.mult))
                    v.sem_inc(g9, 1)
                    x = XR[0:w, t, ADD:]
                    nc.vector.tensor_tensor(x, x, lnp[0:w, 1, ADD:], op=ALU.add).then_inc(h9v, 1)

                link(nc.vector.memset(eps[:, :], EPS))
                v.wait_ge(c8, 64)
                moments(0)
                rstd(0)
                moments(1)
                affine(0)
                rstd(1)
                moments(2)
                affine(1)
                rstd(2)
                affine(2)
                for t in range(3):
                    for q in range(4):
                        v.wait_ge(z9, 4 * t + q + 1)
                        (hi, lo), src = columns(t, q)
                        nc.vector.tensor_tensor(lo, src, hi.bitcast(F32), op=ALU.subtract).then_inc(l9, 1)
        scope.close()

        scope = ExitStack()
        Sst = [sb(scope, f"Sst{i}", [P, 512]) for i in range(2)]
        skT = sb(scope, "skT2", [P, 16, P])
        qg = [sb(scope, f"qg{i}", [P, 16, GT]) for i in range(2)]
        c9 = sem("c9")
        qg_ok = sem("qg_ok")
        sc_m = sem("sc_m")
        sc_c = sem("sc_c")
        sc_st = [sem(f"sc_st{i}") for i in range(2)]
        with nc.Block() as block:
            @block.sync
            def _(sp):
                sp.dma_start(skT[:, :, :], skT_d).then_inc(c9, 16)
                next_loads(sp, L_WQ, N_LOADS - L_WQ)
                for gr in range(NG):
                    sp.wait_ge(sc_c, gr + 1)
                    sp.dma_start(score_d[gr], Sst[gr % 2][:, :]).then_inc(sc_st[gr % 2], 16)
                sp.wait_ge(sc_st[0], 16 * 5)
                sp.wait_ge(sc_st[1], 16 * 4)

            @block.tensor
            def _(pe):
                with pe.Fori(0, (N_LOADS - L_WQ) // SLOTS) as i:
                    for j in range(SLOTS):
                        gemm3(pe, L_WQ, i, j, *hHL)
                pe.wait_ge(c9, 16)
                for gr in range(NG):
                    pe.wait_ge(qg_ok, gr + 1)
                    if gr >= 2:
                        pe.wait_ge(sc_c, gr - 1)
                    for h in range(8):
                        for hf in range(2):
                            m = nc.tensor.matmul(
                                PS[32 * (h // 2):32 * (h // 2) + 32, 2 + gr % 2,
                                   (2 * (h % 2) + hf) * P:(2 * (h % 2) + hf + 1) * P],
                                qg[gr % 2][:, 2 * h + hf, :], skT[:, 2 * h + hf, :], start=True, stop=True,
                                tile_position=(0, 32 * (h // 2)))
                    m.then_inc(sc_m, 1)

            @block.vector
            def _(v):
                with v.Fori(0, (N_LOADS - L_WQ) // SLOTS - 1) as i:
                    for j in range(SLOTS):
                        lo_w(nc.vector, L_WQ, i, j + 2)
                for j in range(2):
                    lo_w(nc.vector, N_LOADS - SLOTS, 0, j + 2)
                v.wait_ge(ge, product(N_LOADS - 1) + 2)
                for gr in range(NG):
                    if gr >= 2:
                        v.wait_ge(sc_m, gr - 1)
                    nc.vector.tensor_copy(qg[gr % 2][:, :, :], pqT[:, :, gr * GT:(gr + 1) * GT]).then_inc(qg_ok, 1)

            @block.scalar
            def _(act):
                def out(i, j):
                    gemm_out(act, L_WQ, i, j)
                    nc.scalar.copy(pqT[:, bass.ds(i * SLOTS + j, 1), :].rearrange("p a t -> p (a t)"),
                                   bank(L_WQ, j)).then_inc(ge, 1)

                last = (N_LOADS - L_WQ) // SLOTS - 1
                with act.Fori(0, last) as i:
                    for j in range(SLOTS):
                        out(i, j)
                        hi_w(L_WQ, i, j + 2)
                for j in range(SLOTS):
                    out(last, j)
                    if j < 2:
                        hi_w(N_LOADS - SLOTS, 0, j + 2)
                for gr in range(NG):
                    act.wait_ge(sc_m, gr + 1)
                    if gr >= 2:
                        act.wait_ge(sc_st[gr % 2], 16 * (gr // 2))
                    nc.scalar.copy(Sst[gr % 2][:, :], PS[:, 2 + gr % 2, :]).then_inc(sc_c, 1)
        scope.close()
        actT.close()
        rings.close()

        Ur = [sb(top, f"Ur{s}", [P, D]) for s in range(SB)]
        Vr = [sb(top, f"Vr{s}", [P, D]) for s in range(SB)]
        hnext = sb(top, "hnext", [P, D])
        hcur = sb(top, "hcur", [P, D])
        hres = sb(top, "hres", [GT, D])
        R = sb(top, "R", [GT, D])
        lnq = sb(top, "lnq", [GT, 2, D])
        sel = sb(top, "sel", [P, GT])
        iot = sb(top, "iot", [P, 16])
        sw = sb(top, "sw", [P, 4, P])
        keys = sb(top, "keys", [P, 4, P])
        m16 = sb(top, "m16", [P, 4, 16])
        i16 = sb(top, "i16", [P, 4, 16], U32)
        i16f = sb(top, "i16f", [P, 4, 16])
        cand = sb(top, "cand", [P, 2, 256])
        tv = sb(top, "tv", [P, 2, 16])
        ti = sb(top, "ti", [P, 2, 16], U32)
        tab = sb(top, "tab", [P, 2, 2, 16], U32)
        tabf = sb(top, "tabf", [P, 2, 2, 16])
        oh = sb(top, "oh", [P, 2, 16, 16])
        es = sb(top, "es", [P, 2, 2, 16])
        ef = sb(top, "ef", [P, 2, 16])
        eid_next = sb(top, "eid_next", [P, NSTEP], I32)
        eid = sb(top, "eid", [P, 2, NSTEP], I32)
        gsum = sb(top, "gsum", [P, 2, 2])
        gate_next = sb(top, "gate_next", [P, NSTEP])
        gate = sb(top, "gate", [P, NSTEP])
        dots = sb(top, "dots", [P, 2, SB])
        gel = sb(top, "gel", [P, 2, SB])
        wgt = sb(top, "wgt", [P, 2, SB])
        Dm = sb(top, "Dm", [P, 2, SB, GT])
        bs2 = sb(top, "bs2", [GT, 4, 6])
        mv2 = sb(top, "mv2", [GT, 2])
        rs2 = sb(top, "rs2", [GT, 3])
        ep2 = sb(top, "ep2", [GT, 1])
        cA = sem("cA")
        h_ld, h_fr, h_ok = sem("h_ld"), sem("h_fr"), sem("h_ok")
        sw_ld, sw_fr = sem("sw_ld"), sem("sw_fr")
        top_ok = sem("top_ok")
        eid_ok, eid_own = sem("eid_ok"), sem("eid_own")
        exp_in, exp_ok = sem("exp_in"), sem("exp_ok")
        u_ld = [sem(f"u_ld{s}") for s in range(SB)]
        v_ld = [sem(f"v_ld{s}") for s in range(SB)]
        dot = sem("dot")
        gelu = sem("gelu")
        dm = sem("dm")
        pv = sem("pv")
        z_fr = sem("z_fr")
        ln_a, ln_s, ln_b, ln_c = sem("ln_a"), sem("ln_s"), sem("ln_b"), sem("ln_c")
        y_st, r_fr = sem("y_st"), sem("r_fr")
        dA = sem("dA")
        gathers = sem("gathers")
        with nc.Block() as block:
            @block.sync
            def _(sp):
                sp.dma_start(sel[:, :], sel_d).then_inc(cA, 16)
                sp.dma_start(iot[:, :], iota_d).then_inc(cA, 16)
                for n in range(2):
                    sp.dma_start(lnq[:, n, :], ln_d[2 + n:3 + n, :].to_broadcast([GT, D])).then_inc(cA, 16)

                def load_scores(gr):
                    sp.wait_ge(sw_fr, gr + 1)
                    sp.dma_start(sw[:, :, :].rearrange("p a k -> p (a k)"),
                                 score_d[bass.ds(gr, 1)].rearrange("o p k -> (o p) k")).then_inc(sw_ld, 16)

                def load_h(gr):
                    sp.wait_ge(h_fr, gr + 1)
                    for q in range(4):
                        sp.dma_start(hnext[32 * q:32 * q + 32, :], h_d[bass.ds(gr * GT, GT)]).then_inc(h_ld, 16)

                def store_y(gr):
                    sp.wait_ge(ln_c, gr + 1)
                    sp.dma_start(y_d[bass.ds(gr * GT, GT)], R[:, :]).then_inc(y_st, 16)
                    sp.wait_ge(y_st, gr * 16 + 16)
                    sp.sem_inc(r_fr, 1)

                sp.sem_inc(r_fr, 1)
                load_scores(0)
                load_h(0)
                load_scores(1)
                load_h(1)
                with sp.Fori(0, NG - 2) as i:
                    load_scores(i + 2)
                    load_h(i + 2)
                    store_y(i)
                store_y(NG - 2)
                store_y(NG - 1)
                sp.wait_ge(y_st, 16 * NG)
                sp.wait_ge(raw_out, 64)
                sp.wait_ge(pool_out, 16)
                sp.wait_ge(out_done, 16 * n_out[0])

            @block.gpsimd
            def _(g):
                def group(gr, par):
                    g.wait_ge(top_ok, gr + 1)
                    g.sem_inc(gathers, 1)
                    nc.gpsimd.tensor_copy(eid[:, par, :], eid_next[:, :]).then_inc(eid_own, 1)
                    g.wait_ge(eid_own, 1)
                    g.sem_clear(eid_own)
                    g.sem_inc(eid_ok, 1)
                    for b in range(NB):
                        for s in range(SB):
                            c = b * SB + s
                            g.wait_ge(dot, gr * NSTEP + (c + 1))
                            g.sem_inc(gathers, 1)
                            nc.gpsimd.indirect_dma_start(
                                out=Ur[s][:, :], out_offset=None, in_=u_d,
                                in_offset=bass.IndirectOffsetOnAxis(ap=eid[:, par, c:c + 1], axis=0)).then_inc(u_ld[s], 16)
                        for s in range(SB):
                            c = b * SB + s
                            g.wait_ge(pv, gr * NSTEP + (c + 1))
                            g.sem_inc(gathers, 1)
                            nc.gpsimd.indirect_dma_start(
                                out=Vr[s][:, :], out_offset=None, in_=v_d,
                                in_offset=bass.IndirectOffsetOnAxis(ap=eid[:, par, c:c + 1], axis=0)).then_inc(v_ld[s], 16)


                with g.Fori(0, NG // 2) as i:
                    group(2 * i, 0)
                    group(2 * i + 1, 1)
                group(NG - 1, (NG - 1) % 2)

            @block.tensor
            def _(pe):
                pe.sem_inc(pv, SB)
                with pe.Fori(0, NG) as i:
                    pe.wait_ge(z_fr, i + 1)
                    for b in range(NB):
                        pe.wait_ge(dm, i * NB + (b + 1))
                        for s in range(SB):
                            pe.wait_ge(v_ld[s], i * (16 * NB) + 16 * (b + 1))
                            for q in range(4):
                                m = nc.tensor.matmul(PS[0:GT, q, :], Dm[:, b % 2, s, :], Vr[s][:, q * 512:(q + 1) * 512],
                                                     start=(b == 0 and s == 0), stop=(b == NB - 1 and s == SB - 1),
                                                     tile_position=(0, 0))
                            m.then_inc(pv, 1)

            @block.scalar
            def _(act):
                act.sem_inc(h_fr, 1)

                def exps(gr):
                    act.wait_ge(exp_in, gr + 1)
                    nc.scalar.activation(gate_next[:, :], tv[:, :, :].rearrange("p h k -> p (h k)"), ACT.Exp).then_inc(exp_ok, 1)

                def group(gr, first, last):
                    act.wait_ge(h_ld, gr * 64 + 64)
                    act.wait_ge(dot, gr * NSTEP + SB)
                    if not first:
                        act.wait_ge(h_ok, 2 * gr)
                    nc.scalar.copy(hcur[:, :], hnext[:, :]).then_inc(h_ok, 1)
                    act.wait_ge(h_ok, 2 * gr + 1)
                    act.sem_inc(h_fr, 1)
                    for b in range(NB):
                        act.wait_ge(dot, gr * NSTEP + (b + 2) * SB)
                        nc.scalar.activation(gel[:, b % 2, :], dots[:, b % 2, :], ACT.Gelu).then_inc(gelu, 1)
                        if b == 0 and not first:
                            norm(gr - 1)
                        if b == 1 and not last:
                            exps(gr + 1)
                    if not first:
                        act.wait_ge(z_fr, gr + 1)
                    nc.scalar.copy(hres[:, :], hcur[0:GT, :]).then_inc(h_ok, 1)

                def norm(gr):
                    act.wait_ge(ln_a, gr + 1)
                    nc.scalar.activation(rs2[:, 0:1], mv2[:, 1:2], ACT.Sqrt, bias=ep2[:, 0:1]).then_inc(ln_s, 1)

                exps(0)
                group(0, True, False)
                with act.Fori(1, NG - 1) as i:
                    group(i, False, False)
                group(NG - 1, False, True)
                norm(NG - 1)

            @block.vector
            def _(v):
                n = [0]

                def link(ins):
                    n[0] += 1
                    ins.then_inc(dA, 1)
                    v.wait_ge(dA, n[0])

                def unlink():
                    v.sem_clear(dA)
                    n[0] = 0

                def top16(vals, idx, src):
                    link(nc.vector.max(vals[:, 0:8], src))
                    link(nc.vector.max_index(idx[:, 0:8], vals[:, 0:8], src))
                    link(nc.vector.match_replace(src, vals[:, 0:8], src, NEG))
                    link(nc.vector.max(vals[:, 8:16], src))
                    link(nc.vector.max_index(idx[:, 8:16], vals[:, 8:16], src))

                def choose(gr):
                    v.wait_ge(sw_ld, gr * 16 + 16)
                    link(nc.vector.tensor_copy(keys[:, :, :], sw[:, :, :]))
                    v.sem_inc(sw_fr, 1)
                    for a in range(4):
                        top16(m16[:, a, :], i16[:, a, :], keys[:, a, :])
                    mh = m16[:, :, :].rearrange("p (h f) k -> p h f k", f=2)
                    for h in range(2):
                        link(nc.vector.tensor_tensor(cand[:, h, :].rearrange("p (i j) -> p i j", i=16),
                                                     mh[:, h, 0, :].unsqueeze(2).to_broadcast([P, 16, 16]),
                                                     mh[:, h, 1, :].unsqueeze(1).to_broadcast([P, 16, 16]), op=ALU.add))
                    link(nc.vector.tensor_copy(i16f[:, :, :], i16[:, :, :]))
                    for h in range(2):
                        top16(tv[:, h, :], ti[:, h, :], cand[:, h, :])
                    link(nc.vector.tensor_copy(gsum[:, :, 0:1], tv[:, :, 0:1]))
                    link(nc.vector.tensor_tensor(tv[:, :, :], tv[:, :, :], gsum[:, :, 0:1].to_broadcast([P, 2, 16]),
                                                 op=ALU.subtract))
                    v.sem_inc(exp_in, 1)
                    link(nc.vector.tensor_scalar(tab[:, 0, :, :], ti[:, :, :], 4, None, op0=ALU.logical_shift_right))
                    link(nc.vector.tensor_scalar(tab[:, 1, :, :], ti[:, :, :], 15, None, op0=ALU.bitwise_and))
                    link(nc.vector.tensor_copy(tabf[:, :, :, :], tab[:, :, :, :]))
                    fh = i16f[:, :, :].rearrange("p (h f) k -> p h f k", f=2)
                    for f in range(2):
                        for h in range(2):
                            link(nc.vector.tensor_tensor(oh[:, h, :, :],
                                                         tabf[:, f, h, :].unsqueeze(2).to_broadcast([P, 16, 16]),
                                                         iot[:, :].unsqueeze(1).to_broadcast([P, 16, 16]),
                                                         op=ALU.is_equal))
                            link(nc.vector.tensor_tensor(oh[:, h, :, :], oh[:, h, :, :],
                                                         fh[:, h, f, :].unsqueeze(1).to_broadcast([P, 16, 16]),
                                                         op=ALU.mult))
                        link(nc.vector.tensor_reduce(es[:, f, :, :], oh[:, :, :, :], AX, ALU.add))
                    link(nc.vector.tensor_scalar(es[:, 0, :, :], es[:, 0, :, :], 128.0, None, op0=ALU.mult))
                    link(nc.vector.tensor_tensor(ef[:, :, :], es[:, 0, :, :], es[:, 1, :, :], op=ALU.add))
                    v.wait_ge(eid_ok, gr + 1)
                    link(nc.vector.tensor_copy(eid_next[:, :], ef[:, :, :].rearrange("p h k -> p (h k)")))
                    v.sem_inc(top_ok, 1)
                    v.wait_ge(exp_ok, gr + 1)
                    gn = gate_next[:, :].rearrange("p (h k) -> p h k", h=2)
                    link(nc.vector.tensor_reduce(gsum[:, :, 0], gn, AX, ALU.add))
                    link(nc.vector.reciprocal(gsum[:, :, 1], gsum[:, :, 0]))
                    link(nc.vector.tensor_tensor(gn, gn, gsum[:, :, 1:2].to_broadcast([P, 2, 16]), op=ALU.mult))
                    unlink()

                def norm_a(gr):
                    v.wait_ge(pv, gr * NSTEP + (NSTEP + SB))
                    v.wait_ge(h_ok, 2 * gr + 2)
                    v.wait_ge(r_fr, gr + 1)
                    link(nc.vector.scalar_tensor_tensor(out=R[:, :], in0=hres[:, :], scalar=ALPHA,
                                                        in1=PS[0:GT, 0:4, :].rearrange("p q d -> p (q d)"),
                                                        op0=ALU.mult, op1=ALU.add))
                    v.sem_inc(z_fr, 1)
                    for q in range(4):
                        link(nc.vector.bn_stats(bs2[:, q, :], R[:, q * 512:(q + 1) * 512]))
                    link(nc.vector.bn_aggr(mv2[:, :], bs2[:, :, :]))
                    v.sem_inc(ln_a, 1)
                    unlink()

                def norm_b(gr):
                    v.wait_ge(ln_s, gr + 1)
                    link(nc.vector.reciprocal(rs2[:, 1:2], rs2[:, 0:1]))
                    link(nc.vector.tensor_scalar(R[:, :], R[:, :], mv2[:, 0:1], rs2[:, 1:2], op0=ALU.subtract, op1=ALU.mult))
                    link(nc.vector.tensor_tensor(R[:, :], R[:, :], lnq[:, 0, :], op=ALU.mult))
                    link(nc.vector.tensor_tensor(R[:, :], R[:, :], lnq[:, 1, :], op=ALU.add))
                    v.sem_inc(ln_c, 1)
                    unlink()

                def group(gr, first, last):
                    link(nc.vector.tensor_copy(gate[:, :], gate_next[:, :]))
                    unlink()
                    v.wait_ge(h_ok, 2 * gr + 1)
                    for b in range(NB):
                        for s in range(SB):
                            v.wait_ge(u_ld[s], gr * (16 * NB) + 16 * (b + 1))
                            nc.vector.tensor_tensor_reduce(out=Ur[s][:, :], in0=Ur[s][:, :], in1=hcur[:, :], scale=1.0,
                                                           scalar=0.0, op0=ALU.mult, op1=ALU.add,
                                                           accum_out=dots[:, b % 2, s:s + 1]).then_inc(dot, 1)
                        v.wait_ge(gelu, gr * NB + (b + 1))
                        link(nc.vector.tensor_tensor(wgt[:, b % 2, :], gel[:, b % 2, :], gate[:, b * SB:(b + 1) * SB],
                                                     op=ALU.mult))
                        if b or not first:
                            v.wait_ge(pv, gr * NSTEP + b * SB)
                        link(nc.vector.tensor_tensor(Dm[:, b % 2, :, :],
                                                     sel[:, :].unsqueeze(1).to_broadcast([P, SB, GT]),
                                                     wgt[:, b % 2, :].unsqueeze(2).to_broadcast([P, SB, GT]), op=ALU.mult))
                        v.sem_inc(dm, 1)
                        unlink()
                        if b == 0 and not first:
                            norm_a(gr - 1)
                        if b == 1 and not first:
                            norm_b(gr - 1)
                        if b == 1 and not last:
                            choose(gr + 1)

                v.sem_inc(dot, SB)
                for x in (sw_fr, eid_ok, z_fr):
                    v.sem_inc(x, 1)
                link(nc.vector.memset(ep2[:, :], EPS))
                unlink()
                v.wait_ge(cA, 64)
                choose(0)
                group(0, True, False)
                with v.Fori(1, NG - 1) as i:
                    group(i, False, False)
                group(NG - 1, False, True)
                norm_a(NG - 1)
                norm_b(NG - 1)


_OUTS = [("y", (T, D)), ("kvT", (P, 6, NKV, T)), ("ktail", (BS, 252, 512)), ("vtail", (BS, 252, 512)),
         ("poolT", (P, POOL_CH, POOL_ST + NS_TOK)), ("spool", (BS, 11, 1024))]


def constants(np):
    f = np.float32
    p = np.arange(P)
    ident = np.eye(P, dtype=f)
    rot = np.zeros((P, P), f)
    for m in range(32):
        rot[(m + 16) % 32, m] = 1.0
    pos = np.concatenate([np.arange(NP_TOK), np.tile(256 + np.arange(LS), BS)]).astype(f)
    inv = (f(500000.0) ** (-np.arange(16, dtype=f) / f(16))).astype(f)
    ang = (pos[:, None] * inv).astype(f)
    cs = np.zeros((P, 2, T), f)
    cs[:, 0] = 1.0
    cs[0:16, 0] = cs[16:32, 0] = np.cos(ang).T
    cs[0:16, 1] = -np.sin(ang).T
    cs[16:32, 1] = np.sin(ang).T
    big = f(-1e30)
    diag = np.where(p[None, :] <= p[:, None], f(0), big).astype(f)
    maskp = np.concatenate([diag, np.zeros((P, P), f), diag], 1)
    x = p % 8
    maskn = np.full((P, BS, NS_TOK), big, f)
    for b in range(BS):
        for l2 in range(LS):
            maskn[:, b, b * LS + l2] = np.where(l2 <= x % LS, f(0), big)
    maskc = np.zeros((P, 2, 480), f)
    n = np.arange(NCMP)
    for t in range(TT):
        ok = 16 * n[None, :] + 31 <= (t * P + p)[:, None]
        maskc[:, 0].reshape(P, NH, TT, NCMP)[:, :, t, :] = np.where(ok, f(0), big)[:, None, :]
    rb = (p % 32) // LS
    ok = rb[:, None] == np.arange(BS)[None, :]
    maskc[:, 1].reshape(P, NKV, BS, NCMP)[:] = np.where(ok, f(0), big)[:, None, :, None]
    keepc = (maskc == 0).astype(f)
    rcnt = np.ones((P, 4, 16), f)
    for g, w in enumerate((2, 4, 8, 16)):
        rcnt[:, g] = (w / np.minimum(w, np.arange(16) + 1)).astype(f)
    sel = (p[:, None] % GT == np.arange(GT)[None, :]).astype(f)
    iota = np.tile(np.arange(16, dtype=f), (P, 1))
    pidx = p.astype(f)[:, None].copy()
    return dict(ident=ident, rot=rot, cs=cs, maskp=maskp, maskn=maskn, maskc=maskc, keepc=keepc, rcnt=rcnt,
                sel=sel, iota=iota, pidx=pidx)


def kernel(**inputs):
    import numpy as np
    import concourse.bacc as _bacc
    from concourse.bass_utils import run_bass_kernel_spmd as _run

    a = {k: np.asarray(v) for k, v in inputs.items()}

    def chunks(w):
        k, n = w.shape
        return w.reshape(k // P, P, n // P, P).transpose(2, 1, 0, 3).reshape(n // P, P, k)

    def pagesT(c):
        return c[0].transpose(0, 3, 2, 1).reshape(-1, NKV * P)

    x = np.concatenate([a["x_prompt"][0], a["x_sample"].reshape(NS_TOK, D)], 0)
    w_in = a["w_in"][0]
    cols = chunks(w_in[:, :6144])
    gates = chunks(w_in[:, 6192:])
    wbp = chunks(a["w_branch_pool"][0]).reshape(8, 2, P, 1024).transpose(0, 2, 1, 3).reshape(8, P, 2048)
    stream = np.concatenate([cols[8:24], cols[32:36], cols[40:44], cols[24:32], cols[36:40], cols[44:48], cols[0:8],
                             gates, wbp, chunks(a["w_branch_attn"][0]), chunks(a["w_out"][0]),
                             chunks(a["peer_wq"][0])])
    kwin = a["cache_k_win"][0].reshape(BS, 256, 512)
    vwin = a["cache_v_win"][0].reshape(BS, 256, 512)
    arrays = dict(
        xT=x.T, x=x, w=stream,
        nsa=w_in[:, 6144:6192].reshape(DK, P, 48).transpose(1, 0, 2),
        grp=a["pool_grp_w"][0],
        pscale=a["pool_scale"][0].reshape(POOL_CH, P).T,
        stateT=a["state_pool"][0].transpose(2, 0, 1).reshape(1024, BS * POOL_ST), state=a["state_pool"][0],
        kcT=pagesT(a["cache_k_cmp"]), vcT=pagesT(a["cache_v_cmp"]), ksT=pagesT(a["cache_k_slc"]),
        vs=a["cache_v_slc"][0].reshape(-1, 512),
        kwT=kwin.reshape(BS, 2, P, NKV, HD).transpose(0, 4, 1, 3, 2).reshape(BS, P, 1024),
        vw=vwin.reshape(BS, 2, P, 512).transpose(0, 2, 1, 3).reshape(BS, P, 1024),
        kwin=kwin, vwin=vwin, ptab=a["page_table"].reshape(-1),
        w1=np.stack([a["cmp_w1_k"][0].transpose(1, 0, 2), a["cmp_w1_v"][0].transpose(1, 0, 2)]),
        w2=np.stack([a["cmp_w2_k"][0], a["cmp_w2_v"][0]], 1),
        peT=np.stack([a["cmp_pe_k"][0].T, a["cmp_pe_v"][0].T], 1),
        ln=np.stack([a["ln1_g"][0], a["ln1_b"][0], a["ln2_g"][0], a["ln2_b"][0]]),
        skT=a["peer_subkeys"][0].reshape(16, P, P).transpose(2, 0, 1), u=a["peer_u"][0], v=a["peer_v"][0])
    arrays.update(constants(np))
    nc = _bacc.Bacc("TRN2", target_bir_lowering=False, num_devices=1)
    feeds, args = {}, []
    for name, arr in arrays.items():
        feeds[f"in_{name}"] = np.ascontiguousarray(arr)
        args.append(nc.dram_tensor(f"in_{name}", arr.shape, mybir.dt.from_np(arr.dtype), kind="ExternalInput").ap())
    for name, shape in _OUTS:
        args.append(nc.dram_tensor(f"out_{name}", shape, F32, kind="ExternalOutput").ap())
    build(nc, *args)
    r = _run(nc, [feeds], core_ids=[0]).results[0]
    y, kvT, ktail, vtail, poolT, spool = [r[f"out_{name}"] for name, _ in _OUTS]
    kv = kvT.transpose(1, 3, 2, 0)
    kv_p = [kv[n, :NP_TOK][None, None] for n in range(6)]
    kv_s = [kv[n, NP_TOK:].reshape(1, BS, LS, NKV, HD) for n in range(6)]

    def tail(old, new):
        return np.concatenate([old.reshape(1, BS, 252, NKV, HD), new], 2)

    pool = poolT.transpose(2, 1, 0).reshape(POOL_ST + NS_TOK, 1024)
    pool_s = np.concatenate([spool, pool[POOL_ST:].reshape(BS, LS, 1024)], 1)[None]
    return (y[None, :NP_TOK], y[NP_TOK:].reshape(BS, LS, D), *kv_p, pool[None, None, :POOL_ST], *kv_s[:4],
            tail(ktail, kv_s[4]), tail(vtail, kv_s[5]), pool_s)
```

```python
import math
from contextlib import ExitStack

import concourse.bass as bass
from concourse import mybir

F32 = mybir.dt.float32
F32R = mybir.dt.float32r
U32 = mybir.dt.uint32
I32 = mybir.dt.int32
ALU = mybir.AluOpType
ACT = mybir.ActivationFunctionType
AX = mybir.AxisListType.X

P = 128
D = 2048
DK = D // P
NP_TOK = 256
NS_TOK = 32
T = NP_TOK + NS_TOK
TT = 2
BS = 8
LS = 4
NKV = 4
HPG = 4
NH = 16
HD = 128
NCMP = 15
NCHUNK = 16
POOL_CH = 8
POOL_ST = 15
SCALE = float(HD) ** -0.5
ALPHA = 2.0 ** 0.25
EPS = 1e-5
SLOTS = 4
Q0, KS0, KW0, KC0, VC0, VS0, VW0 = 8, 24, 28, 32, 36, 40, 44
N1 = 48
L_QKV, L_POOL, L_GP, L_GA, L_BP, L_BA, L_WO, L_WQ = 0, 40, 48, 64, 80, 88, 104, 120
N_LOADS = 136
GT = 32
NG = T // GT
NSTEP = 32
SB = 8
NB = NSTEP // SB
NEG = -3.0e38


def build(nc, xT_d, x_d, w_d, nsa_d, grp_d, pscale_d, stateT_d,
          state_d, kcT_d, vcT_d, ksT_d, vs_d, kwT_d, vw_d, kwin_d, vwin_d, ptab_d, w1_d, w2_d, peT_d,
          ln_d, skT_d, u_d, v_d, ident_d, rot_d, cs_d, maskp_d, maskn_d, maskc_d, keepc_d, rcnt_d,
          sel_d, iota_d, pidx_d,
          y_d, kvT_d, ktail_d, vtail_d, poolT_d, spool_d):
    h_d = nc.dram_tensor("h_rows", (T, D), F32).ap()
    gate_d = nc.dram_tensor("sample_gates", (3 * NH, NS_TOK), F32).ap()
    gatep_d = nc.dram_tensor("sample_gates_by_pair", (3 * NH, 8, 4), F32).ap()
    score_d = nc.dram_tensor("peer_scores", (NG, P, 512), F32).ap()
    top = ExitStack()

    def sem(name):
        return top.enter_context(nc.semaphore(name))

    def sb(scope, name, shape, dt=F32):
        buf = scope.enter_context(nc.sbuf_tensor(name, shape, dt))
        place[name] = nc.sbuf_base - 4 * math.prod(shape[1:])
        return buf

    def sb_far(scope, name, shape, dt=F32):
        return scope.enter_context(nc.sbuf_tensor(name, shape, dt, side="right"))

    place = {}

    def in_place_of(name, shape):
        return nc.alloc_sbuf_tensor_at(name + "_r", shape, F32R, offset=place[name])

    with top:
        PS = top.enter_context(nc.psum_tensor("PS", [P, 8, 512], F32))
        ident = sb(top, "ident", [P, P])
        rings = ExitStack()
        ring = [sb(rings, f"ring{s}", [P, DK, P]) for s in range(SLOTS)]
        ring_lo = [in_place_of(f"ring{s}", [P, DK, P]) for s in range(SLOTS)]
        lds = [sem(f"lds{s}") for s in range(SLOTS)]
        gd = sem("gd")
        ge = sem("ge")
        out_done = sem("out_done")
        raw_out = sem("raw_out")
        pool_out = sem("pool_out")
        n_out = [0]

        def out_dma(eng, dst, src):
            n_out[0] += 1
            eng.dma_start(dst, src).then_inc(out_done, 16)

        GB = 6

        def product(n):
            return n + 1 + min(max(n + 1 - L_BP, 0), L_BA - L_BP)

        w_hi, w_lo = sem("w_hi"), sem("w_lo")
        wh = [None]

        def split(n):
            return n + 1 if n < L_POOL else n + 1 - (L_BP - L_POOL)

        def load(sp, n, s):
            sp.dma_start(ring[s][:, :, :], w_d[bass.ds(n, 1)].rearrange("o p (k c) -> p (o k) c", k=DK)).then_inc(lds[s], 16)

        def next_loads(sp, first, count, per=1):
            count = min(count, N_LOADS - SLOTS - first)
            with sp.Fori(0, count // SLOTS) as i:
                for s in range(SLOTS):
                    sp.wait_ge(gd, i * (SLOTS * per) + (product(first) + s * per))
                    load(sp, i * SLOTS + (first + SLOTS + s), s)

        def gemm(pe, n, i, j, src, part=(0, DK)):
            if part[0] == 0:
                pe.wait_ge(lds[j], i * 16 + 16 * ((n + j) // SLOTS + 1))
                pe.wait_ge(ge, i * SLOTS + product(n + j))
            for k in range(*part):
                m = nc.tensor.matmul(PS[:, GB + (product(n + j) - 1) % 2, 0:T], ring[j][:, k, :], src[:, k, :],
                                     start=(k == 0), stop=(k == DK - 1))
            if part[1] == DK:
                m.then_inc(gd, 1)

        def hi_w(n, i, j):
            nj = n + j
            nc.scalar.wait_ge(lds[nj % SLOTS], i * 16 + 16 * (nj // SLOTS + 1))
            nc.scalar.copy(wh[0][nj % 2], ring[nj % SLOTS][:, :, :]).then_inc(w_hi, 1)

        def lo_w(eng, n, i, j):
            nj = n + j
            r = ring[nj % SLOTS][:, :, :]
            eng.wait_ge(w_hi, i * SLOTS + split(nj))
            eng.tensor_tensor(ring_lo[nj % SLOTS][:, :, :], r, wh[0][nj % 2].bitcast(F32), op=ALU.subtract).then_inc(w_lo, 1)

        def split_gemm(n, j, hi, lo, out, chunks, ready=None):
            nj = n + j
            for c, (a, b) in enumerate(chunks):
                if ready is not None:
                    ready(b)
                for m_, (w, x) in enumerate(((wh[0][nj % 2], hi), (wh[0][nj % 2], lo),
                                             (ring_lo[nj % SLOTS][:, :, :], hi))):
                    m = nc.tensor.matmul(out, w[:, a, :], x[:, b, :], start=(c == 0 and m_ == 0),
                                         stop=(c == len(chunks) - 1 and m_ == 2))
            m.then_inc(gd, 1)

        def gemm3(pe, n, i, j, hi, lo, ready=None):
            pe.wait_ge(w_lo, i * SLOTS + split(n + j))
            pe.wait_ge(ge, i * SLOTS + product(n + j))
            split_gemm(n, j, hi, lo, bank(n, j), [(k, k) for k in range(DK)], ready)

        HALVES = ((0, DK // 2), (DK // 2, DK))
        QUARTERS = [(q * DK // 4, (q + 1) * DK // 4) for q in range(4)]

        def bank(n, j):
            return PS[:, GB + (product(n + j) - 1) % 2, 0:T]

        def gemm_out(eng, n, i, j):
            eng.wait_ge(gd, i * SLOTS + product(n + j))

        actT = ExitStack()
        xT = sb(actT, "xT", [P, DK, T])
        attnT = sb(actT, "attnT", [P, NH, T])
        mergedT = pqT = xT
        ypoolT = sb(actT, "ypoolT", [P, POOL_CH, T])
        PT = sb(actT, "PT", [P, N1, T])
        gatesP = PT[:, KC0:N1, :]
        woT = PT[:, KC0:N1, :]
        x_r, attn_r, PT_r = [in_place_of(b, [P, n, T])[:, :, :] for b, n in (("xT", DK), ("attnT", DK), ("PT", 2 * DK))]
        xHL = (attn_r, x_r)
        ypHL = (PT_r[:, POOL_CH:DK, :], in_place_of("ypoolT", [P, POOL_CH, T])[:, :, :])
        atHL = (PT_r[:, DK:2 * DK, :], attn_r)
        meHL = (PT_r[:, 0:DK, :], x_r)
        hHL = (PT_r[:, 0:DK, :], attn_r)
        gateT = ypoolT[0:3 * NH, 0, :]
        gateq = ypoolT[0:3 * NH, 1, 0:NS_TOK]
        mid = ExitStack()
        kcb = sb(mid, "kcb", [P, NKV * BS * NCMP])
        kcbp = sb(mid, "kcbp", [P, NKV * NCMP])
        vcb = sb(mid, "vcb", [BS * NCMP, NKV, HD])
        vcbp = sb(mid, "vcbp", [NCMP, NKV, HD])
        pgi = sb(mid, "pgi", [P, 2 * BS], I32)
        cmps = ExitStack()
        CT = sb(cmps, "CT", [P, 2 * BS, NKV * P])
        W1 = sb(cmps, "W1", [P, 32, HD])
        w2 = sb(cmps, "w2", [P, 2, HD])
        peT = sb(cmps, "peT", [P, 2, 32])
        ptab = sb(cmps, "ptab", [P, 2 * BS], I32)
        ptf = sb(cmps, "ptf", [P, 2 * BS])
        pidx = sb(cmps, "pidx", [P, 1])
        c3 = sem("c3")
        w1_ld = sem("w1_ld")
        ix = sem("ix")
        ct_ld = sem("ct_ld")

        def gather_past(g, kv):
            for n in range(2 * BS):
                nc.gpsimd.indirect_dma_start(
                    out=CT[:, n, :], out_offset=None, in_=(kcT_d, vcT_d)[kv],
                    in_offset=bass.IndirectOffsetOnAxis(ap=pgi[:, n:n + 1], axis=0)).then_inc(ct_ld, 16)

        Wn = sb(cmps, "Wn", [P, DK, 3 * NH])
        parts = ExitStack()
        whq = sb(parts, "whq", [P, 2, DK, P], F32R)
        wh[0] = [whq[:, n, :, :] for n in range(2)]
        x_ld = [sem(f"x_ld{q}") for q in range(4)]
        x_hi, x_lo = sem("x_hi"), sem("x_lo")
        x_again = sem("x_again")
        g_done = sem("g_done")
        sg_done = sem("sg_done")
        sg_st = sem("sg_st")
        def page_rows(v):
            v.wait_ge(c3, 96)
            nc.vector.tensor_copy(ptf[:, :], ptab[:, :]).then_inc(ix, 1)
            v.wait_ge(ix, 1)
            nc.vector.tensor_scalar(ptf[:, :], ptf[:, :], float(P), pidx[:, 0:1], op0=ALU.mult, op1=ALU.add).then_inc(ix, 1)
            v.wait_ge(ix, 2)
            nc.vector.tensor_copy(pgi[:, :], ptf[:, :]).then_inc(ix, 1)

        with nc.Block() as block:
            @block.sync
            def _(sp):
                for q in range(4):
                    sp.dma_start(xT[:, 4 * q:4 * q + 4, :],
                                 xT_d[q * 512:(q + 1) * 512].rearrange("(k p) t -> p k t", p=P)).then_inc(x_ld[q], 16)
                    load(sp, q, q)
                sp.dma_start(Wn[:, :, :], nsa_d).then_inc(c3, 16)
                sp.dma_start(ptab[:, :], ptab_d.rearrange("(o n) -> o n", o=1).to_broadcast([P, 2 * BS])).then_inc(c3, 16)
                sp.dma_start(pidx[:, :], pidx_d).then_inc(c3, 16)
                sp.dma_start(ident[:, :], ident_d).then_inc(c3, 16)
                sp.dma_start(w2[:, :, :], w2_d).then_inc(c3, 16)
                sp.dma_start(peT[:, :, :], peT_d).then_inc(c3, 16)
                sp.dma_start(W1[:, :, :], w1_d[0]).then_inc(w1_ld, 16)
                next_loads(sp, L_QKV, L_POOL - L_QKV)
                out_dma(sp, ktail_d, kwin_d[:, 4:256])
                out_dma(sp, vtail_d, vwin_d[:, 4:256])
                out_dma(sp, spool_d, state_d[:, 4:15])
                sp.wait_ge(gd, product(L_POOL - 1))
                sp.dma_start(xT[:, :, :], xT_d.rearrange("(k p) t -> p k t", p=P)).then_inc(x_again, 16)

            @block.gpsimd
            def _(g):
                g.wait_ge(ix, 3)
                gather_past(g, 0)

            @block.vector
            def _(v):
                for q in range(4):
                    x = xT[:, 4 * q:4 * q + 4, :]
                    v.wait_ge(x_hi, q + 1)
                    nc.vector.tensor_tensor(xHL[1][:, 4 * q:4 * q + 4, :], x, xHL[0][:, 4 * q:4 * q + 4, :].bitcast(F32),
                                            op=ALU.subtract).then_inc(x_lo, 1)
                    if q < 2:
                        lo_w(nc.vector, L_QKV, 0, q)
                page_rows(v)
                with v.Fori(0, (L_POOL - L_QKV) // SLOTS - 1) as i:
                    for j in range(SLOTS):
                        lo_w(nc.vector, L_QKV, i, j + 2)
                for j in range(2):
                    lo_w(nc.vector, L_POOL - SLOTS, 0, j + 2)

            @block.tensor
            def _(pe):
                with pe.Fori(0, (L_POOL - L_QKV) // SLOTS) as i:
                    for j in range(SLOTS):
                        def ready(k):
                            if j == 0 and k % 4 == 0:
                                pe.wait_ge(x_lo, k // 4 + 1)
                        gemm3(pe, L_QKV, i, j, *xHL, ready)

            @block.scalar
            def _(act):
                def out(i, j):
                    gemm_out(act, L_QKV, i, j)
                    nc.scalar.copy(PT[:, bass.ds(i * SLOTS + (Q0 + j), 1), :].rearrange("p a t -> p (a t)"),
                                   bank(L_QKV, j)).then_inc(ge, 1)

                act.sem_inc(ge, 2)
                for q in range(4):
                    act.wait_ge(x_ld[q], 16)
                    nc.scalar.copy(xHL[0][:, 4 * q:4 * q + 4, :], xT[:, 4 * q:4 * q + 4, :]).then_inc(x_hi, 1)
                    if q < 2:
                        hi_w(L_QKV, 0, q)
                with act.Fori(0, (L_POOL - L_QKV) // SLOTS - 1) as i:
                    for j in range(SLOTS):
                        out(i, j)
                        hi_w(L_QKV, i, j + 2)
                for j in range(SLOTS):
                    out((L_POOL - L_QKV) // SLOTS - 1, j)
                    if j < 2:
                        hi_w(L_POOL - SLOTS, 0, j + 2)
        parts.close()

        A1 = sb(cmps, "A1", [P, 512])
        A1p = sb(cmps, "A1p", [P, 64])
        peb = sb(cmps, "peb", [P, 2])
        PX = sb(cmps, "PX", [P, 16, 66])
        px = sem("px")
        HS = sb(cmps, "HS", [P, NKV, BS, NCMP])
        HP = sb(cmps, "HP", [P, NKV, NCMP])
        HG = sb(cmps, "HG", [P, NKV * BS * NCMP])
        HGp = sb(cmps, "HGp", [P, NKV * NCMP])
        cm = sem("cm")
        cr = sem("cr")
        ch = sem("ch")
        cg = sem("cg")
        ck = sem("ck")
        ce = sem("ce")
        with nc.Block() as block:
            @block.sync
            def _(sp):
                for n, c0 in ((0, KC0), (1, VC0), (3, VS0), (5, VW0)):
                    sp.dma_start(kvT_d[:, n], PT[:, c0:c0 + NKV, :]).then_inc(raw_out, 16)
                sp.wait_ge(cm, 1)
                sp.dma_start(W1[:, :, :], w1_d[1]).then_inc(w1_ld, 16)
                next_loads(sp, L_POOL, SLOTS)
                sp.wait_ge(sg_done, 1)
                sp.dma_start(gate_d, gateT[:, NP_TOK:T]).then_inc(sg_st, 16)
                sp.wait_ge(sg_done, 2)
                sp.dma_start(gatep_d.rearrange("c x p -> c (x p)"), gateq).then_inc(sg_st, 16)
                sp.wait_ge(sg_st, 32)

            @block.gpsimd
            def _(g):
                g.wait_ge(cm, 1)
                gather_past(g, 1)

            @block.tensor
            def _(pe):
                for kv in range(2):
                    pe.wait_ge(w1_ld, 16 * (kv + 1))
                    pe.wait_ge(ct_ld, 16 * 16 * (kv + 1))
                    if kv:
                        pe.wait_ge(ch, 4)
                        pe.wait_ge(cr, 4)
                        pe.wait_ge(sg_done, 1)
                    cv = CT[:, :, :].rearrange("p b (g c s) -> p (b g) c s", g=NKV, s=16)
                    pe.wait_ge(px, 2 * kv + 2)
                    for r in range(2):
                        for s in range(16):
                            w = W1[:, 16 * r + s, :]
                            nc.tensor.matmul(PS[:, r, :], w, cv[:, :, :, s], start=(s == 0), stop=(s == 15))
                            m = nc.tensor.matmul(PS[:, 2 + r, 0:66], w, PX[:, s, :], start=(s == 0), stop=(s == 15))
                    m.then_inc(cm, 1)
                    if kv == 0:
                        pe.wait_ge(x_again, 16)
                    for j in ((0, 1, 2), (3,))[kv]:
                        gemm(pe, L_POOL, 0, j, xT)
                    if kv == 0:
                        pe.wait_ge(ch, 4)
                        pe.wait_ge(cr, 4)
                        for k in range(DK):
                            m = nc.tensor.matmul(PS[0:3 * NH, 2, 0:T], Wn[:, k, :], xT[:, k, :],
                                                 start=(k == 0), stop=(k == DK - 1))
                        m.then_inc(g_done, 1)
                    pe.wait_ge(cg, 2 * (kv + 1))
                    if kv == 0:
                        nc.tensor.matmul(PS[:, 5, 0:480], w2[:, 0, :], HG[:, :], start=True, stop=True)
                        nc.tensor.matmul(PS[:, 4, 0:60], w2[:, 0, :], HGp[:, :], start=True, stop=True).then_inc(ck, 1)
                        pe.wait_ge(ce, 2)
                    else:
                        for g in range(NKV):
                            nc.tensor.matmul(PS[0:120, 5, g * P:(g + 1) * P], HG[:, g * 120:(g + 1) * 120], w2[:, 1, :],
                                             start=True, stop=True)
                            m = nc.tensor.matmul(PS[0:NCMP, 4, g * P:(g + 1) * P], HGp[:, g * NCMP:(g + 1) * NCMP],
                                                 w2[:, 1, :], start=True, stop=True)
                        m.then_inc(ck, 1)

            @block.scalar
            def _(act):
                for kv in range(2):
                    c0 = (KC0, VC0)[kv]
                    if kv:
                        act.wait_ge(cm, 1)
                    nc.scalar.copy(PX[:, :, 0:64].rearrange("p s (g c) -> p g c s", g=NKV),
                                   PT[:, c0:c0 + NKV, 0:NP_TOK].rearrange("p g (c s) -> p g c s", s=16)).then_inc(px, 1)
                    nc.scalar.copy(PX[:, :, 64:66], peT[:, kv, :].rearrange("p (r s) -> p s r", r=2)).then_inc(px, 1)
                    act.wait_ge(cm, kv + 1)
                    if kv:
                        act.wait_ge(ch, 4)
                    nc.scalar.copy(A1[:, :], PS[:, 1, :]).then_inc(cr, 1)
                    nc.scalar.copy(A1p[:, :], PS[:, 3, 0:64]).then_inc(cr, 1)
                    nc.scalar.copy(peb[:, 0:1], PS[:, 3, 65:66]).then_inc(cr, 1)
                    act.wait_ge(cr, 4 * kv + 3)
                    nc.scalar.activation(peb[:, 1:2], PS[:, 2, 64:65], ACT.Identity, bias=peb[:, 0:1]).then_inc(cr, 1)
                    act.wait_ge(cr, 4 * kv + 4)
                    act.wait_ge(ch, 4 * (kv + 1))
                    if kv:
                        act.wait_ge(ck, 1)
                    nc.scalar.activation(HG[:, :], HS[:, :, :, :].rearrange("p g b n -> p (g b n)"), ACT.Gelu,
                                         bias=peb[:, 1:2]).then_inc(cg, 1)
                    nc.scalar.activation(HGp[:, :], HP[:, :, :].rearrange("p g n -> p (g n)"), ACT.Gelu,
                                         bias=peb[:, 1:2]).then_inc(cg, 1)
                    for j in ((0, 1, 2), (3,))[kv]:
                        gemm_out(act, L_POOL, 0, j)
                        nc.scalar.copy(PT[:, j, :], bank(L_POOL, j)).then_inc(ge, 1)
                    if kv == 0:
                        act.wait_ge(g_done, 1)
                        nc.scalar.activation(gateT, PS[0:3 * NH, 2, 0:T], ACT.Sigmoid).then_inc(sg_done, 1)
                        act.wait_ge(sg_done, 1)
                        nc.scalar.copy(gateq.rearrange("c (x p) -> c x p", p=4),
                                       gateT[:, NP_TOK:T].rearrange("c (p x) -> c x p", p=4)).then_inc(sg_done, 1)
                    act.wait_ge(ck, kv + 1)
                    if kv == 0:
                        nc.scalar.copy(kcb[:, :], PS[:, 5, 0:480]).then_inc(ce, 1)
                        nc.scalar.copy(kcbp[:, :], PS[:, 4, 0:60]).then_inc(ce, 1)
                    else:
                        nc.scalar.copy(vcb[:, :, :], PS[0:120, 5, :].rearrange("p (g d) -> p g d", g=NKV)).then_inc(ce, 1)
                        nc.scalar.copy(vcbp[:, :, :], PS[0:NCMP, 4, :].rearrange("p (g d) -> p g d", g=NKV)).then_inc(ce, 1)

            @block.vector
            def _(v):
                a0 = PS[:, 0, :].rearrange("p (b q g c) -> p q g b c", b=BS, q=2, g=NKV)
                a1 = A1[:, :].rearrange("p (b q g c) -> p q g b c", b=BS, q=2, g=NKV)
                a0p = PS[:, 2, 0:64].rearrange("p (g c) -> p g c", g=NKV)
                a1p = A1p[:, :].rearrange("p (g c) -> p g c", g=NKV)
                for kv in range(2):
                    v.wait_ge(cr, 4 * (kv + 1))
                    if kv:
                        v.wait_ge(cg, 2)
                    nc.vector.tensor_tensor(HS[:, :, :, 0:7], a0[:, 0, :, :, 0:7], a1[:, 0, :, :, 1:8], op=ALU.add).then_inc(ch, 1)
                    nc.vector.tensor_tensor(HS[:, :, :, 7:8], a0[:, 0, :, :, 7:8], a1[:, 1, :, :, 0:1], op=ALU.add).then_inc(ch, 1)
                    nc.vector.tensor_tensor(HS[:, :, :, 8:15], a0[:, 1, :, :, 0:7], a1[:, 1, :, :, 1:8], op=ALU.add).then_inc(ch, 1)
                    nc.vector.tensor_tensor(HP[:, :, :], a0p[:, :, 0:15], a1p[:, :, 1:16], op=ALU.add).then_inc(ch, 1)
        cmps.close()

        VR = sb(mid, "VR", [P, 3, 2, NKV * HD])
        PcT = sb(mid, "PcT", [P, NH, NP_TOK])[0:NCMP, :, :]
        PcS = sb(mid, "PcS", [BS * NCMP, NKV, P])
        grow = sb(mid, "grow", [P, TT, 3 * NH])
        gs = sb(mid, "gs", [P, 3, 4])
        scope = ExitStack()
        maskc = sb(scope, "maskc", [P, 2, 480])
        keepc = sb(scope, "keepc", [P, 2, 480])
        E = sb(scope, "E", [P, 2, 480])
        mx = sb(scope, "mx", [P, 2, 32])
        gc = sb(scope, "gc", [P, NKV])
        qS = sb(scope, "qS", [P, NH, NS_TOK])
        rot = sb(scope, "rot", [P, P])
        cs = sb(scope, "cs", [P, 2, T])
        rt = sb(scope, "rt", [P, 4, T])
        rt2 = [sb(scope, f"rt2_{i}", [P, 4, T]) for i in range(2)]
        rq = sem("rq")
        rc = sem("rc")
        rd = sem("rd")
        vt = sem("vt")
        vc = sem("vc")
        c4 = sem("c4")
        c4g = sem("c4g")
        gt = sem("gt")
        s4 = sem("s4")
        d4 = sem("d4")
        e4 = sem("e4")
        t4 = sem("t4")
        k4 = sem("k4")
        k5 = sem("k5")
        QUADS = (KS0, KW0, Q0, Q0 + 4, Q0 + 8, Q0 + 12)
        with nc.Block() as block:
            @block.sync
            def _(sp):
                sp.dma_start(maskc[:, :, :], maskc_d).then_inc(c4, 16)
                sp.dma_start(keepc[:, :, :], keepc_d).then_inc(c4, 16)
                sp.dma_start(rot[:, :], rot_d).then_inc(c4, 16)
                sp.dma_start(cs[:, :, :], cs_d).then_inc(c4, 16)
                sp.dma_start(gc[:, :], gate_d[0:NH].rearrange("(g j) t -> (j t) g", g=NKV),
                             allow_slow_non_contiguous=True).then_inc(c4g, 16)
                sp.dma_start(gs[:, :, :], gatep_d.rearrange("(r h) x p -> (h x) r p", r=3)).then_inc(c4g, 16)
                next_loads(sp, L_POOL + SLOTS, SLOTS)
                sp.wait_ge(rd, 2 * 2)
                for n, c0 in ((2, KS0), (4, KW0)):
                    out_dma(sp, kvT_d[:, n], PT[:, c0:c0 + NKV, :])
                sp.wait_ge(c4g, 32)

            @block.gpsimd
            def _(g):
                cos = cs[:, 0:1, :].to_broadcast([P, 4, T])
                g.wait_ge(c4, 64)
                for n in range(6):
                    if n >= 2:
                        g.wait_ge(rd, 2 * n - 2)
                    nc.gpsimd.tensor_tensor(rt2[n % 2][:, :, :], PT[:, QUADS[n]:QUADS[n] + 4, :], cos,
                                            op=ALU.mult).then_inc(rc, 1)

            @block.tensor
            def _(pe):
                for t in range(TT):
                    m = nc.tensor.transpose(PS[:, 2, t * 48:t * 48 + 48], gateT[:, t * P:(t + 1) * P], ident[0:48, 0:48])
                m.then_inc(gt, 1)
                for h in range(NH):
                    for t in range(TT):
                        m = nc.tensor.matmul(PS[:, 0, (2 * h + t) * NCMP:(2 * h + t + 1) * NCMP],
                                             PT[:, Q0 + h, t * P:(t + 1) * P],
                                             kcbp[:, (h // HPG) * NCMP:(h // HPG + 1) * NCMP], start=True, stop=True)
                m.then_inc(s4, 1)
                pe.wait_ge(d4, 1)
                for g in range(NKV):
                    m = nc.tensor.matmul(PS[:, 1, g * 120:(g + 1) * 120],
                                         qS[:, 4 * g:4 * g + 4, :].rearrange("p h t -> p (h t)"),
                                         kcb[:, g * 120:(g + 1) * 120], start=True, stop=True)
                m.then_inc(s4, 1)

                def swap(n):
                    if n > 0:
                        pe.wait_ge(rd, 2 * n - 1)
                    for j in range(4):
                        m = nc.tensor.matmul(PS[:, 2 + j, 0:T], rot[:, :], PT[:, QUADS[n] + j, :], start=True, stop=True)
                    m.then_inc(rq, 1)

                gemm(pe, L_POOL + SLOTS, 0, 0, xT)
                pe.wait_ge(d4, 10)
                for n in range(8):
                    if n >= 2:
                        pe.wait_ge(k4, n - 1)
                    for j in range(4):
                        h, t = 2 * n + j // 2, j % 2
                        m = nc.tensor.transpose(PS[0:NCMP, 4 + n % 2, j * P:(j + 1) * P],
                                                E[:, 0, (2 * h + t) * NCMP:(2 * h + t + 1) * NCMP], ident[:, :])
                    m.then_inc(t4, 1)
                pe.wait_ge(d4, 11)
                for n in range(6):
                    t, v = n // 2, n % 2
                    w = P if t < TT else NS_TOK
                    c0 = (VS0, VW0)[v]
                    if n >= 2:
                        pe.wait_ge(vc, n - 1)
                    for j in range(NKV):
                        m = nc.tensor.transpose(PS[0:w, n % 2, j * P:(j + 1) * P],
                                                PT[:, c0 + j, t * P:t * P + w], ident[:, :])
                    m.then_inc(vt, 1)
                pe.wait_ge(d4, 19)
                pe.wait_ge(vc, 6)
                for g in range(NKV):
                    m = nc.tensor.transpose(PS[0:120, 0, g * P:(g + 1) * P], E[:, 1, g * 120:(g + 1) * 120], ident[:, :])
                m.then_inc(t4, 1)
                pe.wait_ge(c4, 64)
                pe.wait_ge(k4, 8)
                for n in range(6):
                    swap(n)
                    if n < 3:
                        gemm(pe, L_POOL + SLOTS, 0, n + 1, xT)

            @block.scalar
            def _(act):
                act.wait_ge(gt, 1)
                nc.scalar.copy(grow[:, :, :], PS[:, 2, 0:96].rearrange("p (t c) -> p t c", t=TT)).then_inc(e4, 1)
                for u in range(2):
                    act.wait_ge(d4, 1 + 9 * u + 3)
                    nc.scalar.activation(E[:, u, :], E[:, u, :], ACT.Exp).then_inc(e4, 1)
                    if u == 0:
                        gemm_out(act, L_POOL + SLOTS, 0, 0)
                        nc.scalar.copy(PT[:, SLOTS, :], bank(L_POOL + SLOTS, 0)).then_inc(ge, 1)
                for n in range(8):
                    act.wait_ge(t4, n + 1)
                    nc.scalar.copy(PcT[:, 2 * n:2 * n + 2, :], PS[0:NCMP, 4 + n % 2, :].rearrange(
                        "p (h t) -> p h t", h=2)).then_inc(k4, 1)
                for n in range(6):
                    t, v = n // 2, n % 2
                    w = P if t < TT else NS_TOK
                    act.wait_ge(vt, n + 1)
                    nc.scalar.copy(VR[0:w, t, v, :], PS[0:w, n % 2, :]).then_inc(vc, 1)
                act.wait_ge(t4, 9)
                nc.scalar.copy(PcS[:, :, :], PS[0:120, 0, :].rearrange("p (g t) -> p g t", g=NKV)).then_inc(k4, 1)
                for j in range(1, SLOTS):
                    gemm_out(act, L_POOL + SLOTS, 0, j)
                    nc.scalar.copy(PT[:, SLOTS + j, :], bank(L_POOL + SLOTS, j)).then_inc(ge, 1)

            @block.vector
            def _(v):
                n = [0]

                def link(ins):
                    n[0] += 1
                    ins.then_inc(d4, 1)
                    v.wait_ge(d4, n[0])

                link(nc.vector.tensor_copy(qS[:, :, :], PT[:, Q0:Q0 + NH, NP_TOK:T]))
                v.wait_ge(c4, 64)
                for u in range(2):
                    A, B = (32, NCMP) if u == 0 else (4, 120)
                    e = E[:, u, :].rearrange("p (a b) -> p a b", a=A)
                    m = mx[:, 0, 0:A]
                    r = mx[:, 1, 0:A]
                    v.wait_ge(s4, u + 1)
                    link(nc.vector.scalar_tensor_tensor(out=E[:, u, :], in0=PS[:, u, 0:480], scalar=SCALE, in1=maskc[:, u, :],
                                                        op0=ALU.mult, op1=ALU.add))
                    link(nc.vector.tensor_reduce(m, e, AX, ALU.max))
                    link(nc.vector.tensor_tensor(e, e, m.unsqueeze(2).to_broadcast([P, A, B]), op=ALU.subtract))
                    v.wait_ge(e4, 2 + u)
                    link(nc.vector.tensor_tensor(E[:, u, :], E[:, u, :], keepc[:, u, :], op=ALU.mult))
                    link(nc.vector.tensor_reduce(r, e, AX, ALU.add))
                    link(nc.vector.tensor_scalar(r, r, 0.5, None, op0=ALU.max))
                    link(nc.vector.reciprocal(r, r))
                    if u == 0:
                        for t in range(TT):
                            ins = nc.vector.tensor_tensor(r.rearrange("p (h t) -> p h t", t=TT)[:, :, t],
                                                          r.rearrange("p (h t) -> p h t", t=TT)[:, :, t],
                                                          grow[:, t, 0:NH], op=ALU.mult)
                            if t == 0:
                                ins.then_inc(k5, 1)
                        link(ins)
                        v.wait_ge(k5, 1)
                    else:
                        v.wait_ge(c4g, 32)
                        link(nc.vector.tensor_tensor(r, r, gc[:, :], op=ALU.mult))
                    link(nc.vector.tensor_tensor(e, e, r.unsqueeze(2).to_broadcast([P, A, B]), op=ALU.mult))
                sin = cs[:, 1:2, :].to_broadcast([P, 4, T])
                v.wait_ge(c4, 64)
                for n in range(6):
                    x = PT[:, QUADS[n]:QUADS[n] + 4, :]
                    v.wait_ge(rq, n + 1)
                    if n > 0:
                        v.wait_ge(rd, 2 * n)
                    nc.vector.tensor_tensor(rt[:, :, :], PS[:, 2:6, 0:T], sin, op=ALU.mult).then_inc(rd, 1)
                    v.wait_ge(rd, 2 * n + 1)
                    v.wait_ge(rc, n + 1)
                    nc.vector.tensor_tensor(x, rt[:, :, :], rt2[n % 2][:, :, :], op=ALU.add).then_inc(rd, 1)
        scope.close()

        NKS = NP_TOK + NS_TOK
        scope = ExitStack()
        KT = [sb(scope, f"KT{i}", [P, 2, 2, NKV * P]) for i in range(2)]
        V = [sb(scope, f"V{i}", [P, 2, 2, NKV * HD]) for i in range(2)]
        maskn = sb(scope, "maskn", [P, BS, NS_TOK])
        qcur = sb(scope, "qcur", [P, NH, 8])
        stg = sb(scope, "stg", [P, 4], I32)
        Pr = [sb(scope, f"Pr{i}", [P, NKS]) for i in range(2)]
        PTr = [sb(scope, f"PTr{i}", [P, 3, P]) for i in range(2)]
        st5 = sb(scope, "st5", [P, 2, 4])
        c5 = sem("c5")
        kv_ld = [sem(f"kv_ld{i}") for i in range(2)]
        kw_ld = [sem(f"kw_ld{i}") for i in range(2)]
        kv_fr = [sem(f"kv_fr{i}") for i in range(2)]
        stg_ok = sem("stg_ok")
        gathers = sem("gathers")
        q_ok = sem("q_ok")
        q_fr = sem("q_fr")
        s5 = sem("s5")
        a5 = sem("a5")
        e5 = sem("e5")
        b5 = sem("b5")
        t5 = sem("t5")
        k5b = sem("k5b")
        v5 = sem("v5")
        o5 = sem("o5")
        d5 = sem("d5")
        d5a = sem("d5a")
        cmp_o = sem("cmp_o")
        cmp_c = sem("cmp_c")

        def done(i, per, u):
            return i * per + (u + 3)

        def free(i, per, u):
            return i * per + (u + 1)

        with nc.Block() as block:
            @block.sync
            def _(sp):
                sp.dma_start(maskn[:, :, :], maskn_d).then_inc(c5, 16)
                sp.dma_start(poolT_d, PT[:, 0:POOL_CH, NP_TOK - POOL_ST:T]).then_inc(pool_out, 16)
                with sp.Fori(0, BS // 2) as i:
                    for b in range(2):
                        sp.wait_ge(kv_fr[b], i + 1)
                        sp.dma_start(KT[b][:, 1, :, :].rearrange("p a n -> p (a n)"),
                                     kwT_d[bass.ds(2 * i + b, 1)].rearrange("o p n -> p (o n)")).then_inc(kw_ld[b], 16)
                        sp.dma_start(V[b][:, 1, :, :].rearrange("p a n -> p (a n)"),
                                     vw_d[bass.ds(2 * i + b, 1)].rearrange("o p n -> p (o n)")).then_inc(kw_ld[b], 16)
                    for s in range(SLOTS):
                        sp.wait_ge(gd, i * SLOTS + product(L_GP + s))
                        load(sp, i * SLOTS + (L_GP + SLOTS + s), s)

            @block.gpsimd
            def _(g):
                with g.Fori(0, BS // 2) as i:
                    g.wait_ge(kv_fr[0], i + 1)
                    g.sem_inc(gathers, 1)
                    nc.gpsimd.tensor_copy(stg[:, :], pgi[:, bass.ds(i * 4, 4)]).then_inc(stg_ok, 1)
                    g.wait_ge(stg_ok, 1)
                    g.sem_clear(stg_ok)
                    for b in range(2):
                        if b:
                            g.wait_ge(kv_fr[1], i + 1)
                            g.sem_inc(gathers, 1)
                        for pg in range(2):
                            for dst, src in ((KT[b], ksT_d), (V[b], vs_d)):
                                nc.gpsimd.indirect_dma_start(
                                    out=dst[:, 0, pg, :], out_offset=None, in_=src,
                                    in_offset=bass.IndirectOffsetOnAxis(ap=stg[:, 2 * b + pg:2 * b + pg + 1], axis=0)
                                ).then_inc(kv_ld[b], 16)

            @block.tensor
            def _(pe):
                for g in range(NKV):
                    m = nc.tensor.matmul(PS[:, 4, g * P:(g + 1) * P], vcb[:, g, :], PcS[:, g, :], start=True, stop=True)
                m.then_inc(cmp_o, 1)
                pe.sem_inc(kv_fr[0], 1)
                pe.sem_inc(kv_fr[1], 1)
                pe.sem_inc(q_fr, 1)
                for x in (s5, t5, v5):
                    pe.sem_inc(x, 2)
                pe.wait_ge(cmp_c, 1)
                with pe.Fori(0, BS // 2) as i:
                    gemm(pe, L_GP, i, 0, xT)
                    for step in range(6):
                        if step < 4:
                            u = step
                            b, br = u // 2, u % 2
                            if u == 0:
                                pe.wait_ge(q_ok, i + 1)
                            if br == 0:
                                pe.wait_ge(kv_ld[b], i * 64 + 64)
                                pe.wait_ge(kw_ld[b], i * 32 + 32)
                            pe.wait_ge(a5, free(i, 4, u))
                            for g in range(NKV):
                                nc.tensor.matmul(PS[32 * g:32 * g + 32, u % 2, 0:NP_TOK],
                                                 qcur[:, 4 * g:4 * g + 4, :].rearrange("p h x -> p (h x)"),
                                                 KT[b][:, br, :, g * P:(g + 1) * P], start=True, stop=True,
                                                 tile_position=(0, 32 * g))
                                m = nc.tensor.matmul(PS[32 * g:32 * g + 32, u % 2, NP_TOK:NKS],
                                                     qcur[:, 4 * g:4 * g + 4, :].rearrange("p h x -> p (h x)"),
                                                     PT[:, (KS0, KW0)[br] + g, NP_TOK:T], start=True, stop=True,
                                                     tile_position=(0, 32 * g))
                            m.then_inc(s5, 1)
                        gemm(pe, L_GP, i, 1 + step // 2, xT, HALVES[step % 2])
                        if 1 <= step <= 4:
                            u = step - 1
                            pe.wait_ge(b5, done(i, 4, u))
                            pe.wait_ge(k5b, free(i, 4, u))
                            for kb in range(3):
                                w = P if kb < 2 else NS_TOK
                                m = nc.tensor.transpose(PS[0:w, 2 + u % 2, kb * P:(kb + 1) * P],
                                                        Pr[u % 2][:, kb * P:kb * P + w], ident[:, :])
                            m.then_inc(t5, 1)
                        if step >= 2:
                            u = step - 2
                            b, br = u // 2, u % 2
                            pe.wait_ge(k5b, done(i, 4, u))
                            if br == 0:
                                pe.wait_ge(o5, i * 2 + b + 1)
                            for g in range(NKV):
                                for kb in range(3):
                                    w = P if kb < 2 else NS_TOK
                                    lhs = V[b][:, br, kb, g * P:(g + 1) * P] if kb < 2 else VR[0:w, 2, br, g * P:(g + 1) * P]
                                    rhs = PTr[u % 2][0:w, kb, :].rearrange("k (h x) -> k h x", x=8)[
                                        :, 4 * g:4 * g + 4, 4 * b:4 * b + 4]
                                    m = nc.tensor.matmul(PS[:, 4 + b, g * 16:(g + 1) * 16], lhs, rhs,
                                                         start=(br == 0 and kb == 0 and g == 0),
                                                         stop=(br == 1 and kb == 2), skip_group_check=True)
                            m.then_inc(v5, 1)
                            if br == 1:
                                pe.wait_ge(v5, done(i, 4, u))
                                pe.sem_inc(kv_fr[b], 1)
                                if b:
                                    pe.sem_inc(q_fr, 1)

            @block.scalar
            def _(act):
                act.wait_ge(cmp_o, 1)
                nc.scalar.copy(attnT[:, :, NP_TOK:T], PS[:, 4, :].rearrange("p (h t) -> p h t", h=NH)).then_inc(cmp_c, 1)
                for x in (e5, k5b):
                    act.sem_inc(x, 2)
                act.wait_ge(raw_out, 64)
                def gate(i, n):
                    gemm_out(act, L_GP, i, n)
                    nc.scalar.copy(gatesP[:, bass.ds(i * SLOTS + n, 1), :].rearrange("p a t -> p (a t)"),
                                   bank(L_GP, n)).then_inc(ge, 1)

                with act.Fori(0, BS // 2) as i:
                    for step in range(5):
                        if step % 2 == 0:
                            gate(i, step // 2)
                        if step < 4:
                            u = step
                            act.wait_ge(a5, done(i, 4, u))
                            nc.scalar.activation(Pr[u % 2][:, :], Pr[u % 2][:, :], ACT.Exp, bias=st5[:, u % 2, 0:1],
                                                 accum_out=st5[:, u % 2, 1:2]).then_inc(e5, 1)
                        if step >= 1:
                            u = step - 1
                            act.wait_ge(t5, done(i, 4, u))
                            act.wait_ge(v5, free(i, 4, u))
                            nc.scalar.copy(PTr[u % 2][:, 0:2, :], PS[:, 2 + u % 2, 0:256].rearrange(
                                "p (k r) -> p k r", k=2)).then_inc(d5a, 1)
                            nc.scalar.copy(PTr[u % 2][0:NS_TOK, 2, :], PS[0:NS_TOK, 2 + u % 2, 256:384]).then_inc(d5a, 1)
                            act.wait_ge(d5a, 2 * step)
                            act.sem_inc(k5b, 1)
                    gate(i, 3)
                    act.sem_clear(d5a)

            @block.vector
            def _(v):
                for x in (a5, b5, o5):
                    v.sem_inc(x, 2)
                v.wait_ge(c5, 16)
                v.wait_ge(cmp_c, 1)
                with v.Fori(0, BS // 2) as i:
                    n = [0]

                    def link(ins):
                        n[0] += 1
                        ins.then_inc(d5, 1)
                        v.wait_ge(d5, n[0])

                    v.wait_ge(q_fr, i + 1)
                    nc.vector.tensor_copy(qcur[:, :, :], PT[:, Q0:Q0 + NH, bass.ds(i * 8 + NP_TOK, 8)]).then_inc(q_ok, 1)
                    for step in range(5):
                        if step < 4:
                            u = step
                            b = u // 2
                            v.wait_ge(s5, done(i, 4, u))
                            v.wait_ge(t5, free(i, 4, u))
                            link(nc.vector.tensor_scalar(Pr[u % 2][:, 0:NP_TOK], PS[:, u % 2, 0:NP_TOK], SCALE, None,
                                                         op0=ALU.mult))
                            link(nc.vector.scalar_tensor_tensor(
                                out=Pr[u % 2][:, NP_TOK:NKS], in0=PS[:, u % 2, NP_TOK:NKS], scalar=SCALE,
                                in1=maskn[:, bass.ds(i * 2 + b, 1), :].rearrange("p o k -> p (o k)"),
                                op0=ALU.mult, op1=ALU.add))
                            link(nc.vector.tensor_reduce(st5[:, u % 2, 0:1], Pr[u % 2][:, :], AX, ALU.max))
                            link(nc.vector.tensor_scalar(st5[:, u % 2, 0:1], st5[:, u % 2, 0:1], -1.0, None, op0=ALU.mult))
                            v.sem_inc(a5, 1)
                        if step >= 1:
                            u = step - 1
                            br = u % 2
                            v.wait_ge(e5, done(i, 4, u))
                            link(nc.vector.reciprocal(st5[:, u % 2, 2:3], st5[:, u % 2, 1:2]))
                            link(nc.vector.tensor_tensor(st5[:, u % 2, 3:4], st5[:, u % 2, 2:3],
                                                         gs[:, 1 + br, bass.ds(i, 1)], op=ALU.mult))
                            link(nc.vector.tensor_scalar(Pr[u % 2][:, :], Pr[u % 2][:, :], st5[:, u % 2, 3:4], None,
                                                         op0=ALU.mult))
                            v.sem_inc(b5, 1)
                    for b in range(2):
                        v.wait_ge(v5, done(i, 4, 2 * b + 1))
                        dst = attnT[:, :, bass.ds(i * 8 + (NP_TOK + 4 * b), 4)]
                        link(nc.vector.tensor_tensor(dst, dst, PS[:, 4 + b, 0:64].rearrange("p (h l) -> p h l", l=4),
                                                     op=ALU.add))
                        v.sem_inc(o5, 1)
                    v.sem_clear(d5)
        scope.close()

        NKP = 384
        gas = ExitStack()
        gatesA = sb(gas, "gatesA", [P, DK, T])
        scope = ExitStack()
        past = sb(scope, "past", [P, POOL_CH, BS * POOL_ST])
        EP = [sb(scope, f"EP{i}", [P, POOL_ST + NP_TOK]) for i in range(2)]
        ES = [sb(scope, f"ES{i}", [P, BS, POOL_ST + LS]) for i in range(2)]
        rcnt = sb(scope, "rcnt", [P, 4, 16])
        pst = sem("pst")
        pl = sem("pl")
        QR = sb(scope, "QR", [P, HPG, NP_TOK])
        VG = sb(scope, "VG", [P, TT, 2, HD])
        VCG = sb(scope, "VCG", [NCMP, HD])
        maskp = sb(scope, "maskp", [P, NKP])
        Pp = [sb(scope, f"Pp{i}", [P, NKP]) for i in range(2)]
        PTp = [sb(scope, f"PTp{i}", [P, NKP]) for i in range(2)]
        st6 = sb(scope, "st6", [P, 2, 4, TT])
        c6 = sem("c6")
        stg6 = sem("stg6")
        s6, a6, e6, b6, t6, k6, v6, o6 = [sem(f"{x}6_") for x in "saebtkvo"]
        d6, d6a = sem("d6"), sem("d6a")
        SEG = ((0, P), (P, NKP))
        with nc.Block() as block:
            @block.sync
            def _(sp):
                sp.dma_start(maskp[:, :], maskp_d).then_inc(c6, 16)
                sp.dma_start(past[:, :, :], stateT_d.rearrange("(c p) n -> p c n", p=P)).then_inc(pst, 16)
                sp.dma_start(rcnt[:, :, :], rcnt_d).then_inc(pst, 16)
                next_loads(sp, L_GA, L_BP - L_GA)

            @block.gpsimd
            def _(g):
                n = [0]

                def link(ins):
                    n[0] += 1
                    ins.then_inc(pl, 1)
                    g.wait_ge(pl, n[0])

                def mean_minus_input(c):
                    w = 2 ** (c // 2 + 1)
                    (a, b), (sa, sbf) = EP, ES
                    ud = PT[:, c, NP_TOK:T].rearrange("p (b l) -> p b l", l=LS)
                    link(nc.gpsimd.memset(a[:, 0:POOL_ST], 0.0))
                    link(nc.gpsimd.tensor_copy(a[:, POOL_ST:], PT[:, c, 0:NP_TOK]))
                    link(nc.gpsimd.tensor_copy(sa[:, :, 0:POOL_ST], past[:, c, :].rearrange("p (b s) -> p b s", s=POOL_ST)))
                    link(nc.gpsimd.tensor_copy(sa[:, :, POOL_ST:], ud))
                    LP, LSx = POOL_ST + NP_TOK, POOL_ST + LS
                    sh = 1
                    while sh < w:
                        lo = 2 * sh - 1
                        link(nc.gpsimd.tensor_tensor(b[:, lo:LP], a[:, lo:LP], a[:, lo - sh:LP - sh], op=ALU.add))
                        link(nc.gpsimd.tensor_tensor(sbf[:, :, lo:LSx], sa[:, :, lo:LSx], sa[:, :, lo - sh:LSx - sh],
                                                     op=ALU.add))
                        a, b, sa, sbf = b, a, sbf, sa
                        sh *= 2
                    link(nc.gpsimd.tensor_tensor(a[:, POOL_ST:POOL_ST + 16], a[:, POOL_ST:POOL_ST + 16],
                                                 rcnt[:, c // 2, :], op=ALU.mult))
                    link(nc.gpsimd.tensor_scalar(b[:, POOL_ST:], a[:, POOL_ST:], 1.0 / w, None, op0=ALU.mult))
                    link(nc.gpsimd.tensor_tensor(PT[:, c, 0:NP_TOK], b[:, POOL_ST:], PT[:, c, 0:NP_TOK], op=ALU.subtract))
                    link(nc.gpsimd.tensor_scalar(sbf[:, :, POOL_ST:], sa[:, :, POOL_ST:], 1.0 / w, None, op0=ALU.mult))
                    link(nc.gpsimd.tensor_tensor(ud, sbf[:, :, POOL_ST:], ud, op=ALU.subtract))

                for g0 in range(NKV):
                    if g0:
                        g.wait_ge(v6, g0 * 8 + 2)
                    nc.gpsimd.tensor_copy(QR[:, :, :], PT[:, Q0 + g0 * HPG:Q0 + (g0 + 1) * HPG, 0:NP_TOK]).then_inc(stg6, 1)
                    for t in range(TT):
                        nc.gpsimd.tensor_copy(VG[:, t, :, :], VR[:, t, :, g0 * HD:(g0 + 1) * HD]).then_inc(stg6, 1)
                    nc.gpsimd.tensor_copy(VCG[:, :], vcbp[:, g0, :]).then_inc(stg6, 1)
                    if g0 == 0:
                        g.wait_ge(pst, 32)
                        g.wait_ge(pool_out, 16)
                    for c in (2 * g0, 2 * g0 + 1):
                        mean_minus_input(c)

            @block.tensor
            def _(pe):
                for x in (s6, t6, v6):
                    pe.sem_inc(x, 2)
                with pe.Fori(0, NKV) as i:
                    gemm(pe, L_GA, i, 0, xT)
                    pe.wait_ge(stg6, i * 4 + 4)
                    for step in range(10):
                        if step < 8:
                            u = step
                            j, br = u // 2, u % 2
                            key = PT[:, bass.ds(i + (KS0, KW0)[br], 1), :].rearrange("p o t -> p (o t)")
                            pe.wait_ge(a6, free(i, 8, u))
                            nc.tensor.matmul(PS[:, u % 2, 0:P], QR[:, j, 0:P], key[:, 0:P], start=True, stop=True)
                            nc.tensor.matmul(PS[:, u % 2, P:NKP], QR[:, j, P:NP_TOK], key[:, 0:NP_TOK],
                                             start=True, stop=True).then_inc(s6, 1)
                            gemm(pe, L_GA, i, 1 + u // 4, xT, QUARTERS[u % 4])
                        else:
                            gemm(pe, L_GA, i, 3, xT, HALVES[step - 8])
                        if 1 <= step <= 8:
                            u = step - 1
                            pe.wait_ge(b6, done(i, 8, u))
                            pe.wait_ge(k6, free(i, 8, u))
                            for kb in range(3):
                                m = nc.tensor.transpose(PS[:, 2 + u % 2, kb * P:(kb + 1) * P],
                                                        Pp[u % 2][:, kb * P:(kb + 1) * P], ident[:, :])
                            m.then_inc(t6, 1)
                        if step >= 2:
                            u = step - 2
                            j, br = u // 2, u % 2
                            o = PS[:, 4 + j % 2, 0:NP_TOK]
                            pe.wait_ge(k6, done(i, 8, u))
                            if br == 0:
                                pe.wait_ge(o6, free(i, 4, j))
                                nc.tensor.matmul(o, VCG[:, :],
                                                 PcT[:, bass.ds(i * HPG + j, 1), :].rearrange("p o t -> p (o t)"),
                                                 start=True, stop=False, skip_group_check=True)
                            nc.tensor.matmul(o, VG[:, 0, br, :], PTp[u % 2][:, 0:NP_TOK], start=False, stop=False,
                                             skip_group_check=True)
                            nc.tensor.matmul(o[:, P:NP_TOK], VG[:, 1, br, :], PTp[u % 2][:, NP_TOK:NKP],
                                             start=False, stop=(br == 1), skip_group_check=True).then_inc(v6, 1)

            @block.scalar
            def _(act):
                for x in (e6, k6):
                    act.sem_inc(x, 2)
                def gate(i, n):
                    gemm_out(act, L_GA, i, n)
                    nc.scalar.copy(gatesA[:, bass.ds(i * SLOTS + n, 1), :].rearrange("p a t -> p (a t)"),
                                   bank(L_GA, n)).then_inc(ge, 1)

                with act.Fori(0, NKV) as i:
                    for step in range(9):
                        if step % 4 == 0:
                            gate(i, step // 4)
                        if step < 8:
                            u = step
                            act.wait_ge(a6, done(i, 8, u))
                            for t, (a, b) in enumerate(SEG):
                                m = nc.scalar.activation(Pp[u % 2][:, a:b], Pp[u % 2][:, a:b], ACT.Exp,
                                                         bias=st6[:, u % 2, 0, t:t + 1], accum_out=st6[:, u % 2, 1, t:t + 1])
                                m.then_inc(d6a, 1)
                            act.wait_ge(d6a, 2 * u + 2)
                            act.sem_inc(e6, 1)
                        if step >= 1:
                            u = step - 1
                            act.wait_ge(t6, done(i, 8, u))
                            act.wait_ge(v6, free(i, 8, u))
                            nc.scalar.copy(PTp[u % 2][:, :], PS[:, 2 + u % 2, 0:NKP]).then_inc(k6, 1)
                    gate(i, 3)
                    act.sem_clear(d6a)

            @block.vector
            def _(v):
                for x in (a6, b6, o6):
                    v.sem_inc(x, 2)
                v.wait_ge(c6, 16)
                with v.Fori(0, NKV) as i:
                    n = [0]

                    def link(ins):
                        n[0] += 1
                        ins.then_inc(d6, 1)
                        v.wait_ge(d6, n[0])

                    for step in range(10):
                        if step < 8:
                            u = step
                            v.wait_ge(s6, done(i, 8, u))
                            v.wait_ge(t6, free(i, 8, u))
                            link(nc.vector.scalar_tensor_tensor(out=Pp[u % 2][:, :], in0=PS[:, u % 2, 0:NKP], scalar=SCALE,
                                                                in1=maskp[:, :], op0=ALU.mult, op1=ALU.add))
                            for t, (a, b) in enumerate(SEG):
                                link(nc.vector.tensor_reduce(st6[:, u % 2, 0, t:t + 1], Pp[u % 2][:, a:b], AX, ALU.max))
                            link(nc.vector.tensor_scalar(st6[:, u % 2, 0, :], st6[:, u % 2, 0, :], -1.0, None, op0=ALU.mult))
                            v.sem_inc(a6, 1)
                        if 1 <= step <= 8:
                            u = step - 1
                            j, br = u // 2, u % 2
                            v.wait_ge(e6, done(i, 8, u))
                            link(nc.vector.reciprocal(st6[:, u % 2, 2, :], st6[:, u % 2, 1, :]))
                            link(nc.vector.tensor_tensor(st6[:, u % 2, 3, :], st6[:, u % 2, 2, :],
                                                         grow[:, :, bass.ds(i * HPG + ((1 + br) * NH + j), 1)].rearrange(
                                                             "p t o -> p (t o)"), op=ALU.mult))
                            for t, (a, b) in enumerate(SEG):
                                link(nc.vector.tensor_scalar(Pp[u % 2][:, a:b], Pp[u % 2][:, a:b],
                                                             st6[:, u % 2, 3, t:t + 1], None, op0=ALU.mult))
                            v.sem_inc(b6, 1)
                        if step >= 3 and step % 2:
                            j = (step - 3) // 2
                            v.wait_ge(v6, done(i, 8, 2 * j + 1))
                            link(nc.vector.tensor_copy(attnT[:, bass.ds(i * HPG + j, 1), 0:NP_TOK].rearrange(
                                "p o t -> p (o t)"), PS[:, 4 + j % 2, 0:NP_TOK]))
                            v.sem_inc(o6, 1)
                    v.sem_clear(d6)
        scope.close()

        scope = ExitStack()
        grpw = sb(scope, "grpw", [P, 4, 2, 256])
        pscale = sb(scope, "pscale", [P, POOL_CH])
        tmp = sb(scope, "tmp", [P, 2, T])
        PcT_r = in_place_of("PcT", [P, 2, DK, P])
        wh[0] = [PcT_r[:, n, :, :] for n in range(2)]
        XR = nc.alloc_sbuf_tensor_at("XR", [P, 3, D], F32, offset=place["kcb"])
        assert place["kcb"] + 2 * D * 4 <= place["PcT"]
        xr_ld = sem("xr_ld")
        c7 = sem("c7")
        ym = sem("ym")
        y_hi, y_lo = sem("y_hi"), sem("y_lo")
        sgp, sga = sem("sgp"), sem("sga")
        a_hi, a_lo = sem("a_hi"), sem("a_lo")
        mg = sem("mg")
        m_hi, m_lo = sem("m_hi"), sem("m_lo")
        d7 = sem("d7")
        N_BP, N_BA, N_WO = L_BA - L_BP, L_WO - L_BA, L_WQ - L_WO

        def chunk(x, c, n=1):
            return x[:, bass.ds(c, n), :].rearrange("p a t -> p (a t)")

        with nc.Block() as block:
            @block.sync
            def _(sp):
                sp.dma_start(grpw[:, :, :, :], grp_d.rearrange("g (k p) e -> p g k e", p=P)).then_inc(c7, 16)
                sp.dma_start(pscale[:, :], pscale_d).then_inc(c7, 16)
                sp.wait_ge(ym, 1)
                sp.dma_start(XR[:, 0:TT, :], x_d[0:NP_TOK].rearrange("(t p) d -> p t d", p=P)).then_inc(xr_ld, 16)
                next_loads(sp, L_BP, N_BP, per=2)
                next_loads(sp, L_BA, N_BA)
                next_loads(sp, L_WO, N_WO)

            @block.tensor
            def _(pe):
                pe.wait_ge(c7, 32)
                for c in range(POOL_CH):
                    g, e = c // 2, c % 2
                    if c >= 2:
                        pe.wait_ge(y_lo, c - 1)
                    for k in range(2):
                        m = nc.tensor.matmul(PS[:, c % 2, 0:T], grpw[:, g, k, e * P:(e + 1) * P],
                                             PT[:, 2 * g + k, :], start=(k == 0), stop=(k == 1))
                    m.then_inc(ym, 1)
                pe.wait_ge(y_lo, POOL_CH)
                first = product(L_BP - 1)
                with pe.Fori(0, N_BP // SLOTS) as i:
                    for j in range(SLOTS):
                        pe.wait_ge(w_lo, i * SLOTS + split(L_BP + j))
                        for h in range(2):
                            pe.wait_ge(ge, i * (2 * SLOTS) + (first + 2 * j + h + 1))
                            split_gemm(L_BP, j, *ypHL, PS[:, GB + h, 0:T],
                                       [(h * POOL_CH + k, k) for k in range(POOL_CH)])
                pe.wait_ge(a_lo, N_BP)
                with pe.Fori(0, N_BA // SLOTS) as i:
                    for j in range(SLOTS):
                        gemm3(pe, L_BA, i, j, *atHL)
                with pe.Fori(0, N_WO // SLOTS) as i:
                    for j in range(SLOTS):
                        def ready(k):
                            if j == 0 and k in (0, DK - 1):
                                pe.wait_ge(m_lo, DK - 1 if k == 0 else DK)
                        gemm3(pe, L_WO, i, j, *meHL, ready)

            @block.scalar
            def _(act):
                hi_w(L_BP, 0, 0)
                act.wait_ge(c7, 32)
                for c in range(POOL_CH):
                    act.wait_ge(ym, c + 1)
                    nc.scalar.activation(ypHL[0][:, c, :], PS[:, c % 2, 0:T], ACT.Copy, scale=pscale[:, c:c + 1]).then_inc(y_hi, 1)
                hi_w(L_BP, 0, 1)
                for q in range(4):
                    x = gatesP[:, 4 * q:4 * q + 4, :]
                    nc.scalar.activation(x, x, ACT.Sigmoid).then_inc(sgp, 1)
                first = product(L_BP - 1)
                with act.Fori(0, N_BP // SLOTS) as i:
                    for j in range(SLOTS):
                        nc.scalar.copy(chunk(atHL[0], i * (2 * SLOTS) + 2 * j, 2),
                                       chunk(attnT, i * (2 * SLOTS) + 2 * j, 2)).then_inc(a_hi, 1)
                        x = chunk(gatesA, i * (2 * SLOTS) + 2 * j, 2)
                        nc.scalar.activation(x, x, ACT.Sigmoid).then_inc(sga, 1)
                        act.wait_ge(gd, i * (2 * SLOTS) + (first + 2 * j + 2))
                        hi_w(L_BP, i, j + 2)
                with act.Fori(0, N_BA // SLOTS) as i:
                    for j in range(SLOTS):
                        gemm_out(act, L_BA, i, j)
                        hi_w(L_BA, i, j + 2)
                        act.wait_ge(mg, i * SLOTS + (j + 1))
                        nc.scalar.copy(chunk(meHL[0], i * SLOTS + j), chunk(mergedT, i * SLOTS + j)).then_inc(m_hi, 1)

                def out(i, j):
                    gemm_out(act, L_WO, i, j)
                    nc.scalar.copy(chunk(woT, i * SLOTS + j), bank(L_WO, j)).then_inc(ge, 1)

                with act.Fori(0, N_WO // SLOTS - 1) as i:
                    for j in range(SLOTS):
                        out(i, j)
                        hi_w(L_WO, i, j + 2)
                for j in range(SLOTS):
                    out(N_WO // SLOTS - 1, j)
                    if j < 2:
                        hi_w(L_WQ - SLOTS, 0, j + 2)

            @block.vector
            def _(v):
                lo_w(nc.vector, L_BP, 0, 0)
                for c in range(POOL_CH):
                    v.wait_ge(y_hi, c + 1)
                    nc.vector.scalar_tensor_tensor(out=ypHL[1][:, c, :], in0=PS[:, c % 2, 0:T], scalar=pscale[:, c:c + 1],
                                                   in1=ypHL[0][:, c, :].bitcast(F32), op0=ALU.mult,
                                                   op1=ALU.subtract).then_inc(y_lo, 1)
                lo_w(nc.vector, L_BP, 0, 1)
                first = product(L_BP - 1)
                v.wait_ge(sgp, 4)
                with v.Fori(0, N_BP // SLOTS) as i:
                    for j in range(SLOTS):
                        v.wait_ge(a_hi, i * SLOTS + (j + 1))
                        c = i * (2 * SLOTS) + 2 * j
                        nc.vector.tensor_tensor(chunk(atHL[1], c, 2), chunk(attnT, c, 2), chunk(atHL[0], c, 2).bitcast(F32),
                                                op=ALU.subtract).then_inc(a_lo, 1)
                        for h in range(2):
                            v.wait_ge(gd, i * (2 * SLOTS) + (first + 2 * j + h + 1))
                            c = i * (2 * SLOTS) + (2 * j + h)
                            nc.vector.tensor_tensor(chunk(mergedT, c), PS[:, GB + h, 0:T], chunk(gatesP, c),
                                                    op=ALU.mult).then_inc(ge, 1)
                        lo_w(nc.vector, L_BP, i, j + 2)
                v.wait_ge(sga, N_BP)
                v.wait_ge(ge, product(L_BA - 1) + 2)
                with v.Fori(0, N_BA // SLOTS) as i:
                    for j in range(SLOTS):
                        c = i * SLOTS + j
                        m = chunk(mergedT, c)
                        gemm_out(v, L_BA, i, j)
                        nc.vector.tensor_tensor(tmp[:, j % 2, :], bank(L_BA, j), chunk(gatesA, c), op=ALU.mult).then_inc(ge, 1)
                        v.wait_ge(ge, i * SLOTS + (product(L_BA + j) + 2))
                        nc.vector.tensor_tensor(m, m, tmp[:, j % 2, :], op=ALU.add).then_inc(mg, 1)
                        lo_w(nc.vector, L_BA, i, j + 2)
                        v.wait_ge(m_hi, i * SLOTS + (j + 1))
                        nc.vector.tensor_tensor(chunk(meHL[1], c), m, chunk(meHL[0], c).bitcast(F32),
                                                op=ALU.subtract).then_inc(m_lo, 1)
                with v.Fori(0, N_WO // SLOTS - 1) as i:
                    for j in range(SLOTS):
                        lo_w(nc.vector, L_WO, i, j + 2)
                for j in range(2):
                    lo_w(nc.vector, L_WQ - SLOTS, 0, j + 2)
        scope.close()
        gas.close()
        mid.close()
        spare = PT_r[:, DK:2 * DK, :].rearrange("p a t -> p (a t)")
        wh[0] = [spare[:, n * D:(n + 1) * D].rearrange("p (k c) -> p k c", c=P) for n in range(2)]

        xrs = ExitStack()
        sb(xrs, "XR_room", [P, 3, D])
        assert place["XR_room"] == place["kcb"]
        skT = sb(xrs, "skT2", [P, 16, P])
        iot = sb_far(top, "iot", [P, 16])
        c9 = sem("c9")
        scope = ExitStack()
        lnp = sb(scope, "lnp", [P, 2, D])
        bst = sb(scope, "bst", [P, 3, 4, 6])
        mv = sb(scope, "mv", [P, 3, 2])
        rs = sb(scope, "rs", [P, 3, 3])
        eps = sb(scope, "eps", [P, 1])
        c8 = sem("c8")
        t9 = sem("t9")
        r9 = sem("r9")
        n9 = sem("n9")
        q9 = sem("q9")
        s9 = sem("s9")
        x9 = sem("x9")
        g9 = sem("g9")
        h9g, h9v = sem("h9g"), sem("h9v")
        u9 = sem("u9")
        z9 = sem("z9")
        l9 = sem("l9")
        ADD = (D, 1024, 768)
        h_st = sem("h_st")
        wd = (P, P, NS_TOK)
        with nc.Block() as block:
            @block.sync
            def _(sp):
                for n in range(2):
                    sp.dma_start(lnp[:, n, :], ln_d[n:n + 1, :].to_broadcast([P, D])).then_inc(c8, 16)
                sp.dma_start(XR[0:NS_TOK, 2, :], x_d[NP_TOK:T]).then_inc(c8, 16)
                sp.dma_start(skT[:, :, :], skT_d).then_inc(c9, 16)
                sp.dma_start(iot[:, :], iota_d).then_inc(c9, 16)
                for t in range(3):
                    sp.wait_ge(h9g, t + 1)
                    sp.wait_ge(h9v, t + 1)
                    sp.dma_start(h_d[t * P:t * P + wd[t], :], XR[0:wd[t], t, :]).then_inc(h_st, 16)

            @block.tensor
            def _(pe):
                for t in range(3):
                    for q in range(4):
                        n = 4 * t + q
                        if n >= 2:
                            pe.wait_ge(r9, n - 1)
                        for j in range(4):
                            m = nc.tensor.transpose(PS[0:wd[t], n % 2, j * P:(j + 1) * P],
                                                    woT[:, 4 * q + j, t * P:t * P + wd[t]], ident[:, :])
                        m.then_inc(t9, 1)
                for t in range(3):
                    pe.wait_ge(h9g, t + 1)
                    pe.wait_ge(h9v, t + 1)
                    for q in range(4):
                        n = 4 * t + q
                        if n >= 4:
                            pe.wait_ge(l9, n - 3)
                        for j in range(4):
                            m = nc.tensor.transpose(PS[:, 2 + n % 4, j * P:j * P + wd[t]],
                                                    XR[0:wd[t], t, (4 * q + j) * P:(4 * q + j + 1) * P],
                                                    ident[0:wd[t], 0:wd[t]])
                        m.then_inc(u9, 1)

            def columns(t, q):
                return ([x[:, 4 * q:4 * q + 4, t * P:t * P + wd[t]] for x in hHL],
                        PS[:, 2 + q, :].rearrange("p (j t) -> p j t", j=4)[:, :, 0:wd[t]])

            @block.scalar
            def _(act):
                for n in range(2):
                    hi_w(L_WQ, 0, n)
                for t in range(3):
                    w = wd[t]
                    act.wait_ge(n9, t + 1)
                    nc.scalar.activation(rs[0:w, t, 0:1], mv[0:w, t, 1:2], ACT.Sqrt, bias=eps[0:w, 0:1]).then_inc(q9, 1)
                    act.wait_ge(s9, t + 1)
                    nc.scalar.activation(XR[0:w, t, :], XR[0:w, t, :], ACT.Identity, bias=rs[0:w, t, 2:3],
                                         scale=rs[0:w, t, 1:2]).then_inc(x9, 1)
                for t in range(3):
                    for q in range(4):
                        act.wait_ge(u9, 4 * t + q + 1)
                        (hi, lo), src = columns(t, q)
                        nc.scalar.copy(hi, src).then_inc(z9, 1)

            @block.gpsimd
            def _(g):
                for n in range(2):
                    lo_w(nc.gpsimd, L_WQ, 0, n)
                for t in range(3):
                    g.wait_ge(g9, t + 1)
                    x = XR[0:wd[t], t, 0:ADD[t]]
                    nc.gpsimd.tensor_tensor(x, x, lnp[0:wd[t], 1, 0:ADD[t]], op=ALU.add).then_inc(h9g, 1)

            @block.vector
            def _(v):
                n = [0]

                def link(ins):
                    n[0] += 1
                    ins.then_inc(d7, 1)
                    v.wait_ge(d7, n[0])

                def moments(t):
                    w = wd[t]
                    for q in range(4):
                        x = XR[0:w, t, q * 512:(q + 1) * 512]
                        v.wait_ge(t9, 4 * t + q + 1)
                        nc.vector.scalar_tensor_tensor(out=x, in0=x, scalar=ALPHA, in1=PS[0:w, (4 * t + q) % 2, :],
                                                       op0=ALU.mult, op1=ALU.add).then_inc(r9, 1)
                        if q > 0:
                            v.wait_ge(r9, 4 * t + q)
                            nc.vector.bn_stats(bst[0:w, t, q - 1, :], XR[0:w, t, (q - 1) * 512:q * 512])
                    v.wait_ge(r9, 4 * t + 4)
                    link(nc.vector.bn_stats(bst[0:w, t, 3, :], XR[0:w, t, 3 * 512:]))
                    nc.vector.bn_aggr(mv[0:w, t, :], bst[0:w, t, :, :]).then_inc(n9, 1)

                def rstd(t):
                    w = wd[t]
                    v.wait_ge(q9, t + 1)
                    link(nc.vector.reciprocal(rs[0:w, t, 1:2], rs[0:w, t, 0:1]))
                    nc.vector.scalar_tensor_tensor(out=rs[0:w, t, 2:3], in0=mv[0:w, t, 0:1], scalar=-1.0,
                                                   in1=rs[0:w, t, 1:2], op0=ALU.mult, op1=ALU.mult).then_inc(s9, 1)

                def affine(t):
                    w = wd[t]
                    v.wait_ge(x9, t + 1)
                    x = XR[0:w, t, :]
                    link(nc.vector.tensor_tensor(x, x, lnp[0:w, 0, :], op=ALU.mult))
                    v.sem_inc(g9, 1)
                    if ADD[t] < D:
                        x = XR[0:w, t, ADD[t]:]
                        link(nc.vector.tensor_tensor(x, x, lnp[0:w, 1, ADD[t]:], op=ALU.add))
                    v.sem_inc(h9v, 1)

                def low_parts(t):
                    for q in range(4):
                        v.wait_ge(z9, 4 * t + q + 1)
                        (hi, lo), src = columns(t, q)
                        nc.vector.tensor_tensor(lo, src, hi.bitcast(F32), op=ALU.subtract).then_inc(l9, 1)

                link(nc.vector.memset(eps[:, :], EPS))
                v.wait_ge(xr_ld, 16)
                moments(0)
                rstd(0)
                moments(1)
                v.wait_ge(c8, 48)
                affine(0)
                rstd(1)
                moments(2)
                rstd(2)
                affine(1)
                affine(2)
                for t in range(3):
                    low_parts(t)
        scope.close()

        selT = sb_far(top, "selT", [GT, 4, GT])
        sw = sb_far(top, "sw", [P, 4, P])
        keys = sb_far(top, "keys", [P, 4, P])
        m16 = sb_far(top, "m16", [P, 4, 16])
        i16 = sb_far(top, "i16", [P, 4, 16], U32)
        i16f = sb_far(top, "i16f", [P, 4, 16])
        cand = sb_far(top, "cand", [P, 2, 256])
        tv = sb_far(top, "tv", [P, 2, 16])
        ti = sb_far(top, "ti", [P, 2, 16], U32)
        tab = sb_far(top, "tab", [P, 2, 2, 16], U32)
        tabf = sb_far(top, "tabf", [P, 2, 2, 16])
        oh = sb_far(top, "oh", [P, 2, 16, 16])
        es = sb_far(top, "es", [P, 2, 2, 16])
        ef = sb_far(top, "ef", [P, 2, 16])
        eid_next = sb_far(top, "eid_next", [P, NSTEP], I32)
        gsum = sb_far(top, "gsum", [P, 2, 2])
        gate_next = sb_far(top, "gate_next", [P, NSTEP])
        sw_ld, sw_fr = sem("sw_ld"), sem("sw_fr")
        sw0_ld = sem("sw0_ld")
        top_ok = sem("top_ok")
        eid_ok, eid_own = sem("eid_ok"), sem("eid_own")
        exp_in, exp_ok = sem("exp_in"), sem("exp_ok")
        dA = sem("dA")

        def choosing(v):
            n = [0]

            def link(ins):
                n[0] += 1
                ins.then_inc(dA, 1)
                v.wait_ge(dA, n[0])

            def unlink():
                v.sem_clear(dA)
                n[0] = 0

            def top16(vals, idx, src):
                link(nc.vector.max(vals[:, 0:8], src))
                link(nc.vector.max_index(idx[:, 0:8], vals[:, 0:8], src))
                link(nc.vector.match_replace(src, vals[:, 0:8], src, NEG))
                link(nc.vector.max(vals[:, 8:16], src))
                link(nc.vector.max_index(idx[:, 8:16], vals[:, 8:16], src))

            def choose(gr, heads=(0, 1)):
                h0, h1 = heads[0], heads[-1] + 1
                if h0 == 0:
                    if h1 == 1:
                        v.wait_ge(sw0_ld, 64)
                    else:
                        v.wait_ge(sw_ld, gr * 16)
                    link(nc.vector.tensor_copy(keys[:, :, :], sw[:, :, :]))
                    v.sem_inc(sw_fr, 1)
                for a in range(2 * h0, 2 * h1):
                    top16(m16[:, a, :], i16[:, a, :], keys[:, a, :])
                mh = m16[:, :, :].rearrange("p (h f) k -> p h f k", f=2)
                for h in heads:
                    link(nc.vector.tensor_tensor(cand[:, h, :].rearrange("p (i j) -> p i j", i=16),
                                                 mh[:, h, 0, :].unsqueeze(2).to_broadcast([P, 16, 16]),
                                                 mh[:, h, 1, :].unsqueeze(1).to_broadcast([P, 16, 16]), op=ALU.add))
                link(nc.vector.tensor_copy(i16f[:, 2 * h0:2 * h1, :], i16[:, 2 * h0:2 * h1, :]))
                for h in heads:
                    top16(tv[:, h, :], ti[:, h, :], cand[:, h, :])
                H = slice(h0, h1)
                link(nc.vector.tensor_copy(gsum[:, H, 0:1], tv[:, H, 0:1]))
                link(nc.vector.tensor_tensor(tv[:, H, :], tv[:, H, :], gsum[:, H, 0:1].to_broadcast([P, h1 - h0, 16]),
                                             op=ALU.subtract))
                if h1 == 2:
                    v.sem_inc(exp_in, 1)
                link(nc.vector.tensor_scalar(tab[:, 0, H, :], ti[:, H, :], 4, None, op0=ALU.logical_shift_right))
                link(nc.vector.tensor_scalar(tab[:, 1, H, :], ti[:, H, :], 15, None, op0=ALU.bitwise_and))
                link(nc.vector.tensor_copy(tabf[:, :, H, :], tab[:, :, H, :]))
                fh = i16f[:, :, :].rearrange("p (h f) k -> p h f k", f=2)
                for f in range(2):
                    for h in heads:
                        link(nc.vector.tensor_tensor(oh[:, h, :, :],
                                                     tabf[:, f, h, :].unsqueeze(2).to_broadcast([P, 16, 16]),
                                                     iot[:, :].unsqueeze(1).to_broadcast([P, 16, 16]),
                                                     op=ALU.is_equal))
                        link(nc.vector.tensor_tensor(oh[:, h, :, :], oh[:, h, :, :],
                                                     fh[:, h, f, :].unsqueeze(1).to_broadcast([P, 16, 16]),
                                                     op=ALU.mult))
                    link(nc.vector.tensor_reduce(es[:, f, H, :], oh[:, H, :, :], AX, ALU.add))
                link(nc.vector.tensor_scalar(es[:, 0, H, :], es[:, 0, H, :], 128.0, None, op0=ALU.mult))
                link(nc.vector.tensor_tensor(ef[:, H, :], es[:, 0, H, :], es[:, 1, H, :], op=ALU.add))
                v.wait_ge(eid_ok, gr + 1)
                link(nc.vector.tensor_copy(eid_next[:, 16 * h0:16 * h1], ef[:, H, :].rearrange("p h k -> p (h k)")))
                if h1 == 2:
                    v.sem_inc(top_ok, 1)
                    v.wait_ge(exp_ok, gr + 1)
                    gn = gate_next[:, :].rearrange("p (h k) -> p h k", h=2)
                    link(nc.vector.tensor_reduce(gsum[:, :, 0], gn, AX, ALU.add))
                    link(nc.vector.reciprocal(gsum[:, :, 1], gsum[:, :, 0]))
                    link(nc.vector.tensor_tensor(gn, gn, gsum[:, :, 1:2].to_broadcast([P, 2, 16]), op=ALU.mult))
                unlink()
            return link, unlink, choose

        def exps(act, gr):
            act.wait_ge(exp_in, gr + 1)
            nc.scalar.activation(gate_next[:, :], tv[:, :, :].rearrange("p h k -> p (h k)"), ACT.Exp).then_inc(exp_ok, 1)

        scope = ExitStack()
        Sst = [sb(scope, f"Sst{i}", [P, 4, 512]) for i in range(2)]
        sc_m = sem("sc_m")
        sc_c = sem("sc_c")
        sc_st = [sem(f"sc_st{i}") for i in range(2)]
        with nc.Block() as block:
            @block.sync
            def _(sp):
                next_loads(sp, L_WQ, N_LOADS - L_WQ)
                n = [0, 0]
                for t in range(3):
                    sp.wait_ge(sc_c, 4 * t + 4)
                    for gr in range(4 * t, 4 * t + wd[t] // GT):
                        r = (gr % 4) * GT
                        if gr == 0:
                            for q in range(4):
                                sp.dma_start(sw[32 * q:32 * q + 32, :, :].rearrange("p a k -> p (a k)"),
                                             Sst[0][0:GT, q, :]).then_inc(sw0_ld, 16)
                        else:
                            n[t % 2] += 1
                            sp.dma_start(score_d[gr].rearrange("(q t) k -> t q k", q=4),
                                         Sst[t % 2][r:r + GT, :, :]).then_inc(sc_st[t % 2], 16)
                for i in range(2):
                    sp.wait_ge(sc_st[i], 16 * n[i])
                sp.wait_ge(h_st, 48)

            @block.tensor
            def _(pe):
                with pe.Fori(0, (N_LOADS - L_WQ) // SLOTS) as i:
                    for j in range(SLOTS):
                        gemm3(pe, L_WQ, i, j, *hHL)
                pe.wait_ge(c9, 32)
                pe.wait_ge(ge, product(N_LOADS - 1) + 2)
                for t in range(3):
                    for q in range(4):
                        n = 4 * t + q
                        if n >= 6:
                            pe.wait_ge(sc_c, n - 5)
                        for x in range(4):
                            m = nc.tensor.matmul(PS[0:wd[t], n % 6, x * P:(x + 1) * P],
                                                 pqT[:, 4 * q + x, t * P:t * P + wd[t]], skT[:, 4 * q + x, :],
                                                 start=True, stop=True)
                        m.then_inc(sc_m, 1)

            @block.vector
            def _(v):
                with v.Fori(0, (N_LOADS - L_WQ) // SLOTS - 1) as i:
                    for j in range(SLOTS):
                        lo_w(nc.vector, L_WQ, i, j + 2)
                for j in range(2):
                    lo_w(nc.vector, N_LOADS - SLOTS, 0, j + 2)
                for x in (sw_fr, eid_ok):
                    v.sem_inc(x, 1)
                link, unlink, choose = choosing(v)
                v.wait_ge(c9, 32)
                choose(0, heads=(0,))

            @block.scalar
            def _(act):
                def out(i, j):
                    gemm_out(act, L_WQ, i, j)
                    nc.scalar.copy(pqT[:, bass.ds(i * SLOTS + j, 1), :].rearrange("p a t -> p (a t)"),
                                   bank(L_WQ, j)).then_inc(ge, 1)

                last = (N_LOADS - L_WQ) // SLOTS - 1
                with act.Fori(0, last) as i:
                    for j in range(SLOTS):
                        out(i, j)
                        hi_w(L_WQ, i, j + 2)
                for j in range(SLOTS):
                    out(last, j)
                    if j < 2:
                        hi_w(N_LOADS - SLOTS, 0, j + 2)
                for t in range(3):
                    for q in range(4):
                        n = 4 * t + q
                        act.wait_ge(sc_m, n + 1)
                        if t == 2 and q == 0:
                            act.wait_ge(sw0_ld, 64)
                            act.wait_ge(sc_st[0], 16 * 3)
                        nc.scalar.copy(Sst[t % 2][0:wd[t], q, :], PS[0:wd[t], n % 6, :]).then_inc(sc_c, 1)
                nc.scalar.copy(selT[:, :, :], ident[0:GT, 0:GT].unsqueeze(1).to_broadcast([GT, 4, GT]))
        scope.close()
        xrs.close()
        actT.close()
        rings.close()

        Ur = [sb(top, f"Ur{s}", [P, D]) for s in range(SB)]
        Vr = [sb(top, f"Vr{s}", [P, D]) for s in range(SB)]
        hnext = sb(top, "hnext", [GT, D])
        hcur = sb(top, "hcur", [P, D])
        hres = sb(top, "hres", [GT, D])
        R = sb(top, "R", [GT, D])
        lnq = sb(top, "lnq", [GT, 2, D])
        sel = sb(top, "sel", [P, GT])
        eid = sb(top, "eid", [P, 2, NSTEP], I32)
        gate = sb(top, "gate", [P, NSTEP])
        dots = sb(top, "dots", [P, 2, SB])
        gel = sb(top, "gel", [P, 2, SB])
        wgt = sb(top, "wgt", [P, 2, SB])
        Dm = sb(top, "Dm", [P, 2, SB, GT])
        bs2 = sb(top, "bs2", [GT, 4, 6])
        mv2 = sb(top, "mv2", [GT, 2])
        rs2 = sb(top, "rs2", [GT, 3])
        ep2 = sb(top, "ep2", [GT, 1])
        cA = sem("cA")
        h_ld, h_fr, h_ok = sem("h_ld"), sem("h_fr"), sem("h_ok")
        h_rep = sem("h_rep")
        u_ld = [sem(f"u_ld{s}") for s in range(SB)]
        v_ld = [sem(f"v_ld{s}") for s in range(SB)]
        dot = sem("dot")
        gelu = sem("gelu")
        dm = sem("dm")
        pv = sem("pv")
        z_fr = sem("z_fr")
        ln_a, ln_s, ln_c = sem("ln_a"), sem("ln_s"), sem("ln_c")
        y_st, r_fr = sem("y_st"), sem("r_fr")
        with nc.Block() as block:
            @block.sync
            def _(sp):
                sp.dma_start(sel[:, :], sel_d).then_inc(cA, 16)
                for n in range(2):
                    sp.dma_start(lnq[:, n, :], ln_d[2 + n:3 + n, :].to_broadcast([GT, D])).then_inc(cA, 16)

                def load_scores(gr):
                    sp.wait_ge(sw_fr, gr + 1)
                    sp.dma_start(sw[:, :, :].rearrange("p a k -> p (a k)"),
                                 score_d[bass.ds(gr, 1)].rearrange("o p k -> (o p) k")).then_inc(sw_ld, 16)

                def load_h(gr):
                    sp.wait_ge(h_fr, gr + 1)
                    sp.dma_start(hnext[:, :], h_d[bass.ds(gr * GT, GT)]).then_inc(h_ld, 16)

                def store_y(gr):
                    sp.wait_ge(ln_c, gr + 1)
                    sp.dma_start(y_d[bass.ds(gr * GT, GT)], R[:, :]).then_inc(y_st, 16)
                    sp.wait_ge(y_st, gr * 16 + 16)
                    sp.sem_inc(r_fr, 1)

                sp.sem_inc(r_fr, 1)
                load_h(0)
                load_scores(1)
                load_h(1)
                with sp.Fori(0, NG - 2) as i:
                    load_scores(i + 2)
                    load_h(i + 2)
                    store_y(i)
                store_y(NG - 2)
                store_y(NG - 1)
                sp.wait_ge(y_st, 16 * NG)
                sp.wait_ge(raw_out, 64)
                sp.wait_ge(pool_out, 16)
                sp.wait_ge(out_done, 16 * n_out[0])

            @block.gpsimd
            def _(g):
                def own(par, a, b):
                    nc.gpsimd.tensor_copy(eid[:, par, a:b], eid_next[:, a:b]).then_inc(eid_own, 1)
                    g.wait_ge(eid_own, 1)
                    g.sem_clear(eid_own)

                def group(gr, par, first=False):
                    if first:
                        own(par, 0, 16)
                    else:
                        g.wait_ge(top_ok, gr + 1)
                        g.sem_inc(gathers, 1)
                        own(par, 0, NSTEP)
                        g.sem_inc(eid_ok, 1)
                    for b in range(NB):
                        if first and b * SB == 16:
                            g.wait_ge(top_ok, 1)
                            own(par, 16, NSTEP)
                            g.sem_inc(eid_ok, 1)
                        for s in range(SB):
                            c = b * SB + s
                            g.wait_ge(dot, gr * NSTEP + (c + 1))
                            g.sem_inc(gathers, 1)
                            nc.gpsimd.indirect_dma_start(
                                out=Ur[s][:, :], out_offset=None, in_=u_d,
                                in_offset=bass.IndirectOffsetOnAxis(ap=eid[:, par, c:c + 1], axis=0)).then_inc(u_ld[s], 16)
                        for s in range(SB):
                            c = b * SB + s
                            g.wait_ge(pv, gr * NSTEP + (c + 1))
                            g.sem_inc(gathers, 1)
                            nc.gpsimd.indirect_dma_start(
                                out=Vr[s][:, :], out_offset=None, in_=v_d,
                                in_offset=bass.IndirectOffsetOnAxis(ap=eid[:, par, c:c + 1], axis=0)).then_inc(v_ld[s], 16)


                group(0, 0, first=True)
                group(1, 1)
                with g.Fori(1, NG // 2) as i:
                    group(2 * i, 0)
                    group(2 * i + 1, 1)
                group(NG - 1, (NG - 1) % 2)

            @block.tensor
            def _(pe):
                def spread_h(gr):
                    pe.wait_ge(h_ld, gr * 16 + 16)
                    for q in range(4):
                        m = nc.tensor.matmul(PS[:, 4 + q, :], selT[:, :, :].rearrange("k q t -> k (q t)"),
                                             hnext[:, q * 512:(q + 1) * 512], start=True, stop=True)
                    m.then_inc(h_rep, 1)
                    pe.wait_ge(h_rep, gr + 1)
                    pe.sem_inc(h_fr, 1)

                def group(gr, last):
                    pe.wait_ge(z_fr, gr + 1)
                    for b in range(NB):
                        pe.wait_ge(dm, gr * NB + (b + 1))
                        for s in range(SB):
                            pe.wait_ge(v_ld[s], gr * (16 * NB) + 16 * (b + 1))
                            for q in range(4):
                                m = nc.tensor.matmul(PS[0:GT, q, :], Dm[:, b % 2, s, :], Vr[s][:, q * 512:(q + 1) * 512],
                                                     start=(b == 0 and s == 0), stop=(b == NB - 1 and s == SB - 1),
                                                     tile_position=(0, 0))
                            m.then_inc(pv, 1)
                        if b == 1 and not last:
                            pe.wait_ge(h_ok, 2 * gr + 1)
                            spread_h(gr + 1)

                pe.sem_inc(pv, SB)
                pe.sem_inc(h_fr, 1)
                spread_h(0)
                with pe.Fori(0, NG - 1) as i:
                    group(i, False)
                group(NG - 1, True)

            @block.scalar
            def _(act):
                def group(gr, first, last):
                    act.wait_ge(h_rep, gr + 1)
                    act.wait_ge(dot, gr * NSTEP + SB)
                    if not first:
                        act.wait_ge(h_ok, 2 * gr)
                    nc.scalar.copy(hcur[:, :], PS[:, 4:8, :].rearrange("p q d -> p (q d)")).then_inc(h_ok, 1)
                    for b in range(NB):
                        act.wait_ge(dot, gr * NSTEP + (b + 2) * SB)
                        nc.scalar.activation(gel[:, b % 2, :], dots[:, b % 2, :], ACT.Gelu).then_inc(gelu, 1)
                        if b == 0 and not first:
                            norm(gr - 1)
                        if b == 1 and not last:
                            exps(act, gr + 1)
                    if not first:
                        act.wait_ge(z_fr, gr + 1)
                    nc.scalar.copy(hres[:, :], hcur[0:GT, :]).then_inc(h_ok, 1)

                def norm(gr):
                    act.wait_ge(ln_a, gr + 1)
                    nc.scalar.activation(rs2[:, 0:1], mv2[:, 1:2], ACT.Sqrt, bias=ep2[:, 0:1]).then_inc(ln_s, 1)

                exps(act, 0)
                group(0, True, False)
                with act.Fori(1, NG - 1) as i:
                    group(i, False, False)
                group(NG - 1, False, True)
                norm(NG - 1)

            @block.vector
            def _(v):
                link, unlink, choose = choosing(v)

                def norm_a(gr):
                    v.wait_ge(pv, gr * NSTEP + (NSTEP + SB))
                    v.wait_ge(h_ok, 2 * gr + 2)
                    v.wait_ge(r_fr, gr + 1)
                    link(nc.vector.scalar_tensor_tensor(out=R[:, :], in0=hres[:, :], scalar=ALPHA,
                                                        in1=PS[0:GT, 0:4, :].rearrange("p q d -> p (q d)"),
                                                        op0=ALU.mult, op1=ALU.add))
                    v.sem_inc(z_fr, 1)
                    for q in range(4):
                        link(nc.vector.bn_stats(bs2[:, q, :], R[:, q * 512:(q + 1) * 512]))
                    link(nc.vector.bn_aggr(mv2[:, :], bs2[:, :, :]))
                    v.sem_inc(ln_a, 1)
                    unlink()

                def norm_b(gr):
                    v.wait_ge(ln_s, gr + 1)
                    link(nc.vector.reciprocal(rs2[:, 1:2], rs2[:, 0:1]))
                    link(nc.vector.tensor_scalar(R[:, :], R[:, :], mv2[:, 0:1], rs2[:, 1:2], op0=ALU.subtract, op1=ALU.mult))
                    link(nc.vector.tensor_tensor(R[:, :], R[:, :], lnq[:, 0, :], op=ALU.mult))
                    link(nc.vector.tensor_tensor(R[:, :], R[:, :], lnq[:, 1, :], op=ALU.add))
                    v.sem_inc(ln_c, 1)
                    unlink()

                def group(gr, first, last):
                    link(nc.vector.tensor_copy(gate[:, :], gate_next[:, :]))
                    unlink()
                    v.wait_ge(h_ok, 2 * gr + 1)
                    for b in range(NB):
                        for s in range(SB):
                            v.wait_ge(u_ld[s], gr * (16 * NB) + 16 * (b + 1))
                            nc.vector.tensor_tensor_reduce(out=Ur[s][:, :], in0=Ur[s][:, :], in1=hcur[:, :], scale=1.0,
                                                           scalar=0.0, op0=ALU.mult, op1=ALU.add,
                                                           accum_out=dots[:, b % 2, s:s + 1]).then_inc(dot, 1)
                        v.wait_ge(gelu, gr * NB + (b + 1))
                        link(nc.vector.tensor_tensor(wgt[:, b % 2, :], gel[:, b % 2, :], gate[:, b * SB:(b + 1) * SB],
                                                     op=ALU.mult))
                        if b or not first:
                            v.wait_ge(pv, gr * NSTEP + b * SB)
                        link(nc.vector.tensor_tensor(Dm[:, b % 2, :, :],
                                                     sel[:, :].unsqueeze(1).to_broadcast([P, SB, GT]),
                                                     wgt[:, b % 2, :].unsqueeze(2).to_broadcast([P, SB, GT]), op=ALU.mult))
                        v.sem_inc(dm, 1)
                        unlink()
                        if b == 0 and not first:
                            norm_a(gr - 1)
                        if b == 1 and not first:
                            norm_b(gr - 1)
                        if b == 1 and not last:
                            choose(gr + 1)

                v.sem_inc(dot, SB)
                v.sem_inc(z_fr, 1)
                link(nc.vector.memset(ep2[:, :], EPS))
                unlink()
                choose(0, heads=(1,))
                v.wait_ge(cA, 48)
                group(0, True, False)
                with v.Fori(1, NG - 1) as i:
                    group(i, False, False)
                group(NG - 1, False, True)
                norm_a(NG - 1)
                norm_b(NG - 1)


_OUTS = [("y", (T, D)), ("kvT", (P, 6, NKV, T)), ("ktail", (BS, 252, 512)), ("vtail", (BS, 252, 512)),
         ("poolT", (P, POOL_CH, POOL_ST + NS_TOK)), ("spool", (BS, 11, 1024))]


def constants(np):
    f = np.float32
    p = np.arange(P)
    ident = np.eye(P, dtype=f)
    rot = np.zeros((P, P), f)
    for m in range(32):
        rot[(m + 16) % 32, m] = 1.0
    pos = np.concatenate([np.arange(NP_TOK), np.tile(256 + np.arange(LS), BS)]).astype(f)
    inv = (f(500000.0) ** (-np.arange(16, dtype=f) / f(16))).astype(f)
    ang = (pos[:, None] * inv).astype(f)
    cs = np.zeros((P, 2, T), f)
    cs[:, 0] = 1.0
    cs[0:16, 0] = cs[16:32, 0] = np.cos(ang).T
    cs[0:16, 1] = -np.sin(ang).T
    cs[16:32, 1] = np.sin(ang).T
    big = f(-1e30)
    diag = np.where(p[None, :] <= p[:, None], f(0), big).astype(f)
    maskp = np.concatenate([diag, np.zeros((P, P), f), diag], 1)
    x = p % 8
    maskn = np.full((P, BS, NS_TOK), big, f)
    for b in range(BS):
        for l2 in range(LS):
            maskn[:, b, b * LS + l2] = np.where(l2 <= x % LS, f(0), big)
    maskc = np.zeros((P, 2, 480), f)
    n = np.arange(NCMP)
    for t in range(TT):
        ok = 16 * n[None, :] + 31 <= (t * P + p)[:, None]
        maskc[:, 0].reshape(P, NH, TT, NCMP)[:, :, t, :] = np.where(ok, f(0), big)[:, None, :]
    rb = (p % 32) // LS
    ok = rb[:, None] == np.arange(BS)[None, :]
    maskc[:, 1].reshape(P, NKV, BS, NCMP)[:] = np.where(ok, f(0), big)[:, None, :, None]
    keepc = (maskc == 0).astype(f)
    rcnt = np.ones((P, 4, 16), f)
    for g, w in enumerate((2, 4, 8, 16)):
        rcnt[:, g] = (w / np.minimum(w, np.arange(16) + 1)).astype(f)
    sel = (p[:, None] % GT == np.arange(GT)[None, :]).astype(f)
    iota = np.tile(np.arange(16, dtype=f), (P, 1))
    pidx = p.astype(f)[:, None].copy()
    return dict(ident=ident, rot=rot, cs=cs, maskp=maskp, maskn=maskn, maskc=maskc, keepc=keepc, rcnt=rcnt,
                sel=sel, iota=iota, pidx=pidx)


def kernel(**inputs):
    import numpy as np
    import concourse.bacc as _bacc
    from concourse.bass_utils import run_bass_kernel_spmd as _run

    a = {k: np.asarray(v) for k, v in inputs.items()}

    def chunks(w):
        k, n = w.shape
        return w.reshape(k // P, P, n // P, P).transpose(2, 1, 0, 3).reshape(n // P, P, k)

    def pagesT(c):
        return c[0].transpose(0, 3, 2, 1).reshape(-1, NKV * P)

    x = np.concatenate([a["x_prompt"][0], a["x_sample"].reshape(NS_TOK, D)], 0)
    w_in = a["w_in"][0]
    cols = chunks(w_in[:, :6144])
    gates = chunks(w_in[:, 6192:])
    wbp = chunks(a["w_branch_pool"][0]).reshape(8, 2, P, 1024).transpose(0, 2, 1, 3).reshape(8, P, 2048)
    stream = np.concatenate([cols[8:24], cols[32:36], cols[40:44], cols[24:32], cols[36:40], cols[44:48], cols[0:8],
                             gates, wbp, chunks(a["w_branch_attn"][0]), chunks(a["w_out"][0]),
                             chunks(a["peer_wq"][0])])
    kwin = a["cache_k_win"][0].reshape(BS, 256, 512)
    vwin = a["cache_v_win"][0].reshape(BS, 256, 512)
    arrays = dict(
        xT=x.T, x=x, w=stream,
        nsa=w_in[:, 6144:6192].reshape(DK, P, 48).transpose(1, 0, 2),
        grp=a["pool_grp_w"][0],
        pscale=a["pool_scale"][0].reshape(POOL_CH, P).T,
        stateT=a["state_pool"][0].transpose(2, 0, 1).reshape(1024, BS * POOL_ST), state=a["state_pool"][0],
        kcT=pagesT(a["cache_k_cmp"]), vcT=pagesT(a["cache_v_cmp"]), ksT=pagesT(a["cache_k_slc"]),
        vs=a["cache_v_slc"][0].reshape(-1, 512),
        kwT=kwin.reshape(BS, 2, P, NKV, HD).transpose(0, 4, 1, 3, 2).reshape(BS, P, 1024),
        vw=vwin.reshape(BS, 2, P, 512).transpose(0, 2, 1, 3).reshape(BS, P, 1024),
        kwin=kwin, vwin=vwin, ptab=a["page_table"].reshape(-1),
        w1=np.stack([a["cmp_w1_k"][0].transpose(1, 0, 2), a["cmp_w1_v"][0].transpose(1, 0, 2)]),
        w2=np.stack([a["cmp_w2_k"][0], a["cmp_w2_v"][0]], 1),
        peT=np.stack([a["cmp_pe_k"][0].T, a["cmp_pe_v"][0].T], 1),
        ln=np.stack([a["ln1_g"][0], a["ln1_b"][0], a["ln2_g"][0], a["ln2_b"][0]]),
        skT=a["peer_subkeys"][0].reshape(16, P, P).transpose(2, 0, 1), u=a["peer_u"][0], v=a["peer_v"][0])
    arrays.update(constants(np))
    nc = _bacc.Bacc("TRN2", target_bir_lowering=False, num_devices=1)
    feeds, args = {}, []
    for name, arr in arrays.items():
        feeds[f"in_{name}"] = np.ascontiguousarray(arr)
        args.append(nc.dram_tensor(f"in_{name}", arr.shape, mybir.dt.from_np(arr.dtype), kind="ExternalInput").ap())
    for name, shape in _OUTS:
        args.append(nc.dram_tensor(f"out_{name}", shape, F32, kind="ExternalOutput").ap())
    build(nc, *args)
    r = _run(nc, [feeds], core_ids=[0]).results[0]
    y, kvT, ktail, vtail, poolT, spool = [r[f"out_{name}"] for name, _ in _OUTS]
    kv = kvT.transpose(1, 3, 2, 0)
    kv_p = [kv[n, :NP_TOK][None, None] for n in range(6)]
    kv_s = [kv[n, NP_TOK:].reshape(1, BS, LS, NKV, HD) for n in range(6)]

    def tail(old, new):
        return np.concatenate([old.reshape(1, BS, 252, NKV, HD), new], 2)

    pool = poolT.transpose(2, 1, 0).reshape(POOL_ST + NS_TOK, 1024)
    pool_s = np.concatenate([spool, pool[POOL_ST:].reshape(BS, LS, 1024)], 1)[None]
    return (y[None, :NP_TOK], y[NP_TOK:].reshape(BS, LS, D), *kv_p, pool[None, None, :POOL_ST], *kv_s[:4],
            tail(ktail, kv_s[4]), tail(vtail, kv_s[5]), pool_s)
```
